# Optimizing a Trainium2 kernel written in Bass

```python
import math
import jax, jax.numpy as jnp
from jax import lax
import numpy as np

D_MODEL = 1024
BATCH = 1
SEQ = 256
DEPTH = 1

CHUNK = 64
EPS = 1e-6
GDN_HEADS = 8
GDN_DK = 128
GDN_DV = 128
GDN_QK = GDN_HEADS * GDN_DK
GDN_V = GDN_HEADS * GDN_DV
CONV_W = 4
RWKV_HEAD = 64
RWKV_WIDTH = D_MODEL
RWKV_HEADS = RWKV_WIDTH // RWKV_HEAD
DECAY_LORA = 64
AAA_LORA = 64
GATE_LORA = 128
RWKV_GN_EPS = 64e-5
GDN_QKV_COLS = 2 * GDN_QK + GDN_V
RWKV_COLS = 3 * RWKV_WIDTH + DECAY_LORA + AAA_LORA + GATE_LORA
IN_WIDTHS = (GDN_QKV_COLS, GDN_V, GDN_HEADS, GDN_HEADS, RWKV_COLS, D_MODEL, D_MODEL)
N_IN_COLS = GDN_QKV_COLS + GDN_V + 2 * GDN_HEADS + RWKV_COLS + 2 * D_MODEL
N_EXPERTS = 32
TOP_K = 4
D_FF = D_MODEL
SWIGLU_ALPHA = 1.702
SWIGLU_LIMIT = 7.0
MOE_BLOCK = 128

kernel_name = "hybrid_gdn_rwkv7_moe_block"

def _split(t, widths):
    offs = [int(o) for o in np.cumsum(widths)[:-1]]
    return jnp.split(t, offs, axis=-1)

def _rmsnorm(x, w, eps=EPS):
    xf = x.astype(jnp.float32)
    y = xf * lax.rsqrt(jnp.mean(xf * xf, axis=-1, keepdims=True) + eps)
    return (y * w.astype(jnp.float32)).astype(x.dtype)

def _l2norm(x):
    xf = x.astype(jnp.float32)
    return xf * lax.rsqrt(jnp.sum(xf * xf, axis=-1, keepdims=True) + EPS)

def _shift1(t):
    return jnp.pad(t, ((0, 0), (1, 0), (0, 0)))[:, :-1]

def _causal_dwconv(x, w):
    S = x.shape[1]
    xp = jnp.pad(x, ((0, 0), (CONV_W - 1, 0), (0, 0)))
    y = w[0] * xp[:, 0:S]
    for j in range(1, CONV_W):
        y = y + w[j] * xp[:, j:j + S]
    return y

def _gated_delta_chunked(q, k, v, g, beta):
    f32 = jnp.float32
    Bsz, S, H, _ = q.shape
    nc = S // CHUNK

    def to_chunks(t):
        return t.astype(f32).reshape(Bsz, nc, CHUNK, H, -1).transpose(0, 3, 1, 2, 4)

    q, k, v = to_chunks(q), to_chunks(k), to_chunks(v)
    g = g.astype(f32).reshape(Bsz, nc, CHUNK, H).transpose(0, 3, 1, 2)
    beta = beta.astype(f32).reshape(Bsz, nc, CHUNK, H).transpose(0, 3, 1, 2)
    gc = jnp.cumsum(g, axis=-1)
    idx = jnp.arange(CHUNK)
    incl = idx[:, None] >= idx[None, :]
    strict = idx[:, None] > idx[None, :]
    diff = gc[..., :, None] - gc[..., None, :]
    decay = jnp.where(incl, jnp.exp(jnp.where(incl, diff, 0.0)), 0.0)
    k_beta = k * beta[..., None]
    m = jnp.where(strict, jnp.einsum('bhnik,bhnjk->bhnij', k_beta, k) * decay, 0.0)
    eye = jnp.eye(CHUNK, dtype=f32)
    t_inv = lax.linalg.triangular_solve(eye + m, jnp.broadcast_to(eye, m.shape),
                                        left_side=True, lower=True, unit_diagonal=True)
    u = jnp.matmul(t_inv, v * beta[..., None])
    w = jnp.matmul(t_inv, k_beta * jnp.exp(gc)[..., None])
    attn = jnp.einsum('bhnik,bhnjk->bhnij', q, k) * decay
    q_dec = q * jnp.exp(gc)[..., None]
    k_dec = k * jnp.exp(gc[..., -1:] - gc)[..., None]
    g_last = jnp.exp(gc[..., -1])

    def step(state, inp):
        u_c, w_c, a_c, qd_c, kd_c, gl_c = inp
        v_new = u_c - jnp.matmul(w_c, state)
        o = jnp.matmul(qd_c, state) + jnp.matmul(a_c, v_new)
        state = state * gl_c[..., None, None] + jnp.einsum('bhck,bhcv->bhkv', kd_c, v_new)
        return state, o

    xs = tuple(jnp.moveaxis(t, 2, 0) for t in (u, w, attn, q_dec, k_dec, g_last))
    s0 = jnp.zeros((Bsz, H, q.shape[-1], v.shape[-1]), f32)
    _, o = lax.scan(step, s0, xs)
    return o.transpose(1, 0, 3, 2, 4).reshape(Bsz, S, H, -1)

def _gdn_branch(qkv, z, b, a, conv_w, A_log, dt_bias, norm_w):
    Bsz, S, _ = qkv.shape
    f32 = jnp.float32
    qkv = jax.nn.silu(_causal_dwconv(qkv, conv_w))
    q, k, v = _split(qkv, (GDN_QK, GDN_QK, GDN_V))
    q = _l2norm(q.reshape(Bsz, S, GDN_HEADS, GDN_DK)) * (GDN_DK ** -0.5)
    k = _l2norm(k.reshape(Bsz, S, GDN_HEADS, GDN_DK))
    v = v.reshape(Bsz, S, GDN_HEADS, GDN_DV)
    beta = jax.nn.sigmoid(b.astype(f32))
    g = -jnp.exp(A_log.astype(f32)) * jax.nn.softplus(a.astype(f32) + dt_bias.astype(f32))
    o = _gated_delta_chunked(q, k, v, g, beta)
    o = _rmsnorm(o, norm_w) * jax.nn.silu(z.reshape(Bsz, S, GDN_HEADS, GDN_DV).astype(f32))
    return o.reshape(Bsz, S, GDN_V)

def _rwkv7_scan(r, w, k, v, kk, a):
    f32 = jnp.float32
    Bsz, _, H, N = r.shape
    xs = tuple(jnp.moveaxis(t.astype(f32), 1, 0) for t in (r, w, k, v, kk, a))

    def step(state, inp):
        r_t, w_t, k_t, v_t, kk_t, a_t = inp
        sk = jnp.einsum('bhvk,bhk->bhv', state, kk_t)
        state = (state * w_t[:, :, None, :]
                 - sk[..., None] * (kk_t * a_t)[:, :, None, :]
                 + v_t[..., None] * k_t[:, :, None, :])
        return state, jnp.einsum('bhvk,bhk->bhv', state, r_t)

    _, o = lax.scan(step, jnp.zeros((Bsz, H, N, N), f32), xs)
    return jnp.moveaxis(o, 0, 1)

def _rwkv7_branch(p, mu, w0, w2, a0, a2, g2, k_k, k_a, r_k, ln_w, ln_b):
    Bsz, S, _ = p.shape
    f32 = jnp.float32
    p = p.astype(f32)
    p = p + (_shift1(p) - p) * mu
    r, k, v, xw, xa, xg = _split(p, (RWKV_WIDTH, RWKV_WIDTH, RWKV_WIDTH, DECAY_LORA, AAA_LORA, GATE_LORA))
    w_log = -jax.nn.softplus(-(w0 + jnp.tanh(xw) @ w2)) - 0.5
    decay = jnp.exp(-jnp.exp(w_log))
    aa = jax.nn.sigmoid(a0 + xa @ a2)
    gg = jax.nn.sigmoid(xg) @ g2
    hs = lambda t: t.reshape(Bsz, S, RWKV_HEADS, RWKV_HEAD)
    kk = _l2norm(hs(k * k_k))
    k = k * (1.0 + (aa - 1.0) * k_a)
    r_h, k_h, v_h, aa_h = hs(r), hs(k), hs(v), hs(aa)
    o = _rwkv7_scan(r_h, hs(decay), k_h, v_h, kk, aa_h)
    mean = jnp.mean(o, axis=-1, keepdims=True)
    var = jnp.mean(jnp.square(o - mean), axis=-1, keepdims=True)
    o = ((o - mean) * lax.rsqrt(var + RWKV_GN_EPS)).reshape(Bsz, S, RWKV_WIDTH) * ln_w + ln_b
    bonus = jnp.sum(r_h * k_h * r_k, axis=-1, keepdims=True) * v_h
    return (o + bonus.reshape(Bsz, S, RWKV_WIDTH)) * gg

def _clamped_swiglu(gu):
    glu, lin = gu[..., ::2], gu[..., 1::2]
    glu = jnp.minimum(glu, SWIGLU_LIMIT)
    lin = jnp.clip(lin, -SWIGLU_LIMIT, SWIGLU_LIMIT)
    return glu * jax.nn.sigmoid(SWIGLU_ALPHA * glu) * (lin + 1.0)

def _moe(h, router_w, router_b, w_gu, b_gu, w_down, b_down):
    Bsz, S, D = h.shape
    f32 = jnp.float32
    xt = h.reshape(-1, D)
    T = xt.shape[0]
    logits = (xt @ router_w + router_b).astype(f32)
    top_val, top_idx = lax.top_k(logits, TOP_K)
    gate = jax.nn.softmax(top_val, axis=-1)
    A = T * TOP_K
    flat_e = top_idx.reshape(A)
    flat_tok = jnp.arange(A, dtype=jnp.int32) // TOP_K
    flat_gate = gate.reshape(A)
    order = jnp.argsort(flat_e)
    sorted_e = flat_e[order]
    counts = jnp.bincount(flat_e, length=N_EXPERTS)
    padded = ((counts + MOE_BLOCK - 1) // MOE_BLOCK) * MOE_BLOCK
    start_sorted = jnp.cumsum(counts) - counts
    end_padded = jnp.cumsum(padded)
    start_padded = end_padded - padded
    dest = start_padded[sorted_e] + (jnp.arange(A, dtype=jnp.int32) - start_sorted[sorted_e])
    n_blocks = -(-A // MOE_BLOCK) + N_EXPERTS
    P = n_blocks * MOE_BLOCK
    slot_tok = jnp.zeros((P,), jnp.int32).at[dest].set(flat_tok[order])
    slot_gate = jnp.zeros((P,), f32).at[dest].set(flat_gate[order])
    block_start = jnp.arange(n_blocks, dtype=jnp.int32) * MOE_BLOCK
    block_expert = jnp.minimum(jnp.searchsorted(end_padded, block_start, side='right'), N_EXPERTS - 1)
    xb = xt[slot_tok].reshape(n_blocks, MOE_BLOCK, D)

    def expert_block(args):
        xblk, e = args
        gu = xblk @ w_gu[e] + b_gu[e]
        return _clamped_swiglu(gu) @ w_down[e] + b_down[e]

    yb = lax.map(expert_block, (xb, block_expert)).reshape(P, D)
    y = jax.ops.segment_sum(yb.astype(f32) * slot_gate[:, None], slot_tok, num_segments=T)
    return y.reshape(Bsz, S, D).astype(h.dtype)

def setup_inputs(seed: int = 0) -> dict:
    key = jax.random.key(seed)
    ks = jax.random.split(key, 32)
    f32 = jnp.float32
    L, D = DEPTH, D_MODEL
    nrm = lambda k, shape, s: jax.random.normal(k, shape, f32) * s
    dt = jnp.exp(jax.random.uniform(ks[4], (L, GDN_HEADS), f32, math.log(1e-3), math.log(1e-1)))
    w0_base = jnp.linspace(-6.0, -1.0, RWKV_WIDTH, dtype=f32)
    return {
        "x": nrm(ks[0], (BATCH, SEQ, D), 1.0),
        "norm_mix": 1.0 + nrm(ks[1], (L, D), 0.1),
        "w_in": nrm(ks[2], (L, D, N_IN_COLS), D ** -0.5),
        "gdn_conv": nrm(ks[3], (L, CONV_W, GDN_QKV_COLS), CONV_W ** -0.5),
        "gdn_A_log": jnp.log(jax.random.uniform(ks[5], (L, GDN_HEADS), f32, 1.0, 16.0)),
        "gdn_dt_bias": dt + jnp.log(-jnp.expm1(-dt)),
        "gdn_norm": 1.0 + nrm(ks[6], (L, GDN_DV), 0.1),
        "rwkv_mu": jax.random.uniform(ks[7], (L, RWKV_COLS), f32),
        "rwkv_w0": w0_base + nrm(ks[8], (L, RWKV_WIDTH), 0.1),
        "rwkv_w2": nrm(ks[9], (L, DECAY_LORA, RWKV_WIDTH), 0.1),
        "rwkv_a0": nrm(ks[10], (L, RWKV_WIDTH), 0.1),
        "rwkv_a2": nrm(ks[11], (L, AAA_LORA, RWKV_WIDTH), AAA_LORA ** -0.5),
        "rwkv_g2": nrm(ks[12], (L, GATE_LORA, RWKV_WIDTH), GATE_LORA ** -0.5),
        "rwkv_k_k": 0.85 + nrm(ks[13], (L, RWKV_WIDTH), 0.05),
        "rwkv_k_a": 1.0 + nrm(ks[14], (L, RWKV_WIDTH), 0.05),
        "rwkv_r_k": nrm(ks[15], (L, RWKV_HEADS, RWKV_HEAD), 0.1),
        "rwkv_ln_w": 1.0 + nrm(ks[16], (L, RWKV_WIDTH), 0.1),
        "rwkv_ln_b": nrm(ks[17], (L, RWKV_WIDTH), 0.02),
        "proj_a": nrm(ks[18], (L, GDN_V, D), GDN_V ** -0.5),
        "proj_b": nrm(ks[19], (L, RWKV_WIDTH, D), RWKV_WIDTH ** -0.5),
        "w_out": nrm(ks[20], (L, D, D), D ** -0.5),
        "norm_ffn": 1.0 + nrm(ks[21], (L, D), 0.1),
        "router_w": nrm(ks[22], (L, D, N_EXPERTS), D ** -0.5),
        "router_b": nrm(ks[23], (L, N_EXPERTS), 0.01),
        "w_gate_up": nrm(ks[24], (L, N_EXPERTS, D, 2 * D_FF), D ** -0.5),
        "b_gate_up": nrm(ks[25], (L, N_EXPERTS, 2 * D_FF), 0.02),
        "w_down": nrm(ks[26], (L, N_EXPERTS, D_FF, D), D_FF ** -0.5),
        "b_down": nrm(ks[27], (L, N_EXPERTS, D), 0.02),
        "norm_final": 1.0 + nrm(ks[28], (D,), 0.1),
    }

def reference(x, norm_mix, w_in, gdn_conv, gdn_A_log, gdn_dt_bias, gdn_norm,
              rwkv_mu, rwkv_w0, rwkv_w2, rwkv_a0, rwkv_a2, rwkv_g2, rwkv_k_k, rwkv_k_a,
              rwkv_r_k, rwkv_ln_w, rwkv_ln_b, proj_a, proj_b, w_out, norm_ffn,
              router_w, router_b, w_gate_up, b_gate_up, w_down, b_down, norm_final):
    for l in range(DEPTH):
        h = _rmsnorm(x, norm_mix[l])
        p = h @ w_in[l]
        gdn_qkv, gdn_z, gdn_b, gdn_a, rwkv_p, gate_a, gate_b = _split(p, IN_WIDTHS)
        y_a = _gdn_branch(gdn_qkv, gdn_z, gdn_b, gdn_a, gdn_conv[l], gdn_A_log[l],
                          gdn_dt_bias[l], gdn_norm[l])
        y_b = _rwkv7_branch(rwkv_p, rwkv_mu[l], rwkv_w0[l], rwkv_w2[l], rwkv_a0[l], rwkv_a2[l],
                            rwkv_g2[l], rwkv_k_k[l], rwkv_k_a[l], rwkv_r_k[l],
                            rwkv_ln_w[l], rwkv_ln_b[l])
        merged = (jax.nn.sigmoid(gate_a.astype(jnp.float32)) * (y_a @ proj_a[l])
                  + jax.nn.sigmoid(gate_b.astype(jnp.float32)) * (y_b @ proj_b[l]))
        x = x + (merged @ w_out[l]).astype(x.dtype)
        h = _rmsnorm(x, norm_ffn[l])
        x = x + _moe(h, router_w[l], router_b[l], w_gate_up[l], b_gate_up[l], w_down[l], b_down[l])
    return _rmsnorm(x, norm_final)


_drawn_inputs = setup_inputs


def setup_inputs(seed=0):
    import zlib

    import numpy as np

    out = dict(_drawn_inputs(seed))
    spreads = {}
    factors = {'b_gate_up': 5.396, 'b_down': 6.261}
    for name, (base, spread) in spreads.items():
        noise = np.random.default_rng([zlib.crc32(name.encode()), seed]).standard_normal(out[name].shape)
        drawn = base * np.exp(spread * noise) if base else spread * noise
        out[name] = __import__('jax').numpy.asarray(drawn.astype(out[name].dtype))
    for name, factor in factors.items():
        out[name] = (out[name] * factor).astype(out[name].dtype)
    return out
```

```python
from contextlib import ExitStack
from math import exp

import numpy as np
import concourse.bass as bass
from concourse import mybir

F32 = mybir.dt.float32
I32 = mybir.dt.int32
U32 = mybir.dt.uint32
U8 = mybir.dt.uint8
ALU = mybir.AluOpType
ACT = mybir.ActivationFunctionType
AX = mybir.AxisListType

P = 128
T = 256
NT = T // P
D = 1024
KT = D // P
HEADS = 8
NE = 32
SLOTS = 64
PANEL = 512
EPS = 1e-6
GN_EPS = 64e-5
DECAY = exp(-0.5)
GLU_ALPHA, GLU_LIMIT = 1.702, 7.0

C_Q, C_K, C_V, C_Z, C_B, C_A = 0, 1024, 2048, 3072, 4096, 4104
C_R, C_RK, C_RV, C_LORA, C_GA, C_GB = 4112, 5136, 6160, 7184, 7440, 8464

K_ID, K_ONE, K_BLK, K_INC, K_STR, K_M4, K_SEL, K_IOTA, K_COL = 0, 128, 256, 384, 512, 640, 1152, 2176, 2304
K_N = 2320
LEVELS = 7

ROWS_A = 8 + 4 * 24
PB = 128
(P_MU, P_A0, P_KK, P_KA, P_RK, P_LNW, P_LNB, P_NF, P_GN) = (PB + r for r in (0, 26, 34, 42, 50, 58, 66, 74, 82))
ROWS_B = 83


def shape_constants(slots=SLOTS):
    t = np.arange(P)
    c = np.zeros((P, K_N), np.float32)
    c[:, K_ID:K_ID + P] = np.eye(P)
    c[:, K_ONE:K_ONE + P] = 1
    c[:, K_BLK:K_BLK + P] = (t[:, None] // 64) == (t[None] // 64)
    incl = (t[:, None] <= t[None]).astype(np.float32)
    strict = (t[:, None] < t[None]).astype(np.float32)
    c[:, K_INC:K_INC + P] = incl
    c[:, K_STR:K_STR + P] = strict
    c[:, K_M4:K_M4 + 4 * P] = np.concatenate([-strict, incl, strict, incl], 1)
    for h in range(HEADS):
        c[h, K_SEL + h * P:K_SEL + (h + 1) * P] = 1
    j = np.arange(P) % 64
    c[:, K_IOTA:K_IOTA + P] = np.where(j < slots, j, -1000)
    c[:, K_COL:K_COL + 8] = [EPS, P * EPS, GN_EPS, 1.0, 0, 0, 0, 0]
    c[:, K_COL + 8:K_COL + 16] = [b * slots if b * slots < T else 1e9 for b in range(8)]
    m = np.zeros((P, LEVELS, 2, P), np.float32)
    for lv in range(LEVELS):
        b = 1 << lv
        low = ((t[:, None] // (2 * b)) == (t[None] // (2 * b))) & ((t[:, None] // b) % 2 == 1) & ((t[None] // b) % 2 == 0)
        m[:, lv, 0], m[:, lv, 1] = low, low.T
    return c, m.reshape(P, -1)


def hybrid_block(nc, A, slots=SLOTS):
    ctx = ExitStack()
    with ctx:
        def sb(name, shape, dt=F32):
            return ctx.enter_context(nc.sbuf_tensor(name, shape, dt))

        sems = {}

        def S(name):
            if name not in sems:
                sems[name] = ctx.enter_context(nc.semaphore(name))
            return sems[name]

        cst = sb("cst", [P, K_N])
        msk = sb("msk", [P, LEVELS * 2 * P], U8)
        lvl = sb("lvl", [P, 2, P], U8)
        par = sb("par", [P, 2 * P])
        omm = sb("omm", [P, 26])
        omka = sb("omka", [P, 8])
        small = sb("small", [P, 256])
        lora = sb("lora", [P, 2, T])
        x = sb("x", [P, NT, D])
        ring = sb("ring", [P, 6 * 2048])
        scr = sb("scr", [P, 6 * 2048])
        arena = sb("arena", [P, 11 * 2048])
        passes = sb("passes", [1, 1], I32)
        ps = ctx.enter_context(nc.psum_tensor("ps", [P, 8, 512], F32))

        rows = scr[0:8, 10240:10240 + 6 * T].rearrange("p (w t) -> p w t", w=6)
        R = [arena[:, 2048 * r:2048 * (r + 1)] for r in range(11)]
        W3 = [r.rearrange("p (m t) -> p m t", m=8) for r in R]
        W4 = [r.rearrange("p (c m t) -> p c m t", c=2, m=8) for r in R]

        def C(k, n=P, rows_=P):
            return cst[0:rows_, k:k + n]

        ident, ones, blk = C(K_ID), C(K_ONE), C(K_BLK)
        incl, strict = C(K_INC), C(K_STR)

        def col(j):
            return cst[:, K_COL + j:K_COL + j + 1]

        def cols8(j, n=T, k=8):
            return par[:, j:j + k].unsqueeze(2).broadcast_to([P, k, n])

        panel = [ring[:, s * 4096:(s + 1) * 4096].rearrange("p (k c) -> p k c", k=KT) for s in range(3)]
        hT = W3[0]
        KQ = arena[:, 2048:6144].rearrange("p (h c w t) -> p h c w t", h=8, c=2, w=2)
        AR = arena[:, 2048:6144].rearrange("p (m c w t) -> p m c w t", m=8, c=2, w=2)
        BK = arena[:, 6144:10240].rearrange("p (m c w t) -> p m c w t", m=8, c=2, w=2)
        MM = scr[:, 0:8192].rearrange("p (u w t) -> p u w t", u=16, w=4)
        TI = scr[:, 8192:10240].rearrange("p (u t) -> p u t", u=16)
        TI2 = scr[:, 8192:9216]
        QDt = R[4][:, 0:1024]
        TT = scr[:, 10240:12288].rearrange("p (u t) -> p u t", u=16)
        Ep = scr[:, 0:2064].rearrange("p (m c t) -> p m c t", m=8, c=2)
        En = scr[:, 2064:4112].rearrange("p (m c t) -> p m c t", m=8, c=2)
        AA, T1, SQ = (scr[:, 4112 + 2048 * n:6160 + 2048 * n] for n in range(3))
        LS = ring[:, 4096:8192]

        ss, rstd = small[:, 0:2], small[:, 2:4]
        cc, ncc = small[:, 8:24], small[:, 24:40]
        dsc = small[:, 40:48]
        alog, dtb, negA = small[0:8, 56:57], small[0:8, 57:58], small[0:8, 58:59]
        tb = small[:, 64:128].rearrange("p (w c h) -> p w c h", w=4, c=2)

        w_in = A["w_in"].rearrange("l (k p) c -> p (l k) c", p=P)
        w_proj = [A[n].rearrange("l (k p) c -> p (l k) c", p=P) for n in ("proj_a", "proj_b", "w_out")]
        w_gu = A["w_gate_up"].rearrange("l e (k p) c -> p (l e k) c", p=P)
        w_dn = A["w_down"].rearrange("l e (k p) c -> p (l e k) c", p=P)
        b_gu = A["b_gate_up"].rearrange("l e c -> (l e) c")

        H2 = R[0].rearrange("p (c d) -> p c d", c=2)
        h2T = W3[1]
        rt_w = R[3][:, 0:256].rearrange("p (k e) -> p k e", k=KT)
        rt_b = R[3][0:1, 256:288]
        tab = R[2][:, 0:33 * 4].rearrange("p (e w) -> p e w", e=33)
        lg, sel, gt, tmp32 = (R[2][:, 256 + 64 * n:320 + 64 * n].rearrange("p (c e) -> p c e", c=2) for n in range(4))
        top, topi = R[2][:, 512:528].rearrange("p (c e) -> p c e", c=2), R[2][:, 528:544].rearrange("p (c e) -> p c e", c=2)
        topf = R[2][:, 544:560].rearrange("p (c e) -> p c e", c=2)
        nmx, gsum, grec = R[2][:, 560:562], R[2][:, 562:564], R[2][:, 564:566]
        cur = R[2][:, 568:576].rearrange("p (q w) -> p q w", q=2)
        cnt = R[2][0:1, 576:608]
        cmax, cge, csum = R[2][0:1, 608:609], R[2][0:1, 610:618], R[2][0:1, 618:619]
        gT = R[2][0:32, 640:896]
        nfb = R[5][:, 0:1024]
        bdn = R[4][0:32, 0:1024]
        brow = R[5][0:1, 1024:2048], R[3][0:1, 1024:2048]
        Psel = R[6][:, 0:512].rearrange("p (q c s) -> p q c s", q=2, c=2)
        Pgat = R[6][:, 512:1024].rearrange("p (q c s) -> p q c s", q=2, c=2)
        PgT = R[6][:, 1024:1536].rearrange("p (q c t) -> p q c t", q=2, c=2)
        xgT = R[7][:, 0:1024].rearrange("p (q k s) -> p q k s", q=2, k=KT)
        ysb = R[7][:, 1024:2048].rearrange("p (q n) -> p q n", q=2)
        glu, sgm = R[8][:, 0:512], R[8][:, 512:1024]
        lin, act_h = R[8][:, 1024:1536], R[8][:, 1536:2048]
        actT = R[9][:, 0:512].rearrange("p (c s) -> p c s", c=4)

        def gu_slot(s):
            return ring[:, s * 2048:(s + 1) * 2048] if s < 6 else scr[:, (s - 6) * 2048:(s - 5) * 2048]

        def dn_slot(s):
            return scr[:, (s + 2) * 2048:(s + 3) * 2048].rearrange("p (k c) -> p k c", k=2)

        block = ctx.enter_context(nc.Block())

        first = [C_Q, C_K, C_V, C_Z, C_R, C_RK, C_RV, C_GA, C_GB]
        MM0 = 4
        HB = 6

        @block.sync
        def _(sp):
            def load(dst, src, sem):
                sp.dma_start(dst, src).then_inc(S(sem), 16)

            load(x[:, :, :], A["x"].rearrange("b (c p) d -> p (b c) d", p=P), "x_in")
            load(cst[:, :], A["consts"], "cst_in")
            load(R[7][0:8, 0:P], A["norm_mix"].rearrange("l (r c) -> (l r) c", c=P), "par_in")
            load(R[7][8:ROWS_A, 0:P], A["gdn_conv"].rearrange("l w (r c) -> (l w r) c", c=P), "par_in")
            at = 0
            for name, n in (("rwkv_mu", 26), ("rwkv_a0", 8), ("rwkv_k_k", 8), ("rwkv_k_a", 8), ("rwkv_r_k", 8),
                            ("rwkv_ln_w", 8), ("rwkv_ln_b", 8), ("norm_ffn", 8), ("gdn_norm", 1)):
                src = A[name].rearrange("l h n -> l (h n)") if name == "rwkv_r_k" else A[name]
                load(R[7][at:at + n, P:2 * P], src.rearrange("l (r c) -> (l r) c", c=P), "par_in")
                at += n
            load(panel[0][:, :, 0:256], w_in[:, :, C_LORA:C_LORA + 256], "panel_in0")
            load(panel[0][:, :, 256:272], w_in[:, :, C_B:C_B + 16], "panel_in0")
            load(scr[:, 0:LEVELS * 2 * P], A["masks"], "msk_in")
            load(alog, A["gdn_A_log"].rearrange("l h -> h l"), "row_in")
            load(dtb, A["gdn_dt_bias"].rearrange("l h -> h l"), "row_in")
            with sp.Fori(0, 2) as i:
                for j in range(9):
                    sp.wait_ge(S("mm_ready"), 18 * i + (MM0 + 2 * j - 2))
                    load(panel[(1 + j) % 3], w_in[:, :, bass.ds(512 * i + first[j], PANEL)], f"panel_in{(1 + j) % 3}")
            sp.wait_ge(S("mm_ready"), MM0 + 2 + 2 * 16)
            load(LS[0:64, 0:1024], A["rwkv_w2"].rearrange("l r c -> (l r) c"), "panel_in1")
            load(LS[64:128, 0:1024], A["rwkv_a2"].rearrange("l r c -> (l r) c"), "panel_in1")
            load(LS[:, 1024:2048], A["rwkv_g2"].rearrange("l r c -> (l r) c"), "panel_in1")
            load(LS[0:1, 2048:3072], A["rwkv_w0"], "panel_in1")
            for q in range(6):
                sp.wait_ge(*[(S("mm_ready"), MM0 + 36), (S("mm_ready"), MM0 + 38), (S("gg_ready"), 4),
                             (S("pj_ready"), 2), (S("pj_ready"), 4), (S("pj_ready"), 6)][q])
                load(panel[(20 + q) % 3], w_proj[q // 2][:, :, PANEL * (q % 2):PANEL * (q % 2 + 1)], f"panel_in{(20 + q) % 3}")
            sp.wait_ge(S("pj_ready"), 8)
            load(rt_w, A["router_w"].rearrange("l (k p) e -> p (l k) e", p=P), "rt_in")
            load(rt_b, A["router_b"], "rt_in")
            load(bdn, A["b_down"].rearrange("l e c -> (l e) c"), "bdn_in")
            load(nfb, A["norm_final"].rearrange("(a d) -> a d", a=1).partition_broadcast(P).rearrange("p a d -> p (a d)"), "nf_in")
            sp.wait_ge(S("pj_ready"), 12)

            def expert(it, e):
                for s in range(8):
                    sp.wait_ge(S("gu_used"), 8 * it + (s + 1))
                    load(gu_slot(s), w_gu[:, bass.ds(8 * e + s, 1), :].rearrange("p k c -> p (k c)"), f"gu_in{s}")
                sp.wait_ge(S("brow_used"), it + 1)
                for n in range(2):
                    load(brow[n], b_gu[bass.ds(e, 1), 1024 * n:1024 * (n + 1)], "brow_in")
                for s in range(4):
                    sp.wait_ge(S("dn_used"), 4 * it + (s + 1))
                    load(dn_slot(s), w_dn[:, bass.ds(8 * e + 2 * s, 2), :], f"dn_in{s}")

            with sp.Fori(0, NE) as e:
                expert(e, e)
            sp.wait_ge(S("passes_known"), 1)
            n = sp.value_load(passes[0:1, 0:1], min_val=1, max_val=T // slots)
            with sp.If(n > 1):
                with sp.Fori(1, n) as b:
                    with sp.Fori(0, NE) as e:
                        expert(NE * b + e, e)
            sp.wait_ge(S("y_ready"), 1)
            load(A["out"].rearrange("b (c p) d -> p (b c) d", p=P), R[1].rearrange("p (c d) -> p c d", c=2), "out_done")
            sp.wait_ge(S("out_done"), 16)

        @block.tensor
        def _(pe):
            mm, tr = nc.tensor.matmul, nc.tensor.transpose

            for name, v in (("mm_ready", MM0), ("gu_used", 8), ("dn_used", 4), ("brow_used", 1)):
                pe.sem_inc(S(name), v)
            pe.wait_ge(S("cst_in"), 16)
            pe.wait_ge(S("par_in"), 16 * 11)
            tr(ps[:, 6, 0:ROWS_A], R[7][0:ROWS_A, 0:P], cst[0:ROWS_A, 0:ROWS_A])
            tr(ps[:, 6, P:P + ROWS_B], R[7][0:ROWS_B, P:2 * P], cst[0:ROWS_B, 0:ROWS_B]).then_inc(S("par_T"), 1)
            pe.wait_ge(S("xs_ready"), 2)
            xs = R[10].rearrange("p (c d) -> p c d", c=2)
            for k in range(KT):
                for c in range(NT):
                    ins = tr(ps[:, k // 2, 256 * (k % 2) + P * c:256 * (k % 2) + P * (c + 1)], xs[:, c, P * k:P * (k + 1)], ident)
            ins.then_inc(S("xT_ready"), 1)

            pe.wait_ge(S("hT_ready"), 1)
            pe.wait_ge(S("panel_in0"), 32)
            for f, (c0, w) in enumerate(((256, 8), (264, 8))):
                for k in range(KT):
                    ins = mm(ps[0:8, 0, T * f:T * (f + 1)], panel[0][:, k, c0:c0 + w], hT[:, k, :], start=k == 0, stop=k == KT - 1)
            ins.then_inc(S("mm_ready"), 1)
            for f in range(2):
                for k in range(KT):
                    ins = mm(ps[:, 1, T * f:T * (f + 1)], panel[0][:, k, P * f:P * (f + 1)], hT[:, k, :], start=k == 0, stop=k == KT - 1)
            ins.then_inc(S("mm_ready"), 1)
            with pe.Fori(0, 2) as i:
                for u in range(18):
                    j, half = u // 2, u % 2
                    if half == 0:
                        pe.wait_ge(S(f"panel_in{(1 + j) % 3}"), 48 * i + 16 * (j // 3 + (3 if (1 + j) % 3 == 0 else 1)))
                    pe.wait_ge(S("act_first"), 18 * i + (u - 3) if u >= 4 else (13 + u) * i + 2)
                    pe.wait_ge(S("dve_free"), 14 * i + (min(u - 6, 13) + 3 if u >= 6 else min(u + 1, 2)))
                    for f in range(2):
                        for k in range(KT):
                            ins = mm(ps[:, (2 + u) % HB, T * f:T * (f + 1)],
                                     panel[(1 + j) % 3][:, k, P * (2 * half + f):P * (2 * half + f + 1)], hT[:, k, :],
                                     start=k == 0, stop=k == KT - 1)
                    ins.then_inc(S("mm_ready"), 1)

            pe.wait_ge(S("act_first"), 38)
            pe.wait_ge(S("dve_free"), 30)
            for u in range(8):
                pe.wait_ge(S("gsq_ready"), u + 1)
                mm(ps[:, u, :], ones, scr[:, 512 * u:512 * (u + 1)], start=True, stop=True).then_inc(S("gnm_ready"), 1)
            pe.wait_ge(S("gate_row"), 5)
            pe.wait_ge(S("gnm_read"), 8)
            for w in range(4):
                for c in range(NT):
                    ins = tr(ps[:, 6, 8 * (2 * w + c):8 * (2 * w + c) + 8], rows[0:8, w, P * c:P * (c + 1)], cst[0:8, 0:8])
            ins.then_inc(S("tb_ready"), 1)
            pe.wait_ge(S("conv_done"), 12)
            for w in range(4):
                for q in range(4):
                    ins = tr(ps[:, w, P * q:P * (q + 1)], W3[4][:, 4 * (w % 2) + q, P * (w // 2):P * (w // 2 + 1)], ident)
                ins.then_inc(S("vT_ready"), 1)
            pe.wait_ge(S("vT_read"), 4)
            pe.wait_ge(S("kq_ready"), 8)
            for h in range(HEADS):
                b = 2 * (h % 2)
                if h >= 2:
                    pe.wait_ge(S("head_done"), h - 1)
                mm(ps[:, b, :], cst[0:8, K_SEL + P * h:K_SEL + P * (h + 1)], rows[0:8, 0:2, :].rearrange("h w t -> h (w t)"), start=True, stop=True)
                for c in range(NT):
                    ins = mm(ps[:, b + 1, T * c:T * (c + 1)], KQ[:, h, c, 0, :], KQ[:, h, c, :, :].rearrange("p w t -> p (w t)"), start=True, stop=True)
                ins.then_inc(S("head_ready"), 1)

            def inverse(v):
                WS = R[9] if v else R[0]
                with pe.Fori(0, LEVELS) as lv:
                    for g in range(4):
                        pe.wait_ge(S("t_done"), 4 * lv + (32 * v + g + 1))
                        for q in range(4):
                            ins = mm(ps[:, g, P * q:P * (q + 1)], MM[:, 4 * g + q, 0, :], TI[:, 4 * g + q, :], start=True, stop=True)
                        ins.then_inc(S("w_ready"), 1)
                    for g in range(4):
                        pe.wait_ge(S("w_copied"), 4 * lv + (28 * v + g + 1))
                        pe.wait_ge(S("t_done"), 4 * lv + (32 * v + g + 3))
                        b = 4 + 2 * (g % 2)
                        for q in range(4):
                            mm(ps[:, b, P * q:P * (q + 1)], TT[:, 4 * g + q, :], WS[:, 512 * g + P * q:512 * g + P * (q + 1)], start=True, stop=True)
                        for q in range(4):
                            ins = mm(ps[:, b + 1, P * q:P * (q + 1)], WS[:, 512 * g + P * q:512 * g + P * (q + 1)], TT[:, 4 * g + q, :], start=True, stop=True)
                        ins.then_inc(S("t_ready"), 1)
                pe.wait_ge(S("t_done"), 32 * v + 32)

            pe.wait_ge(S("head_done"), 8)
            inverse(0)

            X, Kd, U = R[0][:, 0:1024], R[0][:, 1024:2048], scr[:, 8192:10240]
            QD, S1 = R[4][:, 0:1024], R[4][:, 1024:2048]
            hs = lambda t, h: t[:, P * h:P * (h + 1)]
            pe.wait_ge(S("gx_ready"), 1)
            for h in range(HEADS):
                ins = mm(ps[:, h // 4, P * (h % 4):P * (h % 4 + 1)], TT[:, 2 * h, :], hs(X, h), start=True, stop=True)
            ins.then_inc(S("gu0_ready"), 1)
            for h in range(HEADS):
                ins = tr(ps[:, 2 + h // 4, P * (h % 4):P * (h % 4 + 1)], KQ[:, h, 0, 0, :], ident)
            ins.then_inc(S("gkd_ready"), 1)
            pe.wait_ge(S("gu0_copied"), 1)
            pe.wait_ge(S("gkd_copied"), 1)
            for h in range(HEADS):
                ins = mm(ps[:, 4 + h // 4, P * (h % 4):P * (h % 4 + 1)], hs(Kd, h), hs(U, h), start=True, stop=True)
            ins.then_inc(S("gs1_ready"), 1)
            pe.wait_ge(S("gs1_copied"), 1)
            for h in range(HEADS):
                ins = mm(ps[:, 6 + h // 4, P * (h % 4):P * (h % 4 + 1)], KQ[:, h, 1, 0, :], hs(S1, h), start=True, stop=True)
            ins.then_inc(S("gks_ready"), 1)
            pe.wait_ge(S("gx_ready"), 2)
            for h in range(HEADS):
                ins = mm(ps[:, 2 + h // 4, P * (h % 4):P * (h % 4 + 1)], TT[:, 2 * h + 1, :], hs(X, h), start=True, stop=True)
            ins.then_inc(S("gu1_ready"), 1)
            pe.wait_ge(S("gu1_copied"), 1)
            for h in range(HEADS):
                b = (0, 1, 4, 5)[h // 2]
                o0, o1 = (ps[:, b, T * (h % 2) + P * c:T * (h % 2) + P * (c + 1)] for c in range(2))
                mm(o0, hs(U, h), MM[:, 2 * h, 1, :], start=True, stop=True)
                mm(o1, hs(S1, h), hs(QD, h), start=True, stop=False)
                ins = mm(o1, U[:, 1024 + P * h:1024 + P * (h + 1)], MM[:, 2 * h + 1, 1, :], start=False, stop=True)
                if h % 2:
                    ins.then_inc(S("got_ready"), 1)
            for q in range(4):
                pe.wait_ge(S("osq_ready"), q + 1)
                mm(ps[:, (2, 3, 6, 7)[q], :], ones, R[1][:, 512 * q:512 * (q + 1)], start=True, stop=True).then_inc(S("onm_ready"), 1)

            pe.wait_ge(S("panel_in1"), 16 * 10)
            pe.wait_ge(S("lora_act"), 1)
            pe.wait_ge(S("got_read"), 4)
            for u in range(4):
                c, n = u // 2, u % 2
                b = (0, 1, 4, 5)[u]
                mm(ps[:, b, :], lora[0:64, 0, P * c:P * (c + 1)], LS[0:64, 512 * n:512 * (n + 1)], start=True, stop=False)
                mm(ps[:, b, :], cst[0:1, K_ONE:K_ONE + P], LS[0:1, 2048 + 512 * n:2560 + 512 * n], start=False, stop=True).then_inc(S("rz_ready"), 1)
            pe.wait_ge(S("onm_read"), 4)
            for m in range(8):
                b = (2, 3, 6, 7)[m // 2]
                ins = mm(ps[:, b, T * (m % 2):T * (m % 2 + 1)], LS[64:128, P * m:P * (m + 1)], lora[64:128, 0, :], start=True, stop=True)
                if m % 2:
                    ins.then_inc(S("raa_ready"), 1)
            SG = R[0].rearrange("p (c d) -> p c d", c=2)
            for m in range(8):
                b = (0, 1, 4, 5)[m // 2]
                if m % 2 == 0:
                    pe.wait_ge(S("rz_read"), 4)
                for c in range(NT):
                    ins = mm(ps[:, b, P * (2 * (m % 2) + c):P * (2 * (m % 2) + c + 1)], SG[:, c, P * m:P * (m + 1)], incl, start=True, stop=True)
                if m % 2:
                    ins.then_inc(S("rg_ready"), 1)
            pe.wait_ge(S("raa_read"), 8)
            pe.wait_ge(S("rsq_ready"), 1)
            for q in range(4):
                mm(ps[:, (2, 3, 6, 7)[q], :], blk, SQ[:, 512 * q:512 * (q + 1)], start=True, stop=True).then_inc(S("rnm_ready"), 1)
            pe.wait_ge(S("rexp_done"), 1)
            for w in range(4):
                for q in range(4):
                    ins = tr(ps[:, (0, 1, 4, 5)[w], P * q:P * (q + 1)], W3[10][:, 4 * (w % 2) + q, P * (w // 2):P * (w // 2 + 1)], ident)
                ins.then_inc(S("rv_ready"), 1)
            pe.wait_ge(S("rnm_read"), 4)
            pe.wait_ge(S("rrk_ready"), 1)
            for q in range(4):
                mm(ps[:, (2, 3, 6, 7)[q], :], blk, R[8][:, 512 * q:512 * (q + 1)], start=True, stop=True).then_inc(S("rbn_ready"), 1)

            V = R[0].rearrange("p (c d) -> p c d", c=2)
            for hf in range(2):
                pe.wait_ge(S("prep_done"), 1)
                pe.wait_ge(S("rv_read"), 4)
                if hf:
                    pe.wait_ge(S("rot_read"), 1)
                for u in range(16):
                    m, p, c = 4 * hf + u // 4, (u // 2) % 2, u % 2
                    q = slice(64 * p, 64 * p + 64)
                    if u >= 4:
                        pe.wait_ge(S("rm_read"), 16 * hf + u - 3)
                    rhs = AR[q, m, c, :, :].rearrange("p w t -> p (w t)")
                    mm(ps[:, u % 4, 0:T], BK[q, m, c, 0, :], rhs, start=True, stop=True)
                    mm(ps[:, u % 4, T:2 * T], BK[q, m, c, 1, :], rhs, start=True, stop=True).then_inc(S("rm_ready"), 1)
                pe.wait_ge(S("rm_read"), 16 * (hf + 1))
                inverse(1 + hf)
                vh = lambda c, h: V[:, c, 512 * hf + 64 * h:512 * hf + 64 * h + 64]
                YS, KB = R[9][:, 0:512], R[9][:, 1024:2048]
                SS = R[9][:, 512:768]
                U0, U1 = scr[:, 8192:8704], scr[:, 8704:9216]
                for h in range(8):
                    ins = mm(ps[:, 0, 64 * h:64 * h + 64], MM[:, 2 * h, 2, :], vh(0, h), start=True, stop=True)
                ins.then_inc(S("ry_ready"), 1)
                for w in range(2):
                    for m in range(4):
                        ins = tr(ps[:, 2 + w, P * m:P * (m + 1)], BK[:, 4 * hf + m, 0, w, :], ident)
                ins.then_inc(S("rkb_ready"), 1)
                pe.wait_ge(S("ry_copied"), 2 * hf + 1)
                for h in range(8):
                    ins = mm(ps[:, 1, 64 * h:64 * h + 64], TT[:, 2 * h, :], YS[:, 64 * h:64 * h + 64], start=True, stop=True)
                ins.then_inc(S("ru_ready"), 1)
                pe.wait_ge(S("ru_copied"), 2 * hf + 1)
                pe.wait_ge(S("rkb_copied"), hf + 1)
                for h in range(8):
                    m, p = h // 2, h % 2
                    out = ps[64 * p:64 * p + 64, 4, 64 * m:64 * m + 64]
                    mm(out, KB[:, 512 + P * m + 64 * p:512 + P * m + 64 * p + 64], vh(0, h), start=True, stop=False)
                    ins = mm(out, KB[:, P * m + 64 * p:P * m + 64 * p + 64], U0[:, 64 * h:64 * h + 64], start=False, stop=True)
                ins.then_inc(S("rs_ready"), 1)
                pe.wait_ge(S("rs_copied"), hf + 1)
                for h in range(8):
                    m, p = h // 2, h % 2
                    q = slice(64 * p, 64 * p + 64)
                    out = ps[:, 5 + 2 * p, 64 * m:64 * m + 64]
                    mm(out, AR[q, 4 * hf + m, 1, 0, :], SS[q, 64 * m:64 * m + 64], start=True, stop=False)
                    ins = mm(out, MM[:, 2 * h + 1, 2, :], vh(1, h), start=False, stop=True)
                ins.then_inc(S("ry_ready"), 1)
                pe.wait_ge(S("ry_copied"), 2 * hf + 2)
                for h in range(8):
                    ins = mm(ps[:, 6, 64 * h:64 * h + 64], TT[:, 2 * h + 1, :], YS[:, 64 * h:64 * h + 64], start=True, stop=True)
                ins.then_inc(S("ru_ready"), 1)
                pe.wait_ge(S("ru_copied"), 2 * hf + 2)
                for h in range(8):
                    m, p = h // 2, h % 2
                    q = slice(64 * p, 64 * p + 64)
                    o0, o1 = (ps[q, 2 + m // 2, T * (m % 2) + P * c:T * (m % 2) + P * (c + 1)] for c in range(2))
                    mm(o0, vh(0, h), MM[:, 2 * h, 3, :], start=True, stop=False)
                    mm(o0, U0[:, 64 * h:64 * h + 64], MM[:, 2 * h, 1, :], start=False, stop=True)
                    mm(o1, vh(1, h), MM[:, 2 * h + 1, 3, :], start=True, stop=False)
                    mm(o1, U1[:, 64 * h:64 * h + 64], MM[:, 2 * h + 1, 1, :], start=False, stop=False)
                    ins = mm(o1, SS[q, 64 * m:64 * m + 64], AR[q, 4 * hf + m, 1, 1, :], start=False, stop=True)
                ins.then_inc(S("rot_ready"), 1)

            pe.wait_ge(S("rot_read"), 2)
            for q in range(4):
                mm(ps[:, 4 + q, :], blk, R[10][:, 512 * q:512 * (q + 1)], start=True, stop=True).then_inc(S("rmu_ready"), 1)
            for q in range(4):
                pe.wait_ge(S("rvs_ready"), q + 1)
                mm(ps[:, q, :], blk, R[0][:, 512 * q:512 * (q + 1)], start=True, stop=True).then_inc(S("rvr_ready"), 1)
            pe.wait_ge(S("rmu_read"), 4)
            for m in range(8):
                ins = mm(ps[:, 4 + m // 2, T * (m % 2):T * (m % 2 + 1)], LS[:, 1024 + P * m:1024 + P * (m + 1)], lora[:, 1, :], start=True, stop=True)
                if m % 2:
                    ins.then_inc(S("gg_ready"), 1)

            pe.wait_ge(S("ya_ready"), 1)
            pe.wait_ge(S("rvr_read"), 4)
            for u in range(8):
                q = u // 2
                if u == 4:
                    pe.wait_ge(S("yb_ready"), 1)
                if u % 2 == 0:
                    pe.wait_ge(S(f"panel_in{(20 + q) % 3}"), (16 * 7, 16 * 9, 16 * 11, 16 * 8)[q])
                src = W3[5] if u < 4 else W3[10]
                for f in range(2):
                    for k in range(KT):
                        ins = mm(ps[:, u, T * f:T * (f + 1)], panel[(20 + q) % 3][:, k, P * (2 * (u % 2) + f):P * (2 * (u % 2) + f + 1)],
                                 src[:, k, :], start=k == 0, stop=k == KT - 1)
                ins.then_inc(S("pj_ready"), 1)
            pe.wait_ge(S("merged"), 1)
            for n in range(2):
                pe.wait_ge(S(f"panel_in{(24 + n) % 3}"), (16 * 10, 16 * 12)[n])
                for c in range(NT):
                    for k in range(KT):
                        ins = mm(ps[:, 2 * n + c, :], W3[6][:, k, P * c:P * (c + 1)], panel[(24 + n) % 3][:, k, :], start=k == 0, stop=k == KT - 1)
                    ins.then_inc(S("pj_ready"), 1)

            pe.wait_ge(S("h2_ready"), 1)
            for k in range(KT):
                for c in range(NT):
                    ins = tr(ps[:, 4 + k // 2, 256 * (k % 2) + P * c:256 * (k % 2) + P * (c + 1)], H2[:, c, P * k:P * (k + 1)], ident)
            ins.then_inc(S("h2T_ready"), 1)
            pe.wait_ge(S("h2T_copied"), 1)
            pe.wait_ge(S("rt_in"), 32)
            for c in range(NT):
                out = ps[:, 0, NE * c:NE * (c + 1)]
                for k in range(KT):
                    mm(out, h2T[:, k, P * c:P * (c + 1)], rt_w[:, k, :], start=k == 0, stop=False)
                ins = mm(out, cst[0:1, K_ONE:K_ONE + P], rt_b, start=False, stop=True)
            ins.then_inc(S("lg_ready"), 1)
            pe.wait_ge(S("sel_ready"), 1)
            mm(ps[:, 1, 0:NE], strict, sel[:, 0, :], start=True, stop=True)
            mm(ps[:, 1, NE:2 * NE], strict, sel[:, 1, :], start=True, stop=False)
            mm(ps[:, 1, NE:2 * NE], ones, sel[:, 0, :], start=False, stop=True)
            mm(ps[0:1, 1, 2 * NE:3 * NE], ones[:, 0:1], sel[:, 0, :], start=True, stop=False)
            mm(ps[0:1, 1, 2 * NE:3 * NE], ones[:, 0:1], sel[:, 1, :], start=False, stop=True)
            for c in range(NT):
                ins = tr(ps[0:NE, 2, P * c:P * (c + 1)], gt[:, c, :], ident)
            ins.then_inc(S("pos_ready"), 1)
            pe.wait_ge(S("pos_read"), 1)
            pe.wait_ge(S("bdn_in"), 16)
            for c in range(NT):
                for n in range(2):
                    mm(ps[:, 2 * c + n, :], gT[:, P * c:P * (c + 1)], bdn[:, 512 * n:512 * (n + 1)], start=True, stop=False, skip_group_check=True)

            def scatter(q, last=False):
                for c in range(NT):
                    for n in range(2):
                        s = slice(64 * n, 64 * n + 64)
                        ins = mm(ps[:, 2 * c + n, :], PgT[s, q, c, :], ysb[s, q, :], start=False, stop=last, skip_group_check=True)
                return ins

            def expert(it, q):
                pe.wait_ge(S("sel_made"), it + 1)
                pe.wait_ge(S("at_copied"), it + 1)
                for k in range(KT):
                    for c in range(NT):
                        ins = mm(ps[:, 7, 64 * k:64 * k + 64], H2[:, c, P * k:P * (k + 1)], Psel[:, q, c, 0:64], start=c == 0, stop=c == NT - 1)
                ins.then_inc(S("xg_ready"), 1)
                pe.wait_ge(S("xg_copied"), it + 1)
                for c in range(NT):
                    ins = tr(ps[:, 7, P * c:P * (c + 1)], Pgat[:, q, c, :], ident)
                ins.then_inc(S("pt_ready"), 1)
                for k in range(KT):
                    pe.wait_ge(S(f"gu_in{k}"), 16 * it + 16)
                    for n in range(4):
                        s = slice(64 * (n % 2), 64 * (n % 2) + 64)
                        ins = mm(ps[s, 4 + n // 2, :], xgT[:, q, k, :], gu_slot(k)[:, 512 * n:512 * (n + 1)], start=k == 0, stop=False, skip_group_check=True)
                    ins.then_inc(S("gu_used"), 1)
                pe.wait_ge(S("brow_in"), 32 * it + 32)
                for n in range(4):
                    s = slice(64 * (n % 2), 64 * (n % 2) + 64)
                    ins = mm(ps[s, 4 + n // 2, :], cst[0:1, K_ONE:K_ONE + 64], brow[n // 2][:, 512 * (n % 2):512 * (n % 2 + 1)],
                             start=False, stop=True, skip_group_check=True)
                ins.then_inc(S("brow_used"), 1)
                pe.wait_ge(S("y_copied"), it + 1)
                scatter(1 - q)
                pe.wait_ge(S("h_ready"), it + 1)
                pe.wait_ge(S("pt_copied"), it + 1)
                for j in range(4):
                    ins = tr(ps[:, 7, P * j:P * (j + 1)], act_h[:, P * j:P * (j + 1)], ident)
                ins.then_inc(S("at_ready"), 1)
                pe.wait_ge(S("at_copied"), it + 2)
                for kk in range(KT):
                    b, half, sub = kk // 4, (kk // 2) % 2, kk % 2
                    if kk % 2 == 0:
                        pe.wait_ge(S(f"dn_in{kk // 2}"), 16 * it + 16)
                    for n in range(2):
                        ins = mm(ps[64 * n:64 * n + 64, 6, :], actT[:, 2 * b + sub, 64 * half:64 * half + 64],
                                 dn_slot(kk // 2)[:, kk % 2, 512 * n:512 * (n + 1)], start=kk == 0, stop=kk == KT - 1, skip_group_check=True)
                    if kk % 2:
                        ins.then_inc(S("dn_used"), 1)

            pe.wait_ge(S("passes_known"), 1)
            n = pe.value_load(passes[0:1, 0:1], min_val=1, max_val=T // slots)
            with pe.Fori(0, n) as b:
                with pe.Fori(0, NE // 2) as i:
                    expert(NE * b + 2 * i, 0)
                    expert(NE * b + 2 * i + 1, 1)
            pe.wait_ge(S("y_copied"), NE * n + 1)
            scatter(1, last=True).then_inc(S("sum_ready"), 1)

        @block.scalar
        def _(act):
            af = nc.scalar.activation

            act.sem_inc(S("at_copied"), 1)
            act.wait_ge(S("x_in"), 16)
            for c in range(NT):
                ins = af(R[9][:, D * c:D * (c + 1)], x[:, c, :], ACT.Square, accum_out=ss[:, c:c + 1])
            ins.then_inc(S("act_step"), 1)
            act.wait_ge(S("act_step"), 1)
            act.wait_ge(S("cst_in"), 16)
            af(rstd, ss, ACT.Sqrt, scale=1.0 / D, bias=col(0)).then_inc(S("ss_ready"), 1)

            act.wait_ge(S("mm_ready"), MM0 + 1)
            af(rows[0:8, 5, :], ps[0:8, 0, T:2 * T], ACT.Copy).then_inc(S("act_first"), 1)
            act.wait_ge(S("mm_ready"), MM0 + 2)
            act.wait_ge(S("par_ready"), 1)
            af(lora[:, 0, :], ps[:, 1, 0:T], ACT.Copy, scale=omm[:, 24:25])
            af(lora[:, 1, :], ps[:, 1, T:2 * T], ACT.Copy, scale=omm[:, 25:26]).then_inc(S("act_first"), 1)
            with act.Fori(0, 2) as i:
                for u in range(18):
                    j, half = u // 2, u % 2
                    b = (2 + u) % HB
                    act.wait_ge(S("mm_ready"), 18 * i + (MM0 + 3 + u))
                    if u < 6:
                        if u:
                            act.wait_ge(S("conv_done"), 6 * i + u)
                        for f in range(2):
                            ins = af(R[3][:, T * f:T * (f + 1)], ps[:, b, T * f:T * (f + 1)], ACT.Copy,
                                     scale=par[:, bass.ds(4 * i + (8 + 24 * 3 + 8 * j + 2 * half + f), 1)])
                        ins.then_inc(S("act_first"), 1)
                        act.wait_ge(S("dve_free"), 14 * i + (u + 3))
                        af(R[3][:, 512:1024], R[3][:, 0:512], ACT.Sigmoid).then_inc(S("act_sig"), 1)
                    elif u < 8:
                        if u == 6:
                            act.wait_ge(S("conv_done"), 6 * i + 6)
                        af(R[3][:, 1024 + 512 * half:1536 + 512 * half], ps[:, b, :], ACT.Sigmoid).then_inc(S("act_first"), 1)
                    elif u < 14:
                        for f in range(2):
                            t = 8 * (j - 4) + 2 * half + f
                            ins = af(R[4 + j][:, bass.ds(1024 * i + T * (2 * half + f), T)], ps[:, b, T * f:T * (f + 1)], ACT.Copy,
                                     scale=omm[:, bass.ds(4 * i + t, 1)])
                        ins.then_inc(S("act_first"), 1)
                    else:
                        af(R[6 + (j - 7)][:, bass.ds(1024 * i + 512 * half, 512)], ps[:, b, :], ACT.Sigmoid).then_inc(S("act_first"), 1)

            act.wait_ge(S("msk_read"), 1)
            act.wait_ge(S("conv_done"), 12)
            for u in range(8):
                af(scr[:, 512 * u:512 * (u + 1)].rearrange("p (h c t) -> p h c t", h=2, c=2), KQ[:, 2 * (u // 2):2 * (u // 2) + 2, :, u % 2, :],
                   ACT.Square).then_inc(S("gsq_ready"), 1)
            act.wait_ge(S("dve_free"), 30)
            act.wait_ge(S("act_first"), 38)
            af(rows[:, 1, :], rows[:, 4, :], ACT.Sigmoid).then_inc(S("gate_row"), 1)
            act.wait_ge(S("row_in"), 32)
            act.wait_ge(S("gate_row"), 2)
            af(negA, alog, ACT.Exp)
            af(rows[:, 3, :], rows[:, 3, :], ACT.Exp).then_inc(S("act_step"), 1)
            act.wait_ge(S("act_step"), 2)
            af(rows[:, 3, :], rows[:, 3, :], ACT.Ln, bias=cst[0:8, K_COL + 3:K_COL + 4]).then_inc(S("gate_row"), 1)
            act.wait_ge(S("gate_row"), 4)
            af(rows[:, 2, :], rows[:, 0, :], ACT.Exp)
            af(rows[:, 3, :], rows[:, 3, :], ACT.Exp).then_inc(S("gate_row"), 1)
            for u in range(8):
                act.wait_ge(S("gnm_ready"), u + 1)
                af(scr[:, 4096 + 512 * u:4608 + 512 * u], ps[:, u, :], ACT.Sqrt, scale=float(P) if u % 2 else 1.0, bias=col(u % 2)).then_inc(S("gnm_read"), 1)
            for w in range(4):
                act.wait_ge(S("vT_ready"), w + 1)
                af(R[3][:, 1024 * (w // 2) + 512 * (w % 2):1024 * (w // 2) + 512 * (w % 2) + 512], ps[:, w, :], ACT.Copy).then_inc(S("vT_read"), 1)
            DM, EG = TI2[:, 0:256], TI2[:, 768:896]
            for h in range(HEADS):
                act.wait_ge(S("gd_ready"), h + 1)
                af(DM, DM, ACT.Exp)
                af(EG, ps[:, 2 * (h % 2), P:2 * P], ACT.Exp).then_inc(S("ge_ready"), 1)

            def inverse(v):
                WS = R[9] if v else R[0]
                with act.Fori(0, LEVELS) as lv:
                    for g in range(4):
                        act.wait_ge(S("w_ready"), 4 * lv + (28 * v + g + 1))
                        af(WS[:, 512 * g:512 * (g + 1)], ps[:, g, :], ACT.Copy).then_inc(S("w_copied"), 1)

            inverse(0)
            U = scr[:, 8192:10240]
            two = lambda r: r.rearrange("p (b c) -> p b c", b=2)
            act.wait_ge(S("gu0_ready"), 1)
            af(two(U[:, 0:1024]), ps[:, 0:2, :], ACT.Copy).then_inc(S("gu0_copied"), 1)
            act.wait_ge(S("gs1_ready"), 1)
            af(two(R[4][:, 1024:2048]), ps[:, 4:6, :], ACT.Copy).then_inc(S("gs1_copied"), 1)
            act.wait_ge(S("gu1_ready"), 1)
            af(two(U[:, 1024:2048]), ps[:, 2:4, :], ACT.Copy).then_inc(S("gu1_copied"), 1)
            for q in range(4):
                act.wait_ge(S("got_ready"), q + 1)
                af(R[1][:, 512 * q:512 * (q + 1)], ps[:, (0, 1, 4, 5)[q], :], ACT.Square).then_inc(S("osq_ready"), 1)
            for q in range(4):
                act.wait_ge(S("onm_ready"), q + 1)
                af(R[1][:, 512 * q:512 * (q + 1)], ps[:, (2, 3, 6, 7)[q], :], ACT.Sqrt, scale=1.0 / P, bias=col(0)).then_inc(S("onm_read"), 1)

            af(lora[0:64, 0, :], lora[0:64, 0, :], ACT.Tanh)
            af(lora[:, 1, :], lora[:, 1, :], ACT.Sigmoid).then_inc(S("lora_act"), 1)
            for u in range(4):
                act.wait_ge(S("rz_ready"), u + 1)
                af(R[0][:, 512 * u:512 * (u + 1)], ps[:, (0, 1, 4, 5)[u], :], ACT.Sigmoid).then_inc(S("rz_read"), 1)
            for m in range(8):
                act.wait_ge(S("raa_ready"), m // 2 + 1)
                af(AA[:, T * m:T * (m + 1)], ps[:, (2, 3, 6, 7)[m // 2], T * (m % 2):T * (m % 2 + 1)], ACT.Sigmoid,
                   bias=par[:, P_A0 + m:P_A0 + m + 1]).then_inc(S("raa_read"), 1)
            act.wait_ge(S("rcc_ready"), 1)
            for m in range(8):
                for c in range(NT):
                    src = ps[:, (0, 1, 4, 5)[m // 2], P * (2 * (m % 2) + c):P * (2 * (m % 2) + c + 1)]
                    af(Ep[:, m, c, 1:P + 1], src, ACT.Exp, scale=-DECAY, bias=cc[:, 2 * m + c:2 * m + c + 1])
                    af(En[:, m, c, :], src, ACT.Exp, scale=DECAY, bias=ncc[:, 2 * m + c:2 * m + c + 1])
            af(Ep[:, :, :, 0], cc.rearrange("p (m c) -> p m c", m=8), ACT.Exp)
            af(dsc, dsc, ACT.Exp).then_inc(S("rexp_done"), 1)
            for q in range(4):
                act.wait_ge(S("rnm_ready"), q + 1)
                af(SQ[:, 512 * q:512 * (q + 1)], ps[:, (2, 3, 6, 7)[q], :], ACT.Sqrt, bias=col(0)).then_inc(S("rnm_read"), 1)
            for w in range(4):
                act.wait_ge(S("rv_ready"), w + 1)
                af(R[0][:, 1024 * (w // 2) + 512 * (w % 2):1024 * (w // 2) + 512 * (w % 2) + 512], ps[:, (0, 1, 4, 5)[w], :], ACT.Copy).then_inc(S("rv_read"), 1)
            for hf in range(2):
                inverse(1 + hf)
                for c in range(NT):
                    act.wait_ge(S("ry_ready"), 2 * hf + c + 1)
                    if c == 0:
                        af(R[9][:, 0:512], ps[:, 0, :], ACT.Copy).then_inc(S("ry_copied"), 1)
                    else:
                        pair = R[9][:, 0:512].rearrange("p (m w v) -> p m w v", m=4, w=2)
                        for w in range(2):
                            ins = af(pair[:, :, w, :], ps[:, 5 + 2 * w, 0:256].rearrange("p (m v) -> p m v", m=4), ACT.Copy)
                        ins.then_inc(S("ry_copied"), 1)
                    act.wait_ge(S("ru_ready"), 2 * hf + c + 1)
                    af(scr[:, 8192 + 512 * c:8704 + 512 * c], ps[:, (1, 6)[c], :], ACT.Copy, scale=-1.0).then_inc(S("ru_copied"), 1)
                act.wait_ge(S("rot_ready"), hf + 1)
                af(two(R[10][:, 1024 * hf:1024 * (hf + 1)]), ps[:, 2:4, :], ACT.Copy).then_inc(S("rot_read"), 1)
            for q in range(4):
                act.wait_ge(S("rmu_read"), q + 1)
                af(R[0][:, 512 * q:512 * (q + 1)], R[10][:, 512 * q:512 * (q + 1)], ACT.Square).then_inc(S("rvs_ready"), 1)
            for q in range(4):
                act.wait_ge(S("rvr_ready"), q + 1)
                af(R[0][:, 512 * q:512 * (q + 1)], ps[:, q, :], ACT.Sqrt, scale=1.0 / 64, bias=col(2)).then_inc(S("rvr_read"), 1)

            act.wait_ge(S("x1_ready"), 4)
            for c in range(NT):
                ins = af(R[1][:, D * c:D * (c + 1)], x[:, c, :], ACT.Square, accum_out=small[:, 128 + c:129 + c])
            ins.then_inc(S("act_step"), 1)
            act.wait_ge(S("act_step"), 3)
            af(small[:, 130:132], small[:, 128:130], ACT.Sqrt, scale=1.0 / D, bias=col(0)).then_inc(S("ms2_ready"), 1)
            act.wait_ge(S("top_ready"), 1)
            for c in range(NT):
                ins = af(tmp32[:, c, :], lg[:, c, :], ACT.Exp, bias=nmx[:, c:c + 1])
            ins.then_inc(S("lgexp_ready"), 1)

            def expert(it):
                act.wait_ge(S("glu_ready"), it + 1)
                af(sgm, glu, ACT.Sigmoid, scale=GLU_ALPHA).then_inc(S("sig_ready"), 1)
                act.wait_ge(S("at_ready"), it + 1)
                af(actT.rearrange("p c s -> p (c s)"), ps[:, 7, :], ACT.Copy).then_inc(S("at_copied"), 1)

            act.wait_ge(S("passes_known"), 1)
            n = act.value_load(passes[0:1, 0:1], min_val=1, max_val=T // slots)
            with act.Fori(0, n) as b:
                with act.Fori(0, NE) as e:
                    expert(NE * b + e)
            act.wait_ge(S("x2_ready"), 1)
            for c in range(NT):
                ins = af(R[0][:, D * c:D * (c + 1)], x[:, c, :], ACT.Square, accum_out=small[:, 132 + c:133 + c])
            ins.then_inc(S("act_step"), 1)
            act.wait_ge(S("act_step"), 4)
            af(small[:, 134:136], small[:, 132:134], ACT.Sqrt, scale=1.0 / D, bias=col(0)).then_inc(S("ms3_ready"), 1)

        @block.vector
        def _(dve):
            V = nc.vector
            steps = [0]

            def then(ins):
                steps[0] += 1
                ins.then_inc(S("dve_step"), 1)
                dve.wait_ge(S("dve_step"), steps[0])

            def bc(ap, n, axis=2, shape=None):
                return ap.unsqueeze(axis).broadcast_to(shape)

            dve.wait_ge(S("ss_ready"), 1)
            then(V.reciprocal(rstd, rstd))
            for c in range(NT):
                V.tensor_scalar(R[10][:, D * c:D * (c + 1)], x[:, c, :], rstd[:, c:c + 1], None, ALU.mult).then_inc(S("xs_ready"), 1)
            dve.wait_ge(S("par_T"), 1)
            V.tensor_copy(par[:, 0:ROWS_A], ps[:, 6, 0:ROWS_A])
            then(V.tensor_copy(par[:, P:P + ROWS_B], ps[:, 6, P:P + ROWS_B]))
            V.tensor_scalar(omka[:, :], par[:, P_KA:P_KA + 8], -1.0, 1.0, ALU.mult, ALU.add)
            V.tensor_scalar(omm[:, :], par[:, P_MU:P_MU + 26], -1.0, 1.0, ALU.mult, ALU.add).then_inc(S("par_ready"), 1)
            dve.wait_ge(S("xT_ready"), 1)
            for k in range(KT):
                ins = V.tensor_scalar(hT[:, k, :], ps[:, k // 2, T * (k % 2):T * (k % 2 + 1)], par[:, k:k + 1], None, ALU.mult)
            ins.then_inc(S("hT_ready"), 1)

            dve.wait_ge(S("msk_in"), 16)
            V.tensor_copy(msk[:, :], scr[:, 0:LEVELS * 2 * P]).then_inc(S("msk_read"), 1)
            dve.wait_ge(S("act_first"), 1)
            V.tensor_copy(rows[0:8, 4, :], ps[0:8, 0, 0:T]).then_inc(S("dve_free"), 1)
            dve.wait_ge(S("act_first"), 2)
            for f in range(2):
                ins = V.scalar_tensor_tensor(out=lora[:, f, 1:T], in0=ps[:, 1, T * f:T * f + T - 1], scalar=par[:, P_MU + 24 + f:P_MU + 25 + f],
                                             in1=lora[:, f, 1:T], op0=ALU.mult, op1=ALU.add)
            ins.then_inc(S("dve_free"), 1)
            with dve.Fori(0, 2) as i:
                for u in range(14):
                    j, half = u // 2, u % 2
                    b = (2 + u) % HB
                    dve.wait_ge(S("act_first"), 18 * i + (u + 3))
                    if u < 6:
                        for w in (2, 1, 0):
                            s = 3 - w
                            for f in range(2):
                                ins = V.scalar_tensor_tensor(out=R[3][:, T * f + s:T * (f + 1)], in0=ps[:, b, T * f:T * (f + 1) - s],
                                                             scalar=par[:, bass.ds(4 * i + (8 + 24 * w + 8 * j + 2 * half + f), 1)],
                                                             in1=R[3][:, T * f + s:T * (f + 1)], op0=ALU.mult, op1=ALU.add)
                            if w:
                                ins.then_inc(S("conv_step"), 1)
                                dve.wait_ge(S("conv_step"), 12 * i + (2 * u + 3 - w))
                        ins.then_inc(S("dve_free"), 1)
                        dve.wait_ge(S("act_sig"), 6 * i + (u + 1))
                        a, g = (R[3][:, 512 * n:512 * (n + 1)].rearrange("p (h c t) -> p h c t", h=2, c=2) for n in range(2))
                        if j < 2:
                            out = KQ[:, bass.ds(4 * i + 2 * half, 2), :, 1 - j, :]
                        else:
                            out = R[4][:, bass.ds(1024 * i + 512 * half, 512)].rearrange("p (h c t) -> p h c t", h=2, c=2)
                        V.tensor_tensor(out, a, g, ALU.mult).then_inc(S("conv_done"), 1)
                    elif u < 8:
                        V.tensor_tensor(R[5][:, bass.ds(1024 * i + 512 * half, 512)], ps[:, b, :], R[3][:, 1024 + 512 * half:1536 + 512 * half],
                                        ALU.mult).then_inc(S("dve_free"), 1)
                    else:
                        for f in range(2):
                            out = R[4 + j][:, bass.ds(1024 * i + T * (2 * half + f) + 1, T - 1)]
                            ins = V.scalar_tensor_tensor(out=out, in0=ps[:, b, T * f:T * (f + 1) - 1],
                                                         scalar=par[:, bass.ds(4 * i + (P_MU + 8 * (j - 4) + 2 * half + f), 1)],
                                                         in1=out, op0=ALU.mult, op1=ALU.add)
                        ins.then_inc(S("dve_free"), 1)

            dve.wait_ge(S("gate_row"), 1)
            dve.wait_ge(S("row_in"), 32)
            then(V.tensor_scalar(rows[:, 2, :], rows[:, 5, :], dtb, None, ALU.add))
            V.scalar_tensor_tensor(out=rows[:, 3, :], in0=rows[:, 2, :], scalar=-1.0, in1=rows[:, 2, :], op0=ALU.mult, op1=ALU.min).then_inc(S("gate_row"), 1)
            dve.wait_ge(S("gate_row"), 3)
            then(V.scalar_tensor_tensor(out=rows[:, 3, :], in0=rows[:, 2, :], scalar=0.0, in1=rows[:, 3, :], op0=ALU.max, op1=ALU.add))
            then(V.tensor_scalar(rows[:, 2, :], rows[:, 3, :], negA, -1.0, ALU.mult, ALU.mult))
            for c in range(NT):
                s = slice(P * c, P * (c + 1))
                ins = V.tensor_tensor_scan(rows[:, 0, s], cst[0:8, K_ONE:K_ONE + P], rows[:, 2, s], 0.0, ALU.mult, ALU.add)
            then(ins)
            for c in range(NT):
                s = slice(P * c, P * (c + 1))
                ins = V.tensor_scalar(rows[:, 3, s], rows[:, 0, s], -1.0, rows[:, 0, P * (c + 1) - 1:P * (c + 1)], ALU.mult, ALU.add)
            ins.then_inc(S("gate_row"), 1)
            for u in range(8):
                dve.wait_ge(S("gnm_read"), u + 1)
                r = scr[:, 4096 + 512 * u:4608 + 512 * u]
                then(V.reciprocal(r, r))
                v = KQ[:, 2 * (u // 2):2 * (u // 2) + 2, :, u % 2, :]
                V.tensor_tensor(v, v, r.rearrange("p (h c t) -> p h c t", h=2, c=2), ALU.mult).then_inc(S("kq_ready"), 1)
            dve.wait_ge(S("tb_ready"), 1)
            then(V.tensor_copy(small[:, 64:128], ps[:, 6, 0:64]))
            DM, DI, DS, EG = TI2[:, 0:256], TI2[:, 256:512], TI2[:, 512:768], TI2[:, 768:896]
            ct = lambda r: r.rearrange("p (c t) -> p c t", c=2)
            both = lambda m: m.unsqueeze(1).broadcast_to([P, 2, P])
            dve.wait_ge(S("vT_ready"), 4)
            for h in range(HEADS):
                b = 2 * (h % 2)
                dve.wait_ge(S("head_ready"), h + 1)
                for c in range(NT):
                    ins = V.tensor_scalar(DM[:, P * c:P * (c + 1)], ps[:, b, P * c:P * (c + 1)], tb[:, 0, c, h:h + 1], 0.0, ALU.subtract, ALU.min)
                ins.then_inc(S("gd_ready"), 1)
                dve.wait_ge(S("ge_ready"), h + 1)
                V.tensor_tensor(QDt[:, P * h:P * (h + 1)], KQ[:, h, 1, 1, :], EG, ALU.mult)
                V.tensor_tensor(ct(DS), ct(DM), both(C(K_M4)), ALU.mult)
                then(V.tensor_tensor(ct(DI), ct(DM), both(incl), ALU.mult))
                prod = ps[:, b + 1, :].rearrange("p (c w t) -> p c w t", c=2, w=2)
                V.tensor_tensor(MM[:, 2 * h:2 * h + 2, 1, :], prod[:, :, 1, :], ct(DI), ALU.mult)
                then(V.tensor_tensor(DS, ps[:, b, T:2 * T], DS, ALU.mult))
                V.tensor_tensor(MM[:, 2 * h:2 * h + 2, 0, :], prod[:, :, 0, :], ct(DS), ALU.mult).then_inc(S("head_done"), 1)

            def inverse(v):
                with dve.Fori(0, LEVELS) as lv:
                    dve.wait_ge(S("t_done"), 4 * lv + (32 * v + 4))
                    V.tensor_copy(lvl[:, :, :].rearrange("p w t -> p (w t)"), msk[:, bass.ds(2 * P * lv, 2 * P)]).then_inc(S("lvl_ready"), 1)
                    dve.wait_ge(S("lvl_ready"), lv + (LEVELS * v + 1))
                    for g in range(4):
                        dve.wait_ge(S("t_ready"), 4 * lv + (28 * v + g + 1))
                        dve.sem_inc(S("t_seen"), 1)
                        for w, t in enumerate((TI, TT)):
                            ins = V.copy_predicated(t[:, 4 * g:4 * g + 4, :], lvl[:, w, :].unsqueeze(1).broadcast_to([P, 4, P]),
                                                    ps[:, 4 + 2 * (g % 2) + w, :].rearrange("p (u t) -> p u t", u=4))
                        ins.then_inc(S("t_done"), 1)

            inverse(0)
            hd = lambda r, k=8: r.rearrange("p (h t) -> p h t", h=k)
            tbc = lambda w, c: tb[:, w, c, :].unsqueeze(2).broadcast_to([P, 8, P])
            two = lambda a: ps[:, a:a + 2, :].rearrange("p b (h t) -> p (b h) t", h=4)
            dve.wait_ge(S("t_done"), 32)
            dve.wait_ge(S("vT_read"), 4)
            V.tensor_tensor(hd(R[0][:, 0:1024]), hd(R[3][:, 0:1024]), tbc(1, 0), ALU.mult).then_inc(S("gx_ready"), 1)
            dve.wait_ge(S("gkd_ready"), 1)
            V.tensor_tensor(hd(R[0][:, 1024:2048]), two(2), tbc(3, 0), ALU.mult).then_inc(S("gkd_copied"), 1)
            dve.wait_ge(S("gks_ready"), 1)
            X = R[0][:, 0:1024]
            then(V.tensor_tensor(hd(X), two(6), tbc(2, 1), ALU.mult))
            then(V.tensor_tensor(X, R[3][:, 1024:2048], X, ALU.subtract))
            V.tensor_tensor(hd(X), hd(X), tbc(1, 1), ALU.mult).then_inc(S("gx_ready"), 1)
            for q in range(4):
                dve.wait_ge(S("osq_ready"), q + 1)
                V.tensor_copy(R[2][:, 512 * q:512 * (q + 1)], ps[:, (0, 1, 4, 5)[q], :]).then_inc(S("got_read"), 1)
            dve.wait_ge(S("got_read"), 4)
            dve.wait_ge(S("onm_read"), 4)
            then(V.reciprocal(R[1], R[1]))
            then(V.scalar_tensor_tensor(out=R[2], in0=R[2], scalar=par[:, P_GN:P_GN + 1], in1=R[1], op0=ALU.mult, op1=ALU.mult))
            V.tensor_tensor(R[5], R[2], R[5], ALU.mult).then_inc(S("ya_ready"), 1)

            ccv = cc.rearrange("p (m c) -> p m c", m=8)
            dsv = small[:, 48:56]
            for q in range(4):
                dve.wait_ge(S("rg_ready"), q + 1)
                ins = V.tensor_scalar(cc[:, 4 * q:4 * q + 4], ps[:, (0, 1, 4, 5)[q], P // 2 - 1::P], DECAY, None, ALU.mult)
            then(ins)
            for q in range(4):
                ins = V.scalar_tensor_tensor(out=dsv[:, 2 * q:2 * q + 2], in0=ps[:, (0, 1, 4, 5)[q], P - 1::2 * P], scalar=-DECAY,
                                             in1=ccv[:, 2 * q:2 * q + 2, 0], op0=ALU.mult, op1=ALU.add)
            then(ins)
            V.tensor_scalar(ncc, cc, -1.0, None, ALU.mult)
            V.tensor_tensor(dsc, dsv, ccv[:, :, 1], ALU.subtract).then_inc(S("rcc_ready"), 1)
            m4 = lambda r: r.rearrange("p (m c t) -> p m c t", m=8, c=2)
            dve.wait_ge(S("rsq_ready"), 1)
            dve.wait_ge(S("rnm_read"), 4)
            then(V.reciprocal(SQ, SQ))
            then(V.tensor_tensor(T1, T1, SQ, ALU.mult))
            dve.wait_ge(S("rexp_done"), 1)
            dve.wait_ge(S("ya_ready"), 1)
            then(V.tensor_tensor(AR[:, :, :, 0, :], m4(T1), Ep[:, :, :, 0:P], ALU.mult))
            V.tensor_tensor(T1, T1, AA, ALU.mult).then_inc(S("rbe_done"), 1)
            dve.wait_ge(S("rbe_done"), 1)
            V.tensor_tensor(BK[:, :, :, 0, :], m4(T1), En, ALU.mult)
            V.tensor_tensor(AR[:, :, :, 1, :], m4(R[8]), Ep[:, :, :, 1:P + 1], ALU.mult).then_inc(S("rrho_done"), 1)
            for q in range(4):
                dve.wait_ge(S("rbn_ready"), q + 1)
                ins = V.tensor_tensor(R[8][:, 512 * q:512 * (q + 1)], ps[:, (2, 3, 6, 7)[q], :], R[10][:, 512 * q:512 * (q + 1)], ALU.mult)
            ins.then_inc(S("prep_done"), 1)
            for hf in range(2):
                for u in range(16):
                    dve.wait_ge(S("rm_ready"), 16 * hf + u + 1)
                    V.tensor_tensor(MM[:, u, :, :].rearrange("p w t -> p (w t)"), ps[:, u % 4, :], C(K_M4, 4 * P), ALU.mult).then_inc(S("rm_read"), 1)
                inverse(1 + hf)
                dve.wait_ge(S("rkb_ready"), hf + 1)
                V.tensor_copy(R[9][:, 1024:2048].rearrange("p (b c) -> p b c", b=2), ps[:, 2:4, :]).then_inc(S("rkb_copied"), 1)
                dve.wait_ge(S("rs_ready"), hf + 1)
                V.tensor_tensor(R[9][:, 512:768].rearrange("p (m v) -> p m v", m=4), ps[:, 4, 0:256].rearrange("p (m v) -> p m v", m=4),
                                dsc[:, 4 * hf:4 * hf + 4].unsqueeze(2).broadcast_to([P, 4, 64]), ALU.mult).then_inc(S("rs_copied"), 1)
            dve.wait_ge(S("rot_read"), 2)
            for q in range(4):
                o = R[10][:, 512 * q:512 * (q + 1)]
                dve.wait_ge(S("rmu_ready"), q + 1)
                V.scalar_tensor_tensor(out=o, in0=ps[:, 4 + q, :], scalar=-1.0 / 64, in1=o, op0=ALU.mult, op1=ALU.add).then_inc(S("rmu_read"), 1)
            dve.wait_ge(S("rmu_read"), 4)
            dve.wait_ge(S("rvr_read"), 4)
            o8 = W3[10]
            then(V.reciprocal(R[0], R[0]))
            then(V.tensor_tensor(R[10], R[10], R[0], ALU.mult))
            then(V.tensor_tensor(o8, o8, cols8(P_LNW), ALU.mult))
            then(V.tensor_tensor(o8, o8, cols8(P_LNB), ALU.add))
            then(V.tensor_tensor(R[10], R[10], R[8], ALU.add))
            for q in range(4):
                dve.wait_ge(S("gg_ready"), q + 1)
                ins = V.tensor_tensor(R[10][:, 512 * q:512 * (q + 1)], ps[:, 4 + q, :], R[10][:, 512 * q:512 * (q + 1)], ALU.mult)
            ins.then_inc(S("yb_ready"), 1)

            for u in range(8):
                g = R[6 + u // 4][:, 512 * (u % 4):512 * (u % 4 + 1)]
                dve.wait_ge(S("pj_ready"), u + 1)
                then(V.tensor_tensor(g, ps[:, u, :], g, ALU.mult))
            V.tensor_tensor(R[6], R[6], R[7], ALU.add).then_inc(S("merged"), 1)
            for n in range(2):
                for c in range(NT):
                    dve.wait_ge(S("pj_ready"), 9 + 2 * n + c)
                    o = x[:, c, 512 * n:512 * (n + 1)]
                    V.tensor_tensor(o, ps[:, 2 * n + c, :], o, ALU.add).then_inc(S("x1_ready"), 1)

            dve.wait_ge(S("ms2_ready"), 1)
            then(V.reciprocal(small[:, 130:132], small[:, 130:132]))
            for c in range(NT):
                ins = V.tensor_scalar(H2[:, c, :], x[:, c, :], small[:, 130 + c:131 + c], None, ALU.mult)
            ins.then_inc(S("h2_ready"), 1)
            dve.wait_ge(S("h2T_ready"), 1)
            for k in range(KT):
                ins = V.tensor_scalar(h2T[:, k, :], ps[:, 4 + k // 2, T * (k % 2):T * (k % 2 + 1)], par[:, P_NF + k:P_NF + k + 1], None, ALU.mult)
            ins.then_inc(S("h2T_copied"), 1)
            dve.wait_ge(S("lg_ready"), 1)
            then(V.tensor_copy(lg.rearrange("p c e -> p (c e)"), ps[:, 0, 0:2 * NE]))
            for c in range(NT):
                ins = V.max(top[:, c, :], lg[:, c, :])
            then(ins)
            V.tensor_scalar(nmx, top[:, :, 0], -1.0, None, ALU.mult).then_inc(S("top_ready"), 1)
            for c in range(NT):
                ins = V.max_index(topi[:, c, :].bitcast(U32), top[:, c, :], lg[:, c, :])
            then(ins)
            then(V.tensor_copy(topf, topi.bitcast(U32)))
            i32 = cst[:, K_IOTA:K_IOTA + NE]
            for q in range(4):
                for c in range(NT):
                    if q == 0:
                        ins = V.tensor_scalar(sel[:, c, :], i32, topf[:, c, 0:1], None, ALU.is_equal)
                    else:
                        ins = V.scalar_tensor_tensor(out=sel[:, c, :], in0=i32, scalar=topf[:, c, q:q + 1], in1=sel[:, c, :], op0=ALU.is_equal, op1=ALU.add)
                then(ins)
            dve.wait_ge(S("lgexp_ready"), 1)
            then(V.tensor_tensor(gt, tmp32, sel, ALU.mult))
            then(V.tensor_reduce(gsum, gt, AX.X, ALU.add))
            then(V.reciprocal(grec, gsum))
            V.tensor_tensor(gt, gt, grec.unsqueeze(2).broadcast_to([P, 2, NE]), ALU.mult).then_inc(S("sel_ready"), 1)
            dve.wait_ge(S("sel_ready"), 1)
            dve.wait_ge(S("pos_ready"), 1)
            tpos, tgat = (tab[:, 0:NE, 2 * w:2 * w + 2].rearrange("p e c -> p c e") for w in range(2))
            V.tensor_copy(gT, ps[0:NE, 2, 0:T])
            V.tensor_copy(tgat, gt)
            V.tensor_copy(cnt, ps[0:1, 1, 2 * NE:3 * NE])
            then(V.scalar_tensor_tensor(out=tmp32, in0=ps[:, 1, 0:2 * NE].rearrange("p (c e) -> p c e", c=2), scalar=1.0, in1=sel, op0=ALU.add, op1=ALU.mult))
            V.tensor_scalar(tpos, tmp32, -1.0, None, ALU.add)
            then(V.tensor_reduce(cmax, cnt, AX.X, ALU.max))
            V.tensor_copy(tab[:, NE, :], tab[:, 0, :]).then_inc(S("pos_read"), 1)
            then(V.tensor_scalar(cge, cst[0:1, K_COL + 8:K_COL + 16], cmax, None, ALU.is_lt))
            V.tensor_scalar(tab[:, NE, 0:2], tab[:, NE, 0:2], -float(slots), None, ALU.add)
            then(V.tensor_reduce(csum, cge, AX.X, ALU.add))
            V.tensor_copy(passes[:, :], csum).then_inc(S("passes_known"), 1)
            iot = C(K_IOTA)

            def choose(q):
                for c in range(NT):
                    V.tensor_scalar(Psel[:, q, c, 0:64], iot[:, 0:64], cur[:, q, c:c + 1], None, ALU.is_equal)
                    ins = V.tensor_scalar(Pgat[:, q, c, :], iot, cur[:, q, c:c + 1], cur[:, q, 2 + c:3 + c], ALU.is_equal, ALU.mult)
                ins.then_inc(S("sel_made"), 1)

            V.memset(PgT[:, 1, :, :].rearrange("p c t -> p (c t)"), 0.0)
            V.memset(ysb[:, 1, :], 0.0).then_inc(S("y_copied"), 1)
            then(V.tensor_copy(cur[:, 0, :], tab[:, 0, :]))
            choose(0)
            nfeat = par[:, P_NF:P_NF + 8].unsqueeze(2).broadcast_to([P, 8, 64])
            fl = lambda w: ps[:, 4:6, :].rearrange("p b (f w) -> p b f w", w=2)[:, :, :, w]
            v2 = lambda r: r.rearrange("p (b f) -> p b f", b=2)

            def expert(it, e, q):
                dve.wait_ge(S("xg_ready"), it + 1)
                V.tensor_tensor(xgT[:, q, :, :], ps[:, 7, :].rearrange("p (k s) -> p k s", k=KT), nfeat, ALU.mult).then_inc(S("xg_copied"), 1)
                V.tensor_copy(cur[:, 1 - q, :], tab[:, bass.ds(e + 1, 1), :].rearrange("p e w -> p (e w)")).then_inc(S("moe_step"), 1)
                dve.wait_ge(S("pt_ready"), it + 1)
                V.tensor_copy(PgT[:, q, :, :].rearrange("p c t -> p (c t)"), ps[:, 7, 0:T]).then_inc(S("pt_copied"), 1)
                dve.wait_ge(S("moe_step"), 3 * it + 1)
                choose(1 - q)
                dve.wait_ge(S("brow_used"), it + 2)
                V.tensor_scalar(v2(glu), fl(0), GLU_LIMIT, None, ALU.min).then_inc(S("glu_ready"), 1)
                V.tensor_scalar(v2(lin), fl(1), GLU_LIMIT, -GLU_LIMIT, ALU.min, ALU.max).then_inc(S("moe_step"), 1)
                dve.wait_ge(S("moe_step"), 3 * it + 2)
                V.scalar_tensor_tensor(out=lin, in0=lin, scalar=1.0, in1=glu, op0=ALU.add, op1=ALU.mult).then_inc(S("moe_step"), 1)
                dve.wait_ge(S("moe_step"), 3 * it + 3)
                dve.wait_ge(S("sig_ready"), it + 1)
                V.tensor_tensor(act_h, lin, sgm, ALU.mult).then_inc(S("h_ready"), 1)
                dve.wait_ge(S("dn_used"), 4 * it + 8)
                V.tensor_copy(ysb[:, q, :], ps[:, 6, :]).then_inc(S("y_copied"), 1)

            dve.wait_ge(S("passes_known"), 1)
            n = dve.value_load(passes[0:1, 0:1], min_val=1, max_val=T // slots)
            with dve.Fori(0, n) as b:
                with dve.Fori(0, NE // 2) as i:
                    expert(NE * b + 2 * i, 2 * i, 0)
                    expert(NE * b + 2 * i + 1, 2 * i + 1, 1)
                V.tensor_scalar(tab[:, :, 0:2], tab[:, :, 0:2], -float(slots), None, ALU.add).then_inc(S("pass_done"), 1)
                dve.wait_ge(S("pass_done"), b + 1)

            dve.wait_ge(S("sum_ready"), 1)
            V.tensor_tensor(x[:, :, :].rearrange("p c d -> p (c d)"), ps[:, 0:4, :].rearrange("p b c -> p (b c)"),
                            x[:, :, :].rearrange("p c d -> p (c d)"), ALU.add).then_inc(S("x2_ready"), 1)
            dve.wait_ge(S("ms3_ready"), 1)
            dve.wait_ge(S("nf_in"), 16)
            then(V.reciprocal(small[:, 134:136], small[:, 134:136]))
            for c in range(NT):
                ins = V.scalar_tensor_tensor(out=R[1][:, D * c:D * (c + 1)], in0=x[:, c, :], scalar=small[:, 134 + c:135 + c], in1=nfb,
                                             op0=ALU.mult, op1=ALU.mult)
            ins.then_inc(S("y_ready"), 1)

        @block.gpsimd
        def _(pool):
            G = nc.gpsimd
            for v in range(3):
                if v == 0:
                    pool.wait_ge(S("head_done"), 8)
                elif v == 1:
                    pool.wait_ge(S("got_ready"), 4)
                    G.tensor_tensor(T1.rearrange("p (m t) -> p m t", m=8), W3[9], cols8(P_KK), ALU.mult).then_inc(S("pool_step"), 1)
                    pool.wait_ge(S("pool_step"), 1)
                    G.tensor_tensor(SQ, T1, T1, ALU.mult).then_inc(S("rsq_ready"), 1)
                    pool.wait_ge(S("rbe_done"), 1)
                    A8 = AA.rearrange("p (m t) -> p m t", m=8)
                    m4 = lambda r: r.rearrange("p (m c t) -> p m c t", m=8, c=2)
                    for n, ins in enumerate((lambda: G.tensor_tensor(A8, A8, cols8(P_KA), ALU.mult),
                                             lambda: G.tensor_tensor(A8, A8, omka[:, :].unsqueeze(2).broadcast_to([P, 8, T]), ALU.add),
                                             lambda: G.tensor_tensor(R[9], R[9], AA, ALU.mult))):
                        ins().then_inc(S("pool_step"), 1)
                        pool.wait_ge(S("pool_step"), n + 2)
                    G.tensor_tensor(BK[:, :, :, 1, :], m4(R[9]), En, ALU.mult)
                    pool.wait_ge(S("rrho_done"), 1)
                    G.tensor_tensor(R[8], R[8], R[9], ALU.mult).then_inc(S("pool_step"), 1)
                    pool.wait_ge(S("pool_step"), 5)
                    G.tensor_tensor(W3[8], W3[8], cols8(P_RK), ALU.mult).then_inc(S("rrk_ready"), 1)
                    pool.wait_ge(S("prep_done"), 1)
                else:
                    pool.wait_ge(S("rot_ready"), 1)
                eye = ident.unsqueeze(1).broadcast_to([P, 16, P])
                G.tensor_copy(TI, eye)
                G.tensor_copy(TT, eye).then_inc(S("t_done"), 4)


_NAMES = ["x", "norm_mix", "w_in", "gdn_conv", "gdn_A_log", "gdn_dt_bias", "gdn_norm", "rwkv_mu", "rwkv_w0", "rwkv_w2", "rwkv_a0",
          "rwkv_a2", "rwkv_g2", "rwkv_k_k", "rwkv_k_a", "rwkv_r_k", "rwkv_ln_w", "rwkv_ln_b", "proj_a", "proj_b", "w_out", "norm_ffn",
          "router_w", "router_b", "w_gate_up", "b_gate_up", "w_down", "b_down", "norm_final"]


def kernel(**inputs):
    import numpy as _np
    import concourse.bacc as _bacc
    from concourse import mybir as _mybir
    from concourse.bass_utils import run_bass_kernel_spmd as _run

    nc = _bacc.Bacc("TRN2", target_bir_lowering=False, num_devices=1)
    consts, masks = shape_constants()
    arrays, aps = {}, {}
    for name in _NAMES:
        arrays[f"in_{name}"] = _np.ascontiguousarray(inputs[name])
    arrays["in_consts"], arrays["in_masks"] = consts, masks
    for full, a in arrays.items():
        aps[full[3:]] = nc.dram_tensor(full, a.shape, _mybir.dt.from_np(a.dtype), kind="ExternalInput").ap()
    aps["out"] = nc.dram_tensor("out_0", (1, T, D), F32, kind="ExternalOutput").ap()
    hybrid_block(nc, aps)
    r = _run(nc, [arrays], core_ids=[0])
    return r.results[0]["out_0"]
```

```python
from contextlib import ExitStack
from math import exp

import numpy as np
import concourse.bass as bass
from concourse import mybir

F32 = mybir.dt.float32
I32 = mybir.dt.int32
U32 = mybir.dt.uint32
U8 = mybir.dt.uint8
ALU = mybir.AluOpType
ACT = mybir.ActivationFunctionType
AX = mybir.AxisListType

P = 128
T = 256
NT = T // P
D = 1024
KT = D // P
HEADS = 8
NE = 32
SLOTS = 64
PANEL = 512
EPS = 1e-6
GN_EPS = 64e-5
DECAY = exp(-0.5)
GLU_ALPHA, GLU_LIMIT = 1.702, 7.0

C_Q, C_K, C_V, C_Z, C_B, C_A = 0, 1024, 2048, 3072, 4096, 4104
C_R, C_RK, C_RV, C_LORA, C_GA, C_GB = 4112, 5136, 6160, 7184, 7440, 8464

K_ID, K_ONE, K_BLK, K_INC, K_STR, K_M4, K_SEL, K_IOTA, K_COL = 0, 128, 256, 384, 512, 640, 1152, 2176, 2304
K_N = 2320
LEVELS = 7

ROWS_A = 8 + 4 * 24
PB = 128
(P_MU, P_A0, P_KK, P_KA, P_RK, P_LNW, P_LNB, P_NF, P_GN) = (PB + r for r in (0, 26, 34, 42, 50, 58, 66, 74, 82))
ROWS_B = 83


def shape_constants(slots=SLOTS):
    t = np.arange(P)
    c = np.zeros((P, K_N), np.float32)
    c[:, K_ID:K_ID + P] = np.eye(P)
    c[:, K_ONE:K_ONE + P] = 1
    c[:, K_BLK:K_BLK + P] = (t[:, None] // 64) == (t[None] // 64)
    incl = (t[:, None] <= t[None]).astype(np.float32)
    strict = (t[:, None] < t[None]).astype(np.float32)
    c[:, K_INC:K_INC + P] = incl
    c[:, K_STR:K_STR + P] = strict
    c[:, K_M4:K_M4 + 4 * P] = np.concatenate([-strict, incl, strict, incl], 1)
    for h in range(HEADS):
        c[h, K_SEL + h * P:K_SEL + (h + 1) * P] = 1
    j = np.arange(P) % 64
    c[:, K_IOTA:K_IOTA + P] = np.where(j < slots, j, -1000)
    c[:, K_COL:K_COL + 8] = [EPS, P * EPS, GN_EPS, 1.0, 0, 0, 0, 0]
    c[:, K_COL + 8:K_COL + 16] = [b * slots if b * slots < T else 1e9 for b in range(8)]
    m = np.zeros((P, LEVELS - 1, 2, P), np.float32)
    for lv in range(LEVELS - 1):
        b = 1 << lv
        low = ((t[:, None] // (2 * b)) == (t[None] // (2 * b))) & ((t[:, None] // b) % 2 == 1) & ((t[None] // b) % 2 == 0)
        m[:, lv, 0], m[:, lv, 1] = low, low.T
    return c, m.reshape(P, -1)


def hybrid_block(nc, A, slots=SLOTS):
    ctx = ExitStack()
    with ctx:
        def sb(name, shape, dt=F32):
            return ctx.enter_context(nc.sbuf_tensor(name, shape, dt))

        sems = {}

        def S(name):
            if name not in sems:
                sems[name] = ctx.enter_context(nc.semaphore(name))
            return sems[name]

        cst = sb("cst", [P, K_N])
        msk = sb("msk", [P, (LEVELS - 1) * 2 * P], U8)
        lvl = sb("lvl", [P, 2 * P], U8)
        par = sb("par", [P, 2 * P])
        omm = sb("omm", [P, 26])
        omka = sb("omka", [P, 8])
        small = sb("small", [P, 256])
        lora = sb("lora", [P, 2, T])
        x = sb("x", [P, NT, D])
        ring = sb("ring", [P, 6 * 2048])
        scr = sb("scr", [P, 6 * 2048])
        arena = sb("arena", [P, 11 * 2048])
        passes = sb("passes", [1, 1], I32)
        ps = ctx.enter_context(nc.psum_tensor("ps", [P, 8, 512], F32))

        rows = scr[0:8, 10240:10240 + 6 * T].rearrange("p (w t) -> p w t", w=6)
        R = [arena[:, 2048 * r:2048 * (r + 1)] for r in range(11)]
        W3 = [r.rearrange("p (m t) -> p m t", m=8) for r in R]
        W4 = [r.rearrange("p (c m t) -> p c m t", c=2, m=8) for r in R]

        def C(k, n=P, rows_=P):
            return cst[0:rows_, k:k + n]

        ident, ones, blk = C(K_ID), C(K_ONE), C(K_BLK)
        incl, strict = C(K_INC), C(K_STR)

        def col(j):
            return cst[:, K_COL + j:K_COL + j + 1]

        def cols8(j, n=T, k=8):
            return par[:, j:j + k].unsqueeze(2).broadcast_to([P, k, n])

        panel = [ring[:, s * 4096:(s + 1) * 4096].rearrange("p (k c) -> p k c", k=KT) for s in range(3)]
        hT = W3[0]
        KQ = arena[:, 2048:6144].rearrange("p (h c w t) -> p h c w t", h=8, c=2, w=2)
        AR = arena[:, 2048:6144].rearrange("p (m c w t) -> p m c w t", m=8, c=2, w=2)
        BK = arena[:, 6144:10240].rearrange("p (m c w t) -> p m c w t", m=8, c=2, w=2)
        MM = scr[:, 0:8192].rearrange("p (u w t) -> p u w t", u=16, w=4)
        TI = scr[:, 8192:10240].rearrange("p (u t) -> p u t", u=16)
        TI2 = scr[:, 8192:9216]
        QDt = R[4][:, 0:1024]
        TT = scr[:, 10240:12288].rearrange("p (u t) -> p u t", u=16)
        Ep = scr[:, 0:2064].rearrange("p (m c t) -> p m c t", m=8, c=2)
        En = scr[:, 2064:4112].rearrange("p (m c t) -> p m c t", m=8, c=2)
        AA, T1, SQ = (scr[:, 4112 + 2048 * n:6160 + 2048 * n] for n in range(3))
        LS = ring[:, 4096:8192]

        ss, rstd = small[:, 0:2], small[:, 2:4]
        cc, ncc = small[:, 8:24], small[:, 24:40]
        dsc = small[:, 40:48]
        alog, dtb, negA = small[0:8, 56:57], small[0:8, 57:58], small[0:8, 58:59]
        tb = small[:, 64:128].rearrange("p (w c h) -> p w c h", w=4, c=2)

        w_in = A["w_in"].rearrange("l (k p) c -> p (l k) c", p=P)
        w_proj = [A[n].rearrange("l (k p) c -> p (l k) c", p=P) for n in ("proj_a", "proj_b", "w_out")]
        w_gu = A["w_gate_up"].rearrange("l e (k p) c -> p (l e k) c", p=P)
        w_dn = A["w_down"].rearrange("l e (k p) c -> p (l e k) c", p=P)
        b_gu = A["b_gate_up"].rearrange("l e c -> (l e) c")

        H2 = R[0].rearrange("p (c d) -> p c d", c=2)
        h2T = W3[1]
        rt_w = R[3][:, 0:256].rearrange("p (k e) -> p k e", k=KT)
        rt_b = R[3][0:1, 256:288]
        tab = R[2][:, 0:34 * 4].rearrange("p (e w) -> p e w", e=34)
        lg, sel, gt, tmp32 = (R[2][:, 256 + 64 * n:320 + 64 * n].rearrange("p (c e) -> p c e", c=2) for n in range(4))
        top, topi = R[2][:, 512:528].rearrange("p (c e) -> p c e", c=2), R[2][:, 528:544].rearrange("p (c e) -> p c e", c=2)
        topf = R[2][:, 544:560].rearrange("p (c e) -> p c e", c=2)
        nmx, gsum, grec = R[2][:, 560:562], R[2][:, 562:564], R[2][:, 564:566]
        cur = R[2][:, 568:576].rearrange("p (q w) -> p q w", q=2)
        cnt = R[2][0:1, 576:608]
        cmax, cge, csum = R[2][0:1, 608:609], R[2][0:1, 610:618], R[2][0:1, 618:619]
        gT = R[2][0:32, 640:896]
        nfb = R[5][:, 0:1024]
        bdn = R[4][0:32, 0:1024]
        brow = R[5][0:1, 1024:2048], R[3][0:1, 1024:2048]
        Psel = R[6][:, 0:256].rearrange("p (c s) -> p c s", c=2)
        Pgat = R[6][:, 256:512].rearrange("p (c s) -> p c s", c=2)
        PgT = R[6][:, 1024:1536].rearrange("p (q c t) -> p q c t", q=2, c=2)
        xgT = R[7].rearrange("p (q k s) -> p q k s", q=2, k=KT)
        ysb = R[10].rearrange("p (q n) -> p q n", q=2)
        glu, sgm = R[8][:, 0:512], R[8][:, 512:1024]
        lin, act_h = R[8][:, 1024:1536], R[8][:, 1536:2048]
        actT = R[9][:, 0:512].rearrange("p (c s) -> p c s", c=4)

        def gu_slot(s):
            return ring[:, s * 2048:(s + 1) * 2048] if s < 6 else scr[:, (s - 6) * 2048:(s - 5) * 2048]

        def dn_slot(s):
            return scr[:, (s + 2) * 2048:(s + 3) * 2048].rearrange("p (k c) -> p k c", k=2)

        block = ctx.enter_context(nc.Block())

        first = [C_Q, C_K, C_V, C_Z, C_R, C_RK, C_RV, C_GA, C_GB]
        MM0 = 4
        HB = 6

        @block.sync
        def _(sp):
            def load(dst, src, sem):
                sp.dma_start(dst, src).then_inc(S(sem), 16)

            load(x[:, :, :], A["x"].rearrange("b (c p) d -> p (b c) d", p=P), "x_in")
            load(cst[:, :], A["consts"], "cst_in")
            load(R[7][0:8, 0:P], A["norm_mix"].rearrange("l (r c) -> (l r) c", c=P), "par_in")
            load(R[7][8:ROWS_A, 0:P], A["gdn_conv"].rearrange("l w (r c) -> (l w r) c", c=P), "par_in")
            at = 0
            for name, n in (("rwkv_mu", 26), ("rwkv_a0", 8), ("rwkv_k_k", 8), ("rwkv_k_a", 8), ("rwkv_r_k", 8),
                            ("rwkv_ln_w", 8), ("rwkv_ln_b", 8), ("norm_ffn", 8), ("gdn_norm", 1)):
                src = A[name].rearrange("l h n -> l (h n)") if name == "rwkv_r_k" else A[name]
                load(R[7][at:at + n, P:2 * P], src.rearrange("l (r c) -> (l r) c", c=P), "par_in")
                at += n
            load(panel[0][:, :, 0:256], w_in[:, :, C_LORA:C_LORA + 256], "panel_in0")
            load(panel[0][:, :, 256:272], w_in[:, :, C_B:C_B + 16], "panel_in0")
            load(scr[:, 0:(LEVELS - 1) * 2 * P], A["masks"], "msk_in")
            load(alog, A["gdn_A_log"].rearrange("l h -> h l"), "row_in")
            load(dtb, A["gdn_dt_bias"].rearrange("l h -> h l"), "row_in")
            with sp.Fori(0, 2) as i:
                for j in range(9):
                    sp.wait_ge(S("mm_ready"), 18 * i + (MM0 + 2 * j - 2))
                    load(panel[(1 + j) % 3], w_in[:, :, bass.ds(512 * i + first[j], PANEL)], f"panel_in{(1 + j) % 3}")
            sp.wait_ge(S("mm_ready"), MM0 + 2 + 2 * 16)
            load(LS[0:64, 0:1024], A["rwkv_w2"].rearrange("l r c -> (l r) c"), "panel_in1")
            load(LS[64:128, 0:1024], A["rwkv_a2"].rearrange("l r c -> (l r) c"), "panel_in1")
            load(LS[:, 1024:2048], A["rwkv_g2"].rearrange("l r c -> (l r) c"), "panel_in1")
            load(LS[0:1, 2048:3072], A["rwkv_w0"], "panel_in1")
            def gate_up(it, e, s):
                sp.wait_ge(S("gu_used"), 8 * it + (s + 1))
                load(gu_slot(s), w_gu[:, bass.ds(8 * e + s, 1), :].rearrange("p k c -> p (k c)"), f"gu_in{s}")

            def down(it, e, s):
                sp.wait_ge(S("dn_used"), 4 * it + (s + 1))
                load(dn_slot(s), w_dn[:, bass.ds(8 * e + 2 * s, 2), :], f"dn_in{s}")

            def biases(it, e):
                sp.wait_ge(S("brow_used"), it + 1)
                for n in range(2):
                    load(brow[n], b_gu[bass.ds(e, 1), 1024 * n:1024 * (n + 1)], "brow_in")

            for q in range(6):
                sp.wait_ge(*[(S("mm_ready"), MM0 + 36), (S("mm_ready"), MM0 + 38), (S("gg_ready"), 4),
                             (S("pj_ready"), 2), (S("pj_ready"), 4), (S("pj_ready"), 6)][q])
                load(panel[(20 + q) % 3], w_proj[q // 2][:, :, PANEL * (q % 2):PANEL * (q % 2 + 1)], f"panel_in{(20 + q) % 3}")
                if q == 2:
                    for s in (6, 7):
                        gate_up(0, 0, s)
                    for s in range(4):
                        down(0, 0, s)
            sp.wait_ge(S("pj_ready"), 8)
            load(rt_w, A["router_w"].rearrange("l (k p) e -> p (l k) e", p=P), "rt_in")
            load(rt_b, A["router_b"], "rt_in")
            load(bdn, A["b_down"].rearrange("l e c -> (l e) c"), "bdn_in")
            load(nfb, A["norm_final"].rearrange("(a d) -> a d", a=1).partition_broadcast(P).rearrange("p a d -> p (a d)"), "nf_in")
            biases(0, 0)
            for s, before in ((4, 8), (5, 8), (0, 10), (1, 10), (2, 12), (3, 12)):
                sp.wait_ge(S("pj_ready"), before)
                gate_up(0, 0, s)

            def expert(it, e):
                for s in range(8):
                    gate_up(it, e, s)
                biases(it, e)
                for s in range(4):
                    down(it, e, s)

            with sp.Fori(1, NE) as e:
                expert(e, e)
            sp.wait_ge(S("passes_known"), 1)
            n = sp.value_load(passes[0:1, 0:1], min_val=1, max_val=T // slots)
            with sp.If(n > 1):
                with sp.Fori(1, n) as b:
                    with sp.Fori(0, NE) as e:
                        expert(NE * b + e, e)
            sp.wait_ge(S("y_ready"), 1)
            load(A["out"].rearrange("b (c p) d -> p (b c) d", p=P), R[1].rearrange("p (c d) -> p c d", c=2), "out_done")
            sp.wait_ge(S("out_done"), 16)

        @block.tensor
        def _(pe):
            mm, tr = nc.tensor.matmul, nc.tensor.transpose

            for name, v in (("mm_ready", MM0), ("gu_used", 8), ("dn_used", 4), ("brow_used", 1)):
                pe.sem_inc(S(name), v)
            pe.wait_ge(S("cst_in"), 16)
            pe.wait_ge(S("par_in"), 16 * 11)
            tr(ps[:, 6, 0:ROWS_A], R[7][0:ROWS_A, 0:P], cst[0:ROWS_A, 0:ROWS_A])
            tr(ps[:, 6, P:P + ROWS_B], R[7][0:ROWS_B, P:2 * P], cst[0:ROWS_B, 0:ROWS_B]).then_inc(S("par_T"), 1)
            pe.wait_ge(S("xs_ready"), 2)
            xs = R[10].rearrange("p (c d) -> p c d", c=2)
            for k in range(KT):
                for c in range(NT):
                    ins = tr(ps[:, k // 2, 256 * (k % 2) + P * c:256 * (k % 2) + P * (c + 1)], xs[:, c, P * k:P * (k + 1)], ident)
            ins.then_inc(S("xT_ready"), 1)

            pe.wait_ge(S("hT_ready"), 1)
            pe.wait_ge(S("panel_in0"), 32)
            for f, (c0, w) in enumerate(((256, 8), (264, 8))):
                for k in range(KT):
                    ins = mm(ps[0:8, 0, T * f:T * (f + 1)], panel[0][:, k, c0:c0 + w], hT[:, k, :], start=k == 0, stop=k == KT - 1)
            ins.then_inc(S("mm_ready"), 1)
            for f in range(2):
                for k in range(KT):
                    ins = mm(ps[:, 1, T * f:T * (f + 1)], panel[0][:, k, P * f:P * (f + 1)], hT[:, k, :], start=k == 0, stop=k == KT - 1)
            ins.then_inc(S("mm_ready"), 1)
            with pe.Fori(0, 2) as i:
                for u in range(18):
                    j, half = u // 2, u % 2
                    if half == 0:
                        pe.wait_ge(S(f"panel_in{(1 + j) % 3}"), 48 * i + 16 * (j // 3 + (3 if (1 + j) % 3 == 0 else 1)))
                    pe.wait_ge(S("act_first"), 18 * i + (u - 3) if u >= 4 else (13 + u) * i + 2)
                    pe.wait_ge(S("dve_free"), 14 * i + (min(u - 6, 13) + 3 if u >= 6 else min(u + 1, 2)))
                    for f in range(2):
                        for k in range(KT):
                            ins = mm(ps[:, (2 + u) % HB, T * f:T * (f + 1)],
                                     panel[(1 + j) % 3][:, k, P * (2 * half + f):P * (2 * half + f + 1)], hT[:, k, :],
                                     start=k == 0, stop=k == KT - 1)
                    ins.then_inc(S("mm_ready"), 1)

            pe.wait_ge(S("act_first"), 38)
            pe.wait_ge(S("dve_free"), 30)
            for u in range(8):
                pe.wait_ge(S("gsq_ready"), u + 1)
                mm(ps[:, u, :], ones, scr[:, 512 * u:512 * (u + 1)], start=True, stop=True).then_inc(S("gnm_ready"), 1)
            pe.wait_ge(S("gate_row"), 5)
            pe.wait_ge(S("gnm_read"), 8)
            for w in range(4):
                for c in range(NT):
                    ins = tr(ps[:, 6, 8 * (2 * w + c):8 * (2 * w + c) + 8], rows[0:8, w, P * c:P * (c + 1)], cst[0:8, 0:8])
            ins.then_inc(S("tb_ready"), 1)
            pe.wait_ge(S("conv_done"), 12)
            for w in range(4):
                for q in range(4):
                    ins = tr(ps[:, w, P * q:P * (q + 1)], W3[4][:, 4 * (w % 2) + q, P * (w // 2):P * (w // 2 + 1)], ident)
                ins.then_inc(S("vT_ready"), 1)
            pe.wait_ge(S("vT_read"), 4)
            pe.wait_ge(S("kq_ready"), 8)
            for h in range(HEADS):
                b = 2 * (h % 2)
                if h >= 2:
                    pe.wait_ge(S("head_done"), h - 1)
                mm(ps[:, b, :], cst[0:8, K_SEL + P * h:K_SEL + P * (h + 1)], rows[0:8, 0:2, :].rearrange("h w t -> h (w t)"), start=True, stop=True)
                for c in range(NT):
                    ins = mm(ps[:, b + 1, T * c:T * (c + 1)], KQ[:, h, c, 0, :], KQ[:, h, c, :, :].rearrange("p w t -> p (w t)"), start=True, stop=True)
                ins.then_inc(S("head_ready"), 1)

            def inverse(v):
                WS = R[9] if v else R[0]
                unit = lambda r, u: r[:, P * u:P * (u + 1)]
                for g in range(4):
                    if g >= 2:
                        pe.wait_ge(S("t_done"), 28 * v + g - 1)
                    for q in range(4):
                        ins = tr(ps[:, 4 + 2 * (g % 2), P * q:P * (q + 1)], MM[:, 4 * g + q, 0, :], ident)
                    ins.then_inc(S("t_ready"), 1)
                with pe.Fori(0, LEVELS - 2) as l:
                    for g in range(4):
                        pe.wait_ge(S("t_done"), 4 * l + (28 * v + g + 1))
                        for q in range(4):
                            ins = mm(unit(ps[:, g, :], q), MM[:, 4 * g + q, 0, :], TI[:, 4 * g + q, :], start=True, stop=True)
                        ins.then_inc(S("w_ready"), 1)
                    for g in range(4):
                        pe.wait_ge(S("w_copied"), 4 * l + (24 * v + g + 1))
                        pe.wait_ge(S("t_done"), 4 * l + (28 * v + g + 3))
                        b = 4 + 2 * (g % 2)
                        for q in range(4):
                            mm(unit(ps[:, b, :], q), TT[:, 4 * g + q, :], unit(WS, 4 * g + q), start=True, stop=True)
                        for q in range(4):
                            ins = mm(unit(ps[:, b + 1, :], q), unit(WS, 4 * g + q), TT[:, 4 * g + q, :], start=True, stop=True)
                        ins.then_inc(S("t_ready"), 1)
                lo, hi = slice(0, 64), slice(64, P)
                for g in range(4):
                    pe.wait_ge(S("t_done"), 28 * v + 4 * (LEVELS - 2) + g + 1)
                    for q in range(4):
                        ins = mm(ps[hi, g, 64 * q:64 * q + 64], MM[lo, 4 * g + q, 0, hi], TI[lo, 4 * g + q, lo], start=True, stop=True)
                    ins.then_inc(S("w_ready"), 1)
                for g in range(4):
                    pe.wait_ge(S("w_copied"), 24 * v + 4 * (LEVELS - 2) + g + 1)
                    pe.wait_ge(S("t_done"), 28 * v + 4 * (LEVELS - 2) + g + 3)
                    for q in range(4):
                        ins = mm(ps[lo, 4 + 2 * (g % 2), 64 * q:64 * q + 64], unit(WS, 4 * g + q)[hi, lo], TT[hi, 4 * g + q, hi], start=True, stop=True)
                    ins.then_inc(S("t_ready"), 1)
                pe.wait_ge(S("t_done"), 28 * (v + 1))

            pe.wait_ge(S("head_done"), 8)
            inverse(0)

            X, Kd, U = R[0][:, 0:1024], R[0][:, 1024:2048], scr[:, 8192:10240]
            QD, S1 = R[4][:, 0:1024], R[4][:, 1024:2048]
            hs = lambda t, h: t[:, P * h:P * (h + 1)]
            pe.wait_ge(S("gx_ready"), 1)
            for h in range(HEADS):
                ins = mm(ps[:, h // 4, P * (h % 4):P * (h % 4 + 1)], TT[:, 2 * h, :], hs(X, h), start=True, stop=True)
            ins.then_inc(S("gu0_ready"), 1)
            for h in range(HEADS):
                ins = tr(ps[:, 2 + h // 4, P * (h % 4):P * (h % 4 + 1)], KQ[:, h, 0, 0, :], ident)
            ins.then_inc(S("gkd_ready"), 1)
            pe.wait_ge(S("gu0_copied"), 1)
            pe.wait_ge(S("gkd_copied"), 1)
            for h in range(HEADS):
                ins = mm(ps[:, 4 + h // 4, P * (h % 4):P * (h % 4 + 1)], hs(Kd, h), hs(U, h), start=True, stop=True)
            ins.then_inc(S("gs1_ready"), 1)
            pe.wait_ge(S("gs1_copied"), 1)
            for h in range(HEADS):
                ins = mm(ps[:, 6 + h // 4, P * (h % 4):P * (h % 4 + 1)], KQ[:, h, 1, 0, :], hs(S1, h), start=True, stop=True)
            ins.then_inc(S("gks_ready"), 1)
            pe.wait_ge(S("gx_ready"), 2)
            for h in range(HEADS):
                ins = mm(ps[:, 2 + h // 4, P * (h % 4):P * (h % 4 + 1)], TT[:, 2 * h + 1, :], hs(X, h), start=True, stop=True)
            ins.then_inc(S("gu1_ready"), 1)
            pe.wait_ge(S("gu1_copied"), 1)
            for h in range(HEADS):
                b = (0, 1, 4, 5)[h // 2]
                o0, o1 = (ps[:, b, T * (h % 2) + P * c:T * (h % 2) + P * (c + 1)] for c in range(2))
                mm(o0, hs(U, h), MM[:, 2 * h, 1, :], start=True, stop=True)
                mm(o1, hs(S1, h), hs(QD, h), start=True, stop=False)
                ins = mm(o1, U[:, 1024 + P * h:1024 + P * (h + 1)], MM[:, 2 * h + 1, 1, :], start=False, stop=True)
                if h % 2:
                    ins.then_inc(S("got_ready"), 1)
            for q in range(4):
                pe.wait_ge(S("osq_ready"), q + 1)
                mm(ps[:, (2, 3, 6, 7)[q], :], ones, R[1][:, 512 * q:512 * (q + 1)], start=True, stop=True).then_inc(S("onm_ready"), 1)

            pe.wait_ge(S("panel_in1"), 16 * 10)
            pe.wait_ge(S("lora_act"), 1)
            pe.wait_ge(S("got_read"), 4)
            for u in range(4):
                c, n = u // 2, u % 2
                b = (0, 1, 4, 5)[u]
                mm(ps[:, b, :], lora[0:64, 0, P * c:P * (c + 1)], LS[0:64, 512 * n:512 * (n + 1)], start=True, stop=False)
                mm(ps[:, b, :], cst[0:1, K_ONE:K_ONE + P], LS[0:1, 2048 + 512 * n:2560 + 512 * n], start=False, stop=True).then_inc(S("rz_ready"), 1)
            pe.wait_ge(S("onm_read"), 4)
            for m in range(8):
                b = (2, 3, 6, 7)[m // 2]
                ins = mm(ps[:, b, T * (m % 2):T * (m % 2 + 1)], LS[64:128, P * m:P * (m + 1)], lora[64:128, 0, :], start=True, stop=True)
                if m % 2:
                    ins.then_inc(S("raa_ready"), 1)
            SG = R[0].rearrange("p (c d) -> p c d", c=2)
            for m in range(8):
                b = (0, 1, 4, 5)[m // 2]
                if m % 2 == 0:
                    pe.wait_ge(S("rz_read"), 4)
                for c in range(NT):
                    ins = mm(ps[:, b, P * (2 * (m % 2) + c):P * (2 * (m % 2) + c + 1)], SG[:, c, P * m:P * (m + 1)], incl, start=True, stop=True)
                if m % 2:
                    ins.then_inc(S("rg_ready"), 1)
            pe.wait_ge(S("raa_read"), 8)
            pe.wait_ge(S("rsq_ready"), 1)
            for q in range(4):
                mm(ps[:, (2, 3, 6, 7)[q], :], blk, SQ[:, 512 * q:512 * (q + 1)], start=True, stop=True).then_inc(S("rnm_ready"), 1)
            pe.wait_ge(S("rexp_done"), 1)
            for w in range(4):
                for q in range(4):
                    ins = tr(ps[:, (0, 1, 4, 5)[w], P * q:P * (q + 1)], W3[10][:, 4 * (w % 2) + q, P * (w // 2):P * (w // 2 + 1)], ident)
                ins.then_inc(S("rv_ready"), 1)
            pe.wait_ge(S("rnm_read"), 4)
            pe.wait_ge(S("rrk_ready"), 1)
            for q in range(4):
                mm(ps[:, (2, 3, 6, 7)[q], :], blk, R[8][:, 512 * q:512 * (q + 1)], start=True, stop=True).then_inc(S("rbn_ready"), 1)

            V = R[0].rearrange("p (c d) -> p c d", c=2)
            for hf in range(2):
                pe.wait_ge(S("prep_done"), 1)
                pe.wait_ge(S("rv_read"), 4)
                if hf:
                    pe.wait_ge(S("rot_read"), 1)
                for u in range(16):
                    m, p, c = 4 * hf + u // 4, (u // 2) % 2, u % 2
                    q = slice(64 * p, 64 * p + 64)
                    if u >= 4:
                        pe.wait_ge(S("rm_read"), 16 * hf + u - 3)
                    rhs = AR[q, m, c, :, :].rearrange("p w t -> p (w t)")
                    mm(ps[:, u % 4, 0:T], BK[q, m, c, 0, :], rhs, start=True, stop=True)
                    mm(ps[:, u % 4, T:2 * T], BK[q, m, c, 1, :], rhs, start=True, stop=True).then_inc(S("rm_ready"), 1)
                pe.wait_ge(S("rm_read"), 16 * (hf + 1))
                inverse(1 + hf)
                vh = lambda c, h: V[:, c, 512 * hf + 64 * h:512 * hf + 64 * h + 64]
                YS, KB = R[9][:, 0:512], R[9][:, 1024:2048]
                SS = R[9][:, 512:768]
                U0, U1 = scr[:, 8192:8704], scr[:, 8704:9216]
                for h in range(8):
                    ins = mm(ps[:, 0, 64 * h:64 * h + 64], MM[:, 2 * h, 2, :], vh(0, h), start=True, stop=True)
                ins.then_inc(S("ry_ready"), 1)
                for w in range(2):
                    for m in range(4):
                        ins = tr(ps[:, 2 + w, P * m:P * (m + 1)], BK[:, 4 * hf + m, 0, w, :], ident)
                ins.then_inc(S("rkb_ready"), 1)
                pe.wait_ge(S("ry_copied"), 2 * hf + 1)
                for h in range(8):
                    ins = mm(ps[:, 1, 64 * h:64 * h + 64], TT[:, 2 * h, :], YS[:, 64 * h:64 * h + 64], start=True, stop=True)
                ins.then_inc(S("ru_ready"), 1)
                pe.wait_ge(S("ru_copied"), 2 * hf + 1)
                pe.wait_ge(S("rkb_copied"), hf + 1)
                for h in range(8):
                    m, p = h // 2, h % 2
                    out = ps[64 * p:64 * p + 64, 4, 64 * m:64 * m + 64]
                    mm(out, KB[:, 512 + P * m + 64 * p:512 + P * m + 64 * p + 64], vh(0, h), start=True, stop=False)
                    ins = mm(out, KB[:, P * m + 64 * p:P * m + 64 * p + 64], U0[:, 64 * h:64 * h + 64], start=False, stop=True)
                ins.then_inc(S("rs_ready"), 1)
                pe.wait_ge(S("rs_copied"), hf + 1)
                for h in range(8):
                    m, p = h // 2, h % 2
                    q = slice(64 * p, 64 * p + 64)
                    out = ps[:, 5 + 2 * p, 64 * m:64 * m + 64]
                    mm(out, AR[q, 4 * hf + m, 1, 0, :], SS[q, 64 * m:64 * m + 64], start=True, stop=False)
                    ins = mm(out, MM[:, 2 * h + 1, 2, :], vh(1, h), start=False, stop=True)
                ins.then_inc(S("ry_ready"), 1)
                pe.wait_ge(S("ry_copied"), 2 * hf + 2)
                for h in range(8):
                    ins = mm(ps[:, 6, 64 * h:64 * h + 64], TT[:, 2 * h + 1, :], YS[:, 64 * h:64 * h + 64], start=True, stop=True)
                ins.then_inc(S("ru_ready"), 1)
                pe.wait_ge(S("ru_copied"), 2 * hf + 2)
                for h in range(8):
                    m, p = h // 2, h % 2
                    q = slice(64 * p, 64 * p + 64)
                    o0, o1 = (ps[q, 2 + m // 2, T * (m % 2) + P * c:T * (m % 2) + P * (c + 1)] for c in range(2))
                    mm(o0, vh(0, h), MM[:, 2 * h, 3, :], start=True, stop=False)
                    mm(o0, U0[:, 64 * h:64 * h + 64], MM[:, 2 * h, 1, :], start=False, stop=True)
                    mm(o1, vh(1, h), MM[:, 2 * h + 1, 3, :], start=True, stop=False)
                    mm(o1, U1[:, 64 * h:64 * h + 64], MM[:, 2 * h + 1, 1, :], start=False, stop=False)
                    ins = mm(o1, SS[q, 64 * m:64 * m + 64], AR[q, 4 * hf + m, 1, 1, :], start=False, stop=True)
                ins.then_inc(S("rot_ready"), 1)

            pe.wait_ge(S("rot_read"), 2)
            for q in range(4):
                mm(ps[:, 4 + q, :], blk, R[10][:, 512 * q:512 * (q + 1)], start=True, stop=True).then_inc(S("rmu_ready"), 1)
            for q in range(4):
                pe.wait_ge(S("rvs_ready"), q + 1)
                mm(ps[:, q, :], blk, R[0][:, 512 * q:512 * (q + 1)], start=True, stop=True).then_inc(S("rvr_ready"), 1)
            pe.wait_ge(S("rmu_read"), 4)
            for m in range(8):
                ins = mm(ps[:, 4 + m // 2, T * (m % 2):T * (m % 2 + 1)], LS[:, 1024 + P * m:1024 + P * (m + 1)], lora[:, 1, :], start=True, stop=True)
                if m % 2:
                    ins.then_inc(S("gg_ready"), 1)

            pe.wait_ge(S("ya_ready"), 1)
            pe.wait_ge(S("rvr_read"), 4)
            for u in range(8):
                q = u // 2
                if u == 4:
                    pe.wait_ge(S("yb_ready"), 1)
                if u % 2 == 0:
                    pe.wait_ge(S(f"panel_in{(20 + q) % 3}"), (16 * 7, 16 * 9, 16 * 11, 16 * 8)[q])
                src = W3[5] if u < 4 else W3[10]
                for f in range(2):
                    for k in range(KT):
                        ins = mm(ps[:, u, T * f:T * (f + 1)], panel[(20 + q) % 3][:, k, P * (2 * (u % 2) + f):P * (2 * (u % 2) + f + 1)],
                                 src[:, k, :], start=k == 0, stop=k == KT - 1)
                ins.then_inc(S("pj_ready"), 1)
            pe.wait_ge(S("merged"), 1)
            for n in range(2):
                pe.wait_ge(S(f"panel_in{(24 + n) % 3}"), (16 * 10, 16 * 12)[n])
                for c in range(NT):
                    for k in range(KT):
                        ins = mm(ps[:, 2 * n + c, :], W3[6][:, k, P * c:P * (c + 1)], panel[(24 + n) % 3][:, k, :], start=k == 0, stop=k == KT - 1)
                    ins.then_inc(S("pj_ready"), 1)

            pe.wait_ge(S("h2_ready"), 1)
            for k in range(KT):
                for c in range(NT):
                    ins = tr(ps[:, 4 + k // 2, 256 * (k % 2) + P * c:256 * (k % 2) + P * (c + 1)], H2[:, c, P * k:P * (k + 1)], ident)
            ins.then_inc(S("h2T_ready"), 1)
            pe.wait_ge(S("h2T_copied"), 1)
            pe.wait_ge(S("rt_in"), 32)
            for c in range(NT):
                out = ps[:, 0, NE * c:NE * (c + 1)]
                for k in range(KT):
                    mm(out, h2T[:, k, P * c:P * (c + 1)], rt_w[:, k, :], start=k == 0, stop=False)
                ins = mm(out, cst[0:1, K_ONE:K_ONE + P], rt_b, start=False, stop=True)
            ins.then_inc(S("lg_ready"), 1)
            pe.wait_ge(S("sel_ready"), 1)
            mm(ps[:, 1, 0:NE], strict, sel[:, 0, :], start=True, stop=True)
            mm(ps[:, 1, NE:2 * NE], strict, sel[:, 1, :], start=True, stop=False)
            mm(ps[:, 1, NE:2 * NE], ones, sel[:, 0, :], start=False, stop=True)
            mm(ps[0:1, 1, 2 * NE:3 * NE], ones[:, 0:1], sel[:, 0, :], start=True, stop=False)
            mm(ps[0:1, 1, 2 * NE:3 * NE], ones[:, 0:1], sel[:, 1, :], start=False, stop=True)
            for c in range(NT):
                ins = tr(ps[0:NE, 2, P * c:P * (c + 1)], gt[:, c, :], ident)
            ins.then_inc(S("pos_ready"), 1)
            pe.wait_ge(S("pos_read"), 1)
            pe.wait_ge(S("bdn_in"), 16)
            for c in range(NT):
                for n in range(2):
                    mm(ps[:, 2 * c + n, :], gT[:, P * c:P * (c + 1)], bdn[:, 512 * n:512 * (n + 1)], start=True, stop=False, skip_group_check=True)

            def scatter(par_, banks=range(4), last=False):
                for bank in banks:
                    c, n = bank // 2, bank % 2
                    ins = mm(ps[:, bank, :], PgT[:, par_, c, :], ysb[:, par_, 512 * n:512 * (n + 1)], start=False, stop=last, skip_group_check=True)
                return ins

            def gather(half):
                for k in range(4):
                    for c in range(NT):
                        kk = 4 * half + k
                        ins = mm(ps[:, 7, P * k:P * (k + 1)], H2[:, c, P * kk:P * (kk + 1)], Psel[:, c, :], start=c == 0, stop=c == NT - 1)
                ins.then_inc(S("xg_ready"), 1)

            def expert(it, pair, par_, q):
                pe.wait_ge(S("xg_copied"), it + 2 - q)
                for k in range(KT):
                    if q == 0 and k == 2:
                        for c in range(NT):
                            ins = tr(ps[:, 7, P * c:P * (c + 1)], Pgat[:, c, :], ident)
                        ins.then_inc(S("pt_ready"), 1)
                    pe.wait_ge(S(f"gu_in{k}"), 16 * it + 16)
                    for n in range(4):
                        s = slice(64 * (n % 2), 64 * (n % 2) + 64)
                        ins = mm(ps[s, 4 + n // 2, :], xgT[:, par_, k, 64 * q:64 * q + 64], gu_slot(k)[:, 512 * n:512 * (n + 1)],
                                 start=k == 0, stop=False, skip_group_check=True)
                    ins.then_inc(S("gu_used"), 1)
                pe.wait_ge(S("brow_in"), 32 * it + 32)
                for n in range(4):
                    s = slice(64 * (n % 2), 64 * (n % 2) + 64)
                    ins = mm(ps[s, 4 + n // 2, :], cst[0:1, K_ONE:K_ONE + 64], brow[n // 2][:, 512 * (n % 2):512 * (n % 2 + 1)],
                             start=False, stop=True, skip_group_check=True)
                ins.then_inc(S("brow_used"), 1)
                pe.wait_ge(S("sel_made"), pair + 2)
                pe.wait_ge(S("pt_copied") if q == 0 else S("xg_copied"), pair + 1 if q == 0 else it + 2)
                gather(q)
                pe.wait_ge(S("y_copied"), it + 1)
                scatter(1 - par_, (2 * q,))
                pe.wait_ge(S("h_ready"), it + 1)
                for j in range(4):
                    ins = tr(ps[:, 6, P * j:P * (j + 1)], act_h[:, P * j:P * (j + 1)], ident)
                ins.then_inc(S("at_ready"), 1)
                scatter(1 - par_, (2 * q + 1,))
                pe.wait_ge(S("at_copied"), it + 1)
                for kk in range(KT):
                    b, half, sub = kk // 4, (kk // 2) % 2, kk % 2
                    if kk % 2 == 0:
                        pe.wait_ge(S(f"dn_in{kk // 2}"), 16 * it + 16)
                    for n in range(2):
                        ins = mm(ps[64 * n:64 * n + 64, 6, :], actT[:, 2 * b + sub, 64 * half:64 * half + 64],
                                 dn_slot(kk // 2)[:, kk % 2, 512 * n:512 * (n + 1)], start=kk == 0, stop=kk == KT - 1, skip_group_check=True)
                    if kk % 2:
                        ins.then_inc(S("dn_used"), 1)

            pe.wait_ge(S("sel_made"), 1)
            gather(0)
            pe.wait_ge(S("xg_copied"), 1)
            gather(1)
            pe.wait_ge(S("passes_known"), 1)
            n = pe.value_load(passes[0:1, 0:1], min_val=1, max_val=T // slots)
            with pe.Fori(0, n) as b:
                with pe.Fori(0, NE // 4) as i:
                    for w in range(4):
                        expert(NE * b + 4 * i + w, NE // 2 * b + 2 * i + w // 2, w // 2, w % 2)
            pe.wait_ge(S("y_copied"), NE * n + 1)
            scatter(1, last=True).then_inc(S("sum_ready"), 1)

        @block.scalar
        def _(act):
            af = nc.scalar.activation

            act.wait_ge(S("x_in"), 16)
            for c in range(NT):
                ins = af(R[9][:, D * c:D * (c + 1)], x[:, c, :], ACT.Square, accum_out=ss[:, c:c + 1])
            ins.then_inc(S("act_step"), 1)
            act.wait_ge(S("act_step"), 1)
            act.wait_ge(S("cst_in"), 16)
            af(rstd, ss, ACT.Sqrt, scale=1.0 / D, bias=col(0)).then_inc(S("ss_ready"), 1)

            act.wait_ge(S("mm_ready"), MM0 + 1)
            af(rows[0:8, 5, :], ps[0:8, 0, T:2 * T], ACT.Copy).then_inc(S("act_first"), 1)
            act.wait_ge(S("mm_ready"), MM0 + 2)
            act.wait_ge(S("par_ready"), 1)
            af(lora[:, 0, :], ps[:, 1, 0:T], ACT.Copy, scale=omm[:, 24:25])
            af(lora[:, 1, :], ps[:, 1, T:2 * T], ACT.Copy, scale=omm[:, 25:26]).then_inc(S("act_first"), 1)
            with act.Fori(0, 2) as i:
                for u in range(18):
                    j, half = u // 2, u % 2
                    b = (2 + u) % HB
                    act.wait_ge(S("mm_ready"), 18 * i + (MM0 + 3 + u))
                    if u < 6:
                        if u:
                            act.wait_ge(S("conv_done"), 6 * i + u)
                        for f in range(2):
                            ins = af(R[3][:, T * f:T * (f + 1)], ps[:, b, T * f:T * (f + 1)], ACT.Copy,
                                     scale=par[:, bass.ds(4 * i + (8 + 24 * 3 + 8 * j + 2 * half + f), 1)])
                        ins.then_inc(S("act_first"), 1)
                        act.wait_ge(S("dve_free"), 14 * i + (u + 3))
                        af(R[3][:, 512:1024], R[3][:, 0:512], ACT.Sigmoid).then_inc(S("act_sig"), 1)
                    elif u < 8:
                        if u == 6:
                            act.wait_ge(S("conv_done"), 6 * i + 6)
                        af(R[3][:, 1024 + 512 * half:1536 + 512 * half], ps[:, b, :], ACT.Sigmoid).then_inc(S("act_first"), 1)
                    elif u < 14:
                        for f in range(2):
                            t = 8 * (j - 4) + 2 * half + f
                            ins = af(R[4 + j][:, bass.ds(1024 * i + T * (2 * half + f), T)], ps[:, b, T * f:T * (f + 1)], ACT.Copy,
                                     scale=omm[:, bass.ds(4 * i + t, 1)])
                        ins.then_inc(S("act_first"), 1)
                    else:
                        af(R[6 + (j - 7)][:, bass.ds(1024 * i + 512 * half, 512)], ps[:, b, :], ACT.Sigmoid).then_inc(S("act_first"), 1)

            act.wait_ge(S("msk_read"), 1)
            act.wait_ge(S("conv_done"), 12)
            for u in range(8):
                af(scr[:, 512 * u:512 * (u + 1)].rearrange("p (h c t) -> p h c t", h=2, c=2), KQ[:, 2 * (u // 2):2 * (u // 2) + 2, :, u % 2, :],
                   ACT.Square).then_inc(S("gsq_ready"), 1)
            act.wait_ge(S("dve_free"), 30)
            act.wait_ge(S("act_first"), 38)
            af(rows[:, 1, :], rows[:, 4, :], ACT.Sigmoid).then_inc(S("gate_row"), 1)
            act.wait_ge(S("row_in"), 32)
            act.wait_ge(S("gate_row"), 2)
            af(negA, alog, ACT.Exp)
            af(rows[:, 3, :], rows[:, 3, :], ACT.Exp).then_inc(S("act_step"), 1)
            act.wait_ge(S("act_step"), 2)
            af(rows[:, 3, :], rows[:, 3, :], ACT.Ln, bias=cst[0:8, K_COL + 3:K_COL + 4]).then_inc(S("gate_row"), 1)
            act.wait_ge(S("gate_row"), 4)
            af(rows[:, 2, :], rows[:, 0, :], ACT.Exp)
            af(rows[:, 3, :], rows[:, 3, :], ACT.Exp).then_inc(S("gate_row"), 1)
            for u in range(8):
                act.wait_ge(S("gnm_ready"), u + 1)
                af(scr[:, 4096 + 512 * u:4608 + 512 * u], ps[:, u, :], ACT.Sqrt, scale=float(P) if u % 2 else 1.0, bias=col(u % 2)).then_inc(S("gnm_read"), 1)
            for w in range(4):
                act.wait_ge(S("vT_ready"), w + 1)
                af(R[3][:, 1024 * (w // 2) + 512 * (w % 2):1024 * (w // 2) + 512 * (w % 2) + 512], ps[:, w, :], ACT.Copy).then_inc(S("vT_read"), 1)
            DM, EG = TI2[:, 0:256], TI2[:, 768:896]
            for h in range(HEADS):
                act.wait_ge(S("gd_ready"), h + 1)
                af(DM, DM, ACT.Exp)
                af(EG, ps[:, 2 * (h % 2), P:2 * P], ACT.Exp).then_inc(S("ge_ready"), 1)

            def inverse(v):
                WS = R[9] if v else R[0]
                act.wait_ge(*[(S("head_done"), 8), (S("prep_done"), 1), (S("rot_ready"), 1)][v])
                af(TI, ident.unsqueeze(1).broadcast_to([P, 16, P]), ACT.Copy).then_inc(S("ti_ready"), 1)
                with act.Fori(0, LEVELS - 2) as l:
                    for g in range(4):
                        act.wait_ge(S("w_ready"), 4 * l + (24 * v + g + 1))
                        af(WS[:, 512 * g:512 * (g + 1)], ps[:, g, :], ACT.Copy).then_inc(S("w_copied"), 1)
                for g in range(4):
                    act.wait_ge(S("w_ready"), 24 * v + 4 * (LEVELS - 2) + g + 1)
                    af(WS[64:P, 512 * g:512 * (g + 1)].rearrange("p (u t) -> p u t", u=4)[:, :, 0:64],
                       ps[64:P, g, 0:T].rearrange("p (u t) -> p u t", u=4), ACT.Copy).then_inc(S("w_copied"), 1)

            inverse(0)
            U = scr[:, 8192:10240]
            two = lambda r: r.rearrange("p (b c) -> p b c", b=2)
            act.wait_ge(S("gu0_ready"), 1)
            af(two(U[:, 0:1024]), ps[:, 0:2, :], ACT.Copy).then_inc(S("gu0_copied"), 1)
            act.wait_ge(S("gs1_ready"), 1)
            af(two(R[4][:, 1024:2048]), ps[:, 4:6, :], ACT.Copy).then_inc(S("gs1_copied"), 1)
            act.wait_ge(S("gu1_ready"), 1)
            af(two(U[:, 1024:2048]), ps[:, 2:4, :], ACT.Copy).then_inc(S("gu1_copied"), 1)
            for q in range(4):
                act.wait_ge(S("got_ready"), q + 1)
                af(R[1][:, 512 * q:512 * (q + 1)], ps[:, (0, 1, 4, 5)[q], :], ACT.Square).then_inc(S("osq_ready"), 1)
            for q in range(4):
                act.wait_ge(S("onm_ready"), q + 1)
                af(R[1][:, 512 * q:512 * (q + 1)], ps[:, (2, 3, 6, 7)[q], :], ACT.Sqrt, scale=1.0 / P, bias=col(0)).then_inc(S("onm_read"), 1)

            af(lora[0:64, 0, :], lora[0:64, 0, :], ACT.Tanh)
            af(lora[:, 1, :], lora[:, 1, :], ACT.Sigmoid).then_inc(S("lora_act"), 1)
            for u in range(4):
                act.wait_ge(S("rz_ready"), u + 1)
                af(R[0][:, 512 * u:512 * (u + 1)], ps[:, (0, 1, 4, 5)[u], :], ACT.Sigmoid).then_inc(S("rz_read"), 1)
            for m in range(8):
                act.wait_ge(S("raa_ready"), m // 2 + 1)
                af(AA[:, T * m:T * (m + 1)], ps[:, (2, 3, 6, 7)[m // 2], T * (m % 2):T * (m % 2 + 1)], ACT.Sigmoid,
                   bias=par[:, P_A0 + m:P_A0 + m + 1]).then_inc(S("raa_read"), 1)
            act.wait_ge(S("rcc_ready"), 1)
            for m in range(8):
                for c in range(NT):
                    src = ps[:, (0, 1, 4, 5)[m // 2], P * (2 * (m % 2) + c):P * (2 * (m % 2) + c + 1)]
                    af(Ep[:, m, c, 1:P + 1], src, ACT.Exp, scale=-DECAY, bias=cc[:, 2 * m + c:2 * m + c + 1])
                    af(En[:, m, c, :], src, ACT.Exp, scale=DECAY, bias=ncc[:, 2 * m + c:2 * m + c + 1])
            af(Ep[:, :, :, 0], cc.rearrange("p (m c) -> p m c", m=8), ACT.Exp)
            af(dsc, dsc, ACT.Exp).then_inc(S("rexp_done"), 1)
            for q in range(4):
                act.wait_ge(S("rnm_ready"), q + 1)
                af(SQ[:, 512 * q:512 * (q + 1)], ps[:, (2, 3, 6, 7)[q], :], ACT.Sqrt, bias=col(0)).then_inc(S("rnm_read"), 1)
            for w in range(4):
                act.wait_ge(S("rv_ready"), w + 1)
                af(R[0][:, 1024 * (w // 2) + 512 * (w % 2):1024 * (w // 2) + 512 * (w % 2) + 512], ps[:, (0, 1, 4, 5)[w], :], ACT.Copy).then_inc(S("rv_read"), 1)
            for hf in range(2):
                inverse(1 + hf)
                for c in range(NT):
                    act.wait_ge(S("ry_ready"), 2 * hf + c + 1)
                    if c == 0:
                        af(R[9][:, 0:512], ps[:, 0, :], ACT.Copy).then_inc(S("ry_copied"), 1)
                    else:
                        pair = R[9][:, 0:512].rearrange("p (m w v) -> p m w v", m=4, w=2)
                        for w in range(2):
                            ins = af(pair[:, :, w, :], ps[:, 5 + 2 * w, 0:256].rearrange("p (m v) -> p m v", m=4), ACT.Copy)
                        ins.then_inc(S("ry_copied"), 1)
                    act.wait_ge(S("ru_ready"), 2 * hf + c + 1)
                    af(scr[:, 8192 + 512 * c:8704 + 512 * c], ps[:, (1, 6)[c], :], ACT.Copy, scale=-1.0).then_inc(S("ru_copied"), 1)
                act.wait_ge(S("rot_ready"), hf + 1)
                af(two(R[10][:, 1024 * hf:1024 * (hf + 1)]), ps[:, 2:4, :], ACT.Copy).then_inc(S("rot_read"), 1)
            for q in range(4):
                act.wait_ge(S("rmu_read"), q + 1)
                af(R[0][:, 512 * q:512 * (q + 1)], R[10][:, 512 * q:512 * (q + 1)], ACT.Square).then_inc(S("rvs_ready"), 1)
            for q in range(4):
                act.wait_ge(S("rvr_ready"), q + 1)
                af(R[0][:, 512 * q:512 * (q + 1)], ps[:, q, :], ACT.Sqrt, scale=1.0 / 64, bias=col(2)).then_inc(S("rvr_read"), 1)

            act.wait_ge(S("x1_ready"), 4)
            for c in range(NT):
                ins = af(R[1][:, D * c:D * (c + 1)], x[:, c, :], ACT.Square, accum_out=small[:, 128 + c:129 + c])
            ins.then_inc(S("act_step"), 1)
            act.wait_ge(S("act_step"), 3)
            af(small[:, 130:132], small[:, 128:130], ACT.Sqrt, scale=1.0 / D, bias=col(0)).then_inc(S("ms2_ready"), 1)
            act.wait_ge(S("top_ready"), 1)
            for c in range(NT):
                ins = af(tmp32[:, c, :], lg[:, c, :], ACT.Exp, bias=nmx[:, c:c + 1])
            ins.then_inc(S("lgexp_ready"), 1)

            def expert(it):
                act.wait_ge(S("glu_ready"), it + 1)
                af(sgm, glu, ACT.Sigmoid, scale=GLU_ALPHA).then_inc(S("sig_ready"), 1)

            act.wait_ge(S("passes_known"), 1)
            n = act.value_load(passes[0:1, 0:1], min_val=1, max_val=T // slots)
            with act.Fori(0, n) as b:
                with act.Fori(0, NE) as e:
                    expert(NE * b + e)
            act.wait_ge(S("x2_ready"), 1)
            for c in range(NT):
                ins = af(R[0][:, D * c:D * (c + 1)], x[:, c, :], ACT.Square, accum_out=small[:, 132 + c:133 + c])
            ins.then_inc(S("act_step"), 1)
            act.wait_ge(S("act_step"), 4)
            af(small[:, 134:136], small[:, 132:134], ACT.Sqrt, scale=1.0 / D, bias=col(0)).then_inc(S("ms3_ready"), 1)

        @block.vector
        def _(dve):
            V = nc.vector
            steps = [0]

            def then(ins):
                steps[0] += 1
                ins.then_inc(S("dve_step"), 1)
                dve.wait_ge(S("dve_step"), steps[0])

            def bc(ap, n, axis=2, shape=None):
                return ap.unsqueeze(axis).broadcast_to(shape)

            dve.wait_ge(S("ss_ready"), 1)
            then(V.reciprocal(rstd, rstd))
            for c in range(NT):
                V.tensor_scalar(R[10][:, D * c:D * (c + 1)], x[:, c, :], rstd[:, c:c + 1], None, ALU.mult).then_inc(S("xs_ready"), 1)
            dve.wait_ge(S("par_T"), 1)
            V.tensor_copy(par[:, 0:ROWS_A], ps[:, 6, 0:ROWS_A])
            then(V.tensor_copy(par[:, P:P + ROWS_B], ps[:, 6, P:P + ROWS_B]))
            V.tensor_scalar(omka[:, :], par[:, P_KA:P_KA + 8], -1.0, 1.0, ALU.mult, ALU.add)
            V.tensor_scalar(omm[:, :], par[:, P_MU:P_MU + 26], -1.0, 1.0, ALU.mult, ALU.add).then_inc(S("par_ready"), 1)
            dve.wait_ge(S("xT_ready"), 1)
            for k in range(KT):
                ins = V.tensor_scalar(hT[:, k, :], ps[:, k // 2, T * (k % 2):T * (k % 2 + 1)], par[:, k:k + 1], None, ALU.mult)
            ins.then_inc(S("hT_ready"), 1)

            dve.wait_ge(S("msk_in"), 16)
            V.tensor_copy(msk[:, :], scr[:, 0:(LEVELS - 1) * 2 * P]).then_inc(S("msk_read"), 1)
            dve.wait_ge(S("act_first"), 1)
            V.tensor_copy(rows[0:8, 4, :], ps[0:8, 0, 0:T]).then_inc(S("dve_free"), 1)
            dve.wait_ge(S("act_first"), 2)
            for f in range(2):
                ins = V.scalar_tensor_tensor(out=lora[:, f, 1:T], in0=ps[:, 1, T * f:T * f + T - 1], scalar=par[:, P_MU + 24 + f:P_MU + 25 + f],
                                             in1=lora[:, f, 1:T], op0=ALU.mult, op1=ALU.add)
            ins.then_inc(S("dve_free"), 1)
            with dve.Fori(0, 2) as i:
                for u in range(14):
                    j, half = u // 2, u % 2
                    b = (2 + u) % HB
                    dve.wait_ge(S("act_first"), 18 * i + (u + 3))
                    if u < 6:
                        for w in (2, 1, 0):
                            s = 3 - w
                            for f in range(2):
                                ins = V.scalar_tensor_tensor(out=R[3][:, T * f + s:T * (f + 1)], in0=ps[:, b, T * f:T * (f + 1) - s],
                                                             scalar=par[:, bass.ds(4 * i + (8 + 24 * w + 8 * j + 2 * half + f), 1)],
                                                             in1=R[3][:, T * f + s:T * (f + 1)], op0=ALU.mult, op1=ALU.add)
                            if w:
                                ins.then_inc(S("conv_step"), 1)
                                dve.wait_ge(S("conv_step"), 12 * i + (2 * u + 3 - w))
                        ins.then_inc(S("dve_free"), 1)
                        dve.wait_ge(S("act_sig"), 6 * i + (u + 1))
                        a, g = (R[3][:, 512 * n:512 * (n + 1)].rearrange("p (h c t) -> p h c t", h=2, c=2) for n in range(2))
                        if j < 2:
                            out = KQ[:, bass.ds(4 * i + 2 * half, 2), :, 1 - j, :]
                        else:
                            out = R[4][:, bass.ds(1024 * i + 512 * half, 512)].rearrange("p (h c t) -> p h c t", h=2, c=2)
                        V.tensor_tensor(out, a, g, ALU.mult).then_inc(S("conv_done"), 1)
                    elif u < 8:
                        V.tensor_tensor(R[5][:, bass.ds(1024 * i + 512 * half, 512)], ps[:, b, :], R[3][:, 1024 + 512 * half:1536 + 512 * half],
                                        ALU.mult).then_inc(S("dve_free"), 1)
                    else:
                        for f in range(2):
                            out = R[4 + j][:, bass.ds(1024 * i + T * (2 * half + f) + 1, T - 1)]
                            ins = V.scalar_tensor_tensor(out=out, in0=ps[:, b, T * f:T * (f + 1) - 1],
                                                         scalar=par[:, bass.ds(4 * i + (P_MU + 8 * (j - 4) + 2 * half + f), 1)],
                                                         in1=out, op0=ALU.mult, op1=ALU.add)
                        ins.then_inc(S("dve_free"), 1)

            dve.wait_ge(S("gate_row"), 1)
            dve.wait_ge(S("row_in"), 32)
            then(V.tensor_scalar(rows[:, 2, :], rows[:, 5, :], dtb, None, ALU.add))
            V.scalar_tensor_tensor(out=rows[:, 3, :], in0=rows[:, 2, :], scalar=-1.0, in1=rows[:, 2, :], op0=ALU.mult, op1=ALU.min).then_inc(S("gate_row"), 1)
            dve.wait_ge(S("gate_row"), 3)
            then(V.scalar_tensor_tensor(out=rows[:, 3, :], in0=rows[:, 2, :], scalar=0.0, in1=rows[:, 3, :], op0=ALU.max, op1=ALU.add))
            then(V.tensor_scalar(rows[:, 2, :], rows[:, 3, :], negA, -1.0, ALU.mult, ALU.mult))
            for c in range(NT):
                s = slice(P * c, P * (c + 1))
                ins = V.tensor_tensor_scan(rows[:, 0, s], cst[0:8, K_ONE:K_ONE + P], rows[:, 2, s], 0.0, ALU.mult, ALU.add)
            then(ins)
            for c in range(NT):
                s = slice(P * c, P * (c + 1))
                ins = V.tensor_scalar(rows[:, 3, s], rows[:, 0, s], -1.0, rows[:, 0, P * (c + 1) - 1:P * (c + 1)], ALU.mult, ALU.add)
            ins.then_inc(S("gate_row"), 1)
            for u in range(8):
                dve.wait_ge(S("gnm_read"), u + 1)
                r = scr[:, 4096 + 512 * u:4608 + 512 * u]
                then(V.reciprocal(r, r))
                v = KQ[:, 2 * (u // 2):2 * (u // 2) + 2, :, u % 2, :]
                V.tensor_tensor(v, v, r.rearrange("p (h c t) -> p h c t", h=2, c=2), ALU.mult).then_inc(S("kq_ready"), 1)
            dve.wait_ge(S("tb_ready"), 1)
            then(V.tensor_copy(small[:, 64:128], ps[:, 6, 0:64]))
            DM, DI, DS, EG = TI2[:, 0:256], TI2[:, 256:512], TI2[:, 512:768], TI2[:, 768:896]
            ct = lambda r: r.rearrange("p (c t) -> p c t", c=2)
            both = lambda m: m.unsqueeze(1).broadcast_to([P, 2, P])
            dve.wait_ge(S("vT_ready"), 4)
            for h in range(HEADS):
                b = 2 * (h % 2)
                dve.wait_ge(S("head_ready"), h + 1)
                for c in range(NT):
                    ins = V.tensor_scalar(DM[:, P * c:P * (c + 1)], ps[:, b, P * c:P * (c + 1)], tb[:, 0, c, h:h + 1], 0.0, ALU.subtract, ALU.min)
                ins.then_inc(S("gd_ready"), 1)
                dve.wait_ge(S("ge_ready"), h + 1)
                V.tensor_tensor(QDt[:, P * h:P * (h + 1)], KQ[:, h, 1, 1, :], EG, ALU.mult)
                V.tensor_tensor(ct(DS), ct(DM), both(C(K_M4)), ALU.mult)
                then(V.tensor_tensor(ct(DI), ct(DM), both(incl), ALU.mult))
                prod = ps[:, b + 1, :].rearrange("p (c w t) -> p c w t", c=2, w=2)
                V.tensor_tensor(MM[:, 2 * h:2 * h + 2, 1, :], prod[:, :, 1, :], ct(DI), ALU.mult)
                then(V.tensor_tensor(DS, ps[:, b, T:2 * T], DS, ALU.mult))
                V.tensor_tensor(MM[:, 2 * h:2 * h + 2, 0, :], prod[:, :, 0, :], ct(DS), ALU.mult).then_inc(S("head_done"), 1)

            def identities():
                then(V.tensor_copy(TT, ident.unsqueeze(1).broadcast_to([P, 16, P])))

            def inverse(v):
                dve.wait_ge(S("ti_ready"), v + 1)
                four = lambda b: ps[:, b, :].rearrange("p (u t) -> p u t", u=4)
                mask = lambda r, w: r[:, P * w:P * (w + 1)].unsqueeze(1).broadcast_to([P, 4, P])
                for g in range(4):
                    dve.wait_ge(S("t_ready"), 28 * v + g + 1)
                    V.copy_predicated(TI[:, 4 * g:4 * g + 4, :], mask(msk, 0), four(4 + 2 * (g % 2)))
                    V.copy_predicated(TT[:, 4 * g:4 * g + 4, :], mask(msk, 1), MM[:, 4 * g:4 * g + 4, 0, :]).then_inc(S("t_done"), 1)
                with dve.Fori(0, LEVELS - 2) as l:
                    dve.wait_ge(S("t_done"), 4 * l + (28 * v + 4))
                    V.tensor_copy(lvl[:, :], msk[:, bass.ds(2 * P * l + 2 * P, 2 * P)]).then_inc(S("lvl_ready"), 1)
                    dve.wait_ge(S("lvl_ready"), l + ((LEVELS - 2) * v + 1))
                    for g in range(4):
                        dve.wait_ge(S("t_ready"), 4 * l + (28 * v + g + 5))
                        dve.sem_inc(S("t_seen"), 1)
                        for w, t in enumerate((TI, TT)):
                            ins = V.copy_predicated(t[:, 4 * g:4 * g + 4, :], mask(lvl, w), four(4 + 2 * (g % 2) + w))
                        ins.then_inc(S("t_done"), 1)
                for g in range(4):
                    dve.wait_ge(S("t_ready"), 28 * v + 4 * (LEVELS - 1) + g + 1)
                    V.tensor_copy(TT[0:64, 4 * g:4 * g + 4, 64:P], ps[0:64, 4 + 2 * (g % 2), 0:T].rearrange("p (u t) -> p u t", u=4)).then_inc(S("t_done"), 1)

            identities()
            inverse(0)
            hd = lambda r, k=8: r.rearrange("p (h t) -> p h t", h=k)
            tbc = lambda w, c: tb[:, w, c, :].unsqueeze(2).broadcast_to([P, 8, P])
            two = lambda a: ps[:, a:a + 2, :].rearrange("p b (h t) -> p (b h) t", h=4)
            dve.wait_ge(S("t_done"), 28)
            dve.wait_ge(S("vT_read"), 4)
            V.tensor_tensor(hd(R[0][:, 0:1024]), hd(R[3][:, 0:1024]), tbc(1, 0), ALU.mult).then_inc(S("gx_ready"), 1)
            dve.wait_ge(S("gkd_ready"), 1)
            V.tensor_tensor(hd(R[0][:, 1024:2048]), two(2), tbc(3, 0), ALU.mult).then_inc(S("gkd_copied"), 1)
            dve.wait_ge(S("gks_ready"), 1)
            X = R[0][:, 0:1024]
            then(V.tensor_tensor(hd(X), two(6), tbc(2, 1), ALU.mult))
            then(V.tensor_tensor(X, R[3][:, 1024:2048], X, ALU.subtract))
            V.tensor_tensor(hd(X), hd(X), tbc(1, 1), ALU.mult).then_inc(S("gx_ready"), 1)
            for q in range(4):
                dve.wait_ge(S("osq_ready"), q + 1)
                V.tensor_copy(R[2][:, 512 * q:512 * (q + 1)], ps[:, (0, 1, 4, 5)[q], :]).then_inc(S("got_read"), 1)
            dve.wait_ge(S("got_read"), 4)
            dve.wait_ge(S("onm_read"), 4)
            then(V.reciprocal(R[1], R[1]))
            then(V.scalar_tensor_tensor(out=R[2], in0=R[2], scalar=par[:, P_GN:P_GN + 1], in1=R[1], op0=ALU.mult, op1=ALU.mult))
            V.tensor_tensor(R[5], R[2], R[5], ALU.mult).then_inc(S("ya_ready"), 1)

            ccv = cc.rearrange("p (m c) -> p m c", m=8)
            dsv = small[:, 48:56]
            for q in range(4):
                dve.wait_ge(S("rg_ready"), q + 1)
                ins = V.tensor_scalar(cc[:, 4 * q:4 * q + 4], ps[:, (0, 1, 4, 5)[q], P // 2 - 1::P], DECAY, None, ALU.mult)
            then(ins)
            for q in range(4):
                ins = V.scalar_tensor_tensor(out=dsv[:, 2 * q:2 * q + 2], in0=ps[:, (0, 1, 4, 5)[q], P - 1::2 * P], scalar=-DECAY,
                                             in1=ccv[:, 2 * q:2 * q + 2, 0], op0=ALU.mult, op1=ALU.add)
            then(ins)
            V.tensor_scalar(ncc, cc, -1.0, None, ALU.mult)
            V.tensor_tensor(dsc, dsv, ccv[:, :, 1], ALU.subtract).then_inc(S("rcc_ready"), 1)
            m4 = lambda r: r.rearrange("p (m c t) -> p m c t", m=8, c=2)
            dve.wait_ge(S("rsq_ready"), 1)
            dve.wait_ge(S("rnm_read"), 4)
            then(V.reciprocal(SQ, SQ))
            then(V.tensor_tensor(T1, T1, SQ, ALU.mult))
            dve.wait_ge(S("rexp_done"), 1)
            dve.wait_ge(S("ya_ready"), 1)
            then(V.tensor_tensor(AR[:, :, :, 0, :], m4(T1), Ep[:, :, :, 0:P], ALU.mult))
            V.tensor_tensor(T1, T1, AA, ALU.mult).then_inc(S("rbe_done"), 1)
            dve.wait_ge(S("rbe_done"), 1)
            V.tensor_tensor(BK[:, :, :, 0, :], m4(T1), En, ALU.mult)
            V.tensor_tensor(AR[:, :, :, 1, :], m4(R[8]), Ep[:, :, :, 1:P + 1], ALU.mult).then_inc(S("rrho_done"), 1)
            for q in range(4):
                dve.wait_ge(S("rbn_ready"), q + 1)
                ins = V.tensor_tensor(R[8][:, 512 * q:512 * (q + 1)], ps[:, (2, 3, 6, 7)[q], :], R[10][:, 512 * q:512 * (q + 1)], ALU.mult)
            ins.then_inc(S("prep_done"), 1)
            for hf in range(2):
                if hf:
                    dve.wait_ge(S("rot_ready"), 1)
                identities()
                for u in range(16):
                    dve.wait_ge(S("rm_ready"), 16 * hf + u + 1)
                    V.tensor_tensor(MM[:, u, :, :].rearrange("p w t -> p (w t)"), ps[:, u % 4, :], C(K_M4, 4 * P), ALU.mult).then_inc(S("rm_read"), 1)
                inverse(1 + hf)
                dve.wait_ge(S("rkb_ready"), hf + 1)
                V.tensor_copy(R[9][:, 1024:2048].rearrange("p (b c) -> p b c", b=2), ps[:, 2:4, :]).then_inc(S("rkb_copied"), 1)
                dve.wait_ge(S("rs_ready"), hf + 1)
                V.tensor_tensor(R[9][:, 512:768].rearrange("p (m v) -> p m v", m=4), ps[:, 4, 0:256].rearrange("p (m v) -> p m v", m=4),
                                dsc[:, 4 * hf:4 * hf + 4].unsqueeze(2).broadcast_to([P, 4, 64]), ALU.mult).then_inc(S("rs_copied"), 1)
            dve.wait_ge(S("rot_read"), 2)
            for q in range(4):
                o = R[10][:, 512 * q:512 * (q + 1)]
                dve.wait_ge(S("rmu_ready"), q + 1)
                V.scalar_tensor_tensor(out=o, in0=ps[:, 4 + q, :], scalar=-1.0 / 64, in1=o, op0=ALU.mult, op1=ALU.add).then_inc(S("rmu_read"), 1)
            dve.wait_ge(S("rmu_read"), 4)
            dve.wait_ge(S("rvr_read"), 4)
            o8 = W3[10]
            then(V.reciprocal(R[0], R[0]))
            then(V.tensor_tensor(R[10], R[10], R[0], ALU.mult))
            then(V.tensor_tensor(o8, o8, cols8(P_LNW), ALU.mult))
            then(V.tensor_tensor(o8, o8, cols8(P_LNB), ALU.add))
            then(V.tensor_tensor(R[10], R[10], R[8], ALU.add))
            for q in range(4):
                dve.wait_ge(S("gg_ready"), q + 1)
                ins = V.tensor_tensor(R[10][:, 512 * q:512 * (q + 1)], ps[:, 4 + q, :], R[10][:, 512 * q:512 * (q + 1)], ALU.mult)
            ins.then_inc(S("yb_ready"), 1)

            for u in range(8):
                g = R[6 + u // 4][:, 512 * (u % 4):512 * (u % 4 + 1)]
                dve.wait_ge(S("pj_ready"), u + 1)
                then(V.tensor_tensor(g, ps[:, u, :], g, ALU.mult))
            V.tensor_tensor(R[6], R[6], R[7], ALU.add).then_inc(S("merged"), 1)
            for n in range(2):
                for c in range(NT):
                    dve.wait_ge(S("pj_ready"), 9 + 2 * n + c)
                    o = x[:, c, 512 * n:512 * (n + 1)]
                    V.tensor_tensor(o, ps[:, 2 * n + c, :], o, ALU.add).then_inc(S("x1_ready"), 1)

            dve.wait_ge(S("ms2_ready"), 1)
            then(V.reciprocal(small[:, 130:132], small[:, 130:132]))
            for c in range(NT):
                ins = V.tensor_scalar(H2[:, c, :], x[:, c, :], small[:, 130 + c:131 + c], None, ALU.mult)
            ins.then_inc(S("h2_ready"), 1)
            dve.wait_ge(S("h2T_ready"), 1)
            for k in range(KT):
                ins = V.tensor_scalar(h2T[:, k, :], ps[:, 4 + k // 2, T * (k % 2):T * (k % 2 + 1)], par[:, P_NF + k:P_NF + k + 1], None, ALU.mult)
            ins.then_inc(S("h2T_copied"), 1)
            dve.wait_ge(S("lg_ready"), 1)
            then(V.tensor_copy(lg.rearrange("p c e -> p (c e)"), ps[:, 0, 0:2 * NE]))
            for c in range(NT):
                ins = V.max(top[:, c, :], lg[:, c, :])
            then(ins)
            V.tensor_scalar(nmx, top[:, :, 0], -1.0, None, ALU.mult).then_inc(S("top_ready"), 1)
            for c in range(NT):
                ins = V.max_index(topi[:, c, :].bitcast(U32), top[:, c, :], lg[:, c, :])
            then(ins)
            then(V.tensor_copy(topf, topi.bitcast(U32)))
            i32 = cst[:, K_IOTA:K_IOTA + NE]
            for q in range(4):
                for c in range(NT):
                    if q == 0:
                        ins = V.tensor_scalar(sel[:, c, :], i32, topf[:, c, 0:1], None, ALU.is_equal)
                    else:
                        ins = V.scalar_tensor_tensor(out=sel[:, c, :], in0=i32, scalar=topf[:, c, q:q + 1], in1=sel[:, c, :], op0=ALU.is_equal, op1=ALU.add)
                then(ins)
            dve.wait_ge(S("lgexp_ready"), 1)
            then(V.tensor_tensor(gt, tmp32, sel, ALU.mult))
            then(V.tensor_reduce(gsum, gt, AX.X, ALU.add))
            then(V.reciprocal(grec, gsum))
            V.tensor_tensor(gt, gt, grec.unsqueeze(2).broadcast_to([P, 2, NE]), ALU.mult).then_inc(S("sel_ready"), 1)
            dve.wait_ge(S("sel_ready"), 1)
            dve.wait_ge(S("pos_ready"), 1)
            tpos, tgat = (tab[:, 0:NE, 2 * w:2 * w + 2].rearrange("p e c -> p c e") for w in range(2))
            V.tensor_copy(gT, ps[0:NE, 2, 0:T])
            V.tensor_copy(tgat, gt)
            V.tensor_copy(cnt, ps[0:1, 1, 2 * NE:3 * NE])
            then(V.scalar_tensor_tensor(out=tmp32, in0=ps[:, 1, 0:2 * NE].rearrange("p (c e) -> p c e", c=2), scalar=1.0, in1=sel, op0=ALU.add, op1=ALU.mult))
            V.tensor_scalar(tpos, tmp32, -1.0, None, ALU.add)
            then(V.tensor_reduce(cmax, cnt, AX.X, ALU.max))
            V.tensor_copy(tab[:, NE:NE + 2, :], tab[:, 0:2, :]).then_inc(S("pos_read"), 1)
            then(V.tensor_scalar(cge, cst[0:1, K_COL + 8:K_COL + 16], cmax, None, ALU.is_lt))
            V.tensor_scalar(tab[:, NE:NE + 2, 0:2], tab[:, NE:NE + 2, 0:2], -float(slots), None, ALU.add)
            then(V.tensor_reduce(csum, cge, AX.X, ALU.add))
            V.tensor_copy(passes[:, :], csum).then_inc(S("passes_known"), 1)
            iot = C(K_IOTA)

            def choose():
                for q in range(2):
                    for c in range(NT):
                        s = slice(64 * q, 64 * q + 64)
                        V.tensor_scalar(Psel[:, c, s], iot[:, s], cur[:, q, c:c + 1], None, ALU.is_equal)
                        ins = V.tensor_scalar(Pgat[:, c, s], iot[:, s], cur[:, q, c:c + 1], cur[:, q, 2 + c:3 + c], ALU.is_equal, ALU.mult)
                ins.then_inc(S("sel_made"), 1)

            V.memset(PgT[:, 1, :, :].rearrange("p c t -> p (c t)"), 0.0)
            V.memset(ysb[:, 1, :], 0.0).then_inc(S("y_copied"), 1)
            then(V.tensor_copy(cur, tab[:, 0:2, :]))
            choose()
            nfeat = par[:, P_NF:P_NF + 8].unsqueeze(2).broadcast_to([P, 8, P])
            fl = lambda w: ps[:, 4:6, :].rearrange("p b (f w) -> p b f w", w=2)[:, :, :, w]
            v2 = lambda r: r.rearrange("p (b f) -> p b f", b=2)

            def take_tokens(halves_before, par_, half):
                k = slice(4 * half, 4 * half + 4)
                dve.wait_ge(S("xg_ready"), halves_before + 1)
                V.tensor_tensor(xgT[:, par_, k, :], ps[:, 7, :].rearrange("p (k s) -> p k s", k=4), nfeat[:, k, :], ALU.mult).then_inc(S("xg_copied"), 1)

            def expert(it, pair, e, par_, q):
                if q == 0:
                    dve.wait_ge(S("pt_ready"), pair + 1)
                    V.tensor_copy(PgT[:, par_, :, :].rearrange("p c t -> p (c t)"), ps[:, 7, 0:T]).then_inc(S("pt_copied"), 1)
                    V.tensor_copy(cur, tab[:, bass.ds(e + 2, 2), :]).then_inc(S("cur_ready"), 1)
                    dve.wait_ge(S("cur_ready"), pair + 1)
                    choose()
                dve.wait_ge(S("brow_used"), it + 2)
                V.tensor_scalar(v2(glu), fl(0), GLU_LIMIT, None, ALU.min).then_inc(S("glu_ready"), 1)
                V.tensor_scalar(v2(lin), fl(1), GLU_LIMIT, -GLU_LIMIT, ALU.min, ALU.max).then_inc(S("moe_step"), 1)
                dve.wait_ge(S("moe_step"), 2 * it + 1)
                V.scalar_tensor_tensor(out=lin, in0=lin, scalar=1.0, in1=glu, op0=ALU.add, op1=ALU.mult).then_inc(S("moe_step"), 1)
                dve.wait_ge(S("moe_step"), 2 * it + 2)
                dve.wait_ge(S("sig_ready"), it + 1)
                V.tensor_tensor(act_h, lin, sgm, ALU.mult).then_inc(S("h_ready"), 1)
                take_tokens(it + 2, 1 - par_, q)
                dve.wait_ge(S("at_ready"), it + 1)
                V.tensor_copy(actT.rearrange("p c s -> p (c s)"), ps[:, 6, :]).then_inc(S("at_copied"), 1)
                dve.wait_ge(S("dn_used"), 4 * it + 8)
                for n in range(2):
                    ins = V.tensor_copy(ysb[64 * q:64 * q + 64, par_, 512 * n:512 * (n + 1)], ps[64 * n:64 * n + 64, 6, :])
                ins.then_inc(S("y_copied"), 1)

            for half in range(2):
                take_tokens(half, 0, half)
            dve.wait_ge(S("passes_known"), 1)
            n = dve.value_load(passes[0:1, 0:1], min_val=1, max_val=T // slots)
            with dve.Fori(0, n) as b:
                with dve.Fori(0, NE // 4) as i:
                    for w in range(4):
                        expert(NE * b + 4 * i + w, NE // 2 * b + 2 * i + w // 2, 4 * i + w, w // 2, w % 2)
                V.tensor_scalar(tab[:, :, 0:2], tab[:, :, 0:2], -float(slots), None, ALU.add).then_inc(S("pass_done"), 1)
                dve.wait_ge(S("pass_done"), b + 1)

            dve.wait_ge(S("sum_ready"), 1)
            V.tensor_tensor(x[:, :, :].rearrange("p c d -> p (c d)"), ps[:, 0:4, :].rearrange("p b c -> p (b c)"),
                            x[:, :, :].rearrange("p c d -> p (c d)"), ALU.add).then_inc(S("x2_ready"), 1)
            dve.wait_ge(S("ms3_ready"), 1)
            dve.wait_ge(S("nf_in"), 16)
            then(V.reciprocal(small[:, 134:136], small[:, 134:136]))
            for c in range(NT):
                ins = V.scalar_tensor_tensor(out=R[1][:, D * c:D * (c + 1)], in0=x[:, c, :], scalar=small[:, 134 + c:135 + c], in1=nfb,
                                             op0=ALU.mult, op1=ALU.mult)
            ins.then_inc(S("y_ready"), 1)

        @block.gpsimd
        def _(pool):
            G = nc.gpsimd
            pool.wait_ge(S("got_ready"), 4)
            G.tensor_tensor(T1.rearrange("p (m t) -> p m t", m=8), W3[9], cols8(P_KK), ALU.mult).then_inc(S("pool_step"), 1)
            pool.wait_ge(S("pool_step"), 1)
            G.tensor_tensor(SQ, T1, T1, ALU.mult).then_inc(S("rsq_ready"), 1)
            pool.wait_ge(S("rbe_done"), 1)
            A8 = AA.rearrange("p (m t) -> p m t", m=8)
            m4 = lambda r: r.rearrange("p (m c t) -> p m c t", m=8, c=2)
            for n, ins in enumerate((lambda: G.tensor_tensor(A8, A8, cols8(P_KA), ALU.mult),
                                     lambda: G.tensor_tensor(A8, A8, omka[:, :].unsqueeze(2).broadcast_to([P, 8, T]), ALU.add),
                                     lambda: G.tensor_tensor(R[9], R[9], AA, ALU.mult))):
                ins().then_inc(S("pool_step"), 1)
                pool.wait_ge(S("pool_step"), n + 2)
            G.tensor_tensor(BK[:, :, :, 1, :], m4(R[9]), En, ALU.mult)
            pool.wait_ge(S("rrho_done"), 1)
            G.tensor_tensor(R[8], R[8], R[9], ALU.mult).then_inc(S("pool_step"), 1)
            pool.wait_ge(S("pool_step"), 5)
            G.tensor_tensor(W3[8], W3[8], cols8(P_RK), ALU.mult).then_inc(S("rrk_ready"), 1)


_NAMES = ["x", "norm_mix", "w_in", "gdn_conv", "gdn_A_log", "gdn_dt_bias", "gdn_norm", "rwkv_mu", "rwkv_w0", "rwkv_w2", "rwkv_a0",
          "rwkv_a2", "rwkv_g2", "rwkv_k_k", "rwkv_k_a", "rwkv_r_k", "rwkv_ln_w", "rwkv_ln_b", "proj_a", "proj_b", "w_out", "norm_ffn",
          "router_w", "router_b", "w_gate_up", "b_gate_up", "w_down", "b_down", "norm_final"]


def kernel(**inputs):
    import numpy as _np
    import concourse.bacc as _bacc
    from concourse import mybir as _mybir
    from concourse.bass_utils import run_bass_kernel_spmd as _run

    nc = _bacc.Bacc("TRN2", target_bir_lowering=False, num_devices=1)
    consts, masks = shape_constants()
    arrays, aps = {}, {}
    for name in _NAMES:
        arrays[f"in_{name}"] = _np.ascontiguousarray(inputs[name])
    arrays["in_consts"], arrays["in_masks"] = consts, masks
    for full, a in arrays.items():
        aps[full[3:]] = nc.dram_tensor(full, a.shape, _mybir.dt.from_np(a.dtype), kind="ExternalInput").ap()
    aps["out"] = nc.dram_tensor("out_0", (1, T, D), F32, kind="ExternalOutput").ap()
    hybrid_block(nc, aps)
    r = _run(nc, [arrays], core_ids=[0])
    return r.results[0]["out_0"]
```

```python
from contextlib import ExitStack
from math import exp

import numpy as np
import concourse.bass as bass
from concourse import mybir

F32 = mybir.dt.float32
F32R = mybir.dt.float32r
I32 = mybir.dt.int32
U32 = mybir.dt.uint32
U8 = mybir.dt.uint8
ALU = mybir.AluOpType
ACT = mybir.ActivationFunctionType
AX = mybir.AxisListType

P = 128
T = 256
NT = T // P
D = 1024
KT = D // P
HEADS = 8
NE = 32
SLOTS = 64
PANEL = 512
EPS = 1e-6
GN_EPS = 64e-5
DECAY = exp(-0.5)
GLU_ALPHA, GLU_LIMIT = 1.702, 7.0

C_Q, C_K, C_V, C_Z, C_B, C_A = 0, 1024, 2048, 3072, 4096, 4104
C_R, C_RK, C_RV, C_LORA, C_GA, C_GB = 4112, 5136, 6160, 7184, 7440, 8464

K_ID, K_ONE, K_BLK, K_INC, K_STR, K_M4, K_SEL, K_IOTA, K_COL, K_UNI, K_DUO = 0, 128, 256, 384, 512, 640, 1152, 2176, 2304, 2320, 2336
K_N = 2368
LEVELS = 7

ROWS_A = 8 + 4 * 24
PB = 128
(P_MU, P_A0, P_KK, P_KA, P_RK, P_LNW, P_LNB, P_NF, P_GN) = (PB + r for r in (0, 26, 34, 42, 50, 58, 66, 74, 82))
ROWS_B = 83


def shape_constants(slots=SLOTS):
    t = np.arange(P)
    c = np.zeros((P, K_N), np.float32)
    c[:, K_ID:K_ID + P] = np.eye(P)
    c[:, K_ONE:K_ONE + P] = 1
    c[:, K_BLK:K_BLK + P] = (t[:, None] // 64) == (t[None] // 64)
    incl = (t[:, None] <= t[None]).astype(np.float32)
    strict = (t[:, None] < t[None]).astype(np.float32)
    c[:, K_INC:K_INC + P] = incl
    c[:, K_STR:K_STR + P] = strict
    c[:, K_M4:K_M4 + 4 * P] = np.concatenate([-strict, incl, strict, incl], 1)
    for h in range(HEADS):
        c[h, K_SEL + h * P:K_SEL + (h + 1) * P] = 1
        for w in range(2):
            c[64 + 2 * h + w, K_SEL + h * P + 64 * w:K_SEL + h * P + 64 * w + 64] = 1
    c[:, K_UNI + 7] = 1
    c[:64, K_DUO + 14] = c[64:, K_DUO + 15] = 1
    j = np.arange(P) % 64
    c[:, K_IOTA:K_IOTA + P] = np.where(j < slots, j, -1000)
    c[:, K_COL:K_COL + 8] = [EPS, P * EPS, GN_EPS, 1.0, 0, 0, 0, 0]
    c[:, K_COL + 8:K_COL + 16] = [b * slots if b * slots < T else 1e9 for b in range(8)]
    m = np.zeros((P, LEVELS - 1, 2, P), np.float32)
    for lv in range(LEVELS - 1):
        b = 1 << lv
        low = ((t[:, None] // (2 * b)) == (t[None] // (2 * b))) & ((t[:, None] // b) % 2 == 1) & ((t[None] // b) % 2 == 0)
        m[:, lv, 0], m[:, lv, 1] = low, low.T
    return c, m.reshape(P, -1)


def hybrid_block(nc, A, slots=SLOTS):
    ctx = ExitStack()
    with ctx:
        def sb(name, shape, dt=F32):
            return ctx.enter_context(nc.sbuf_tensor(name, shape, dt))

        def both_types(name, shape):
            with nc.sbuf_tensor(name + "_r", shape, F32R) as rounded:
                pass
            return sb(name, shape), rounded

        sems = {}

        def S(name):
            if name not in sems:
                sems[name] = ctx.enter_context(nc.semaphore(name))
            return sems[name]

        cst = sb("cst", [P, K_N])
        msk = sb("msk", [P, (LEVELS - 1) * 2 * P], U8)
        lvl = sb("lvl", [P, 2 * P], U8)
        par = sb("par", [P, 2 * P])
        omm = sb("omm", [P, 26])
        omka = sb("omka", [P, 8])
        small = sb("small", [P, 256])
        lora = sb("lora", [P, 2, T])
        x = sb("x", [P, NT, D])
        ring, ring_r = both_types("ring", [P, 6 * 2048])
        scr, scr_r = both_types("scr", [P, 6 * 2048])
        arena, arena_r = both_types("arena", [P, 11 * 2048])
        passes = sb("passes", [1, 1], I32)
        ps = ctx.enter_context(nc.psum_tensor("ps", [P, 8, 512], F32))

        rows = scr[0:8, 10240:10240 + 6 * T].rearrange("p (w t) -> p w t", w=6)
        R = [arena[:, 2048 * r:2048 * (r + 1)] for r in range(11)]
        W3 = [r.rearrange("p (m t) -> p m t", m=8) for r in R]
        W4 = [r.rearrange("p (c m t) -> p c m t", c=2, m=8) for r in R]

        def C(k, n=P, rows_=P):
            return cst[0:rows_, k:k + n]

        ident, ones, blk = C(K_ID), C(K_ONE), C(K_BLK)
        incl, strict = C(K_INC), C(K_STR)

        def col(j):
            return cst[:, K_COL + j:K_COL + j + 1]

        def uni(h):
            return cst[:, K_UNI + 7 - h:K_UNI + 15 - h]

        def duo(m):
            return cst[:, K_DUO + 14 - 2 * m:K_DUO + 30 - 2 * m]

        def spread(m, duos=False):
            return cst[64:80, K_SEL + P * m:K_SEL + P * (m + 1)] if duos else cst[0:8, K_SEL + P * m:K_SEL + P * (m + 1)]

        def cols8(j, n=T, k=8):
            return par[:, j:j + k].unsqueeze(2).broadcast_to([P, k, n])

        panel = [ring[:, s * 4096:(s + 1) * 4096].rearrange("p (k c) -> p k c", k=KT) for s in range(3)]
        hT = W3[0]
        high = [scr_r[:, 2048 * n:2048 * (n + 1)].rearrange("p (k c) -> p k c", k=KT) for n in range(3)]
        hTh, hTl = (scr_r[:, 6144 + 2048 * n:8192 + 2048 * n].rearrange("p (k t) -> p k t", k=KT) for n in range(2))
        high2 = [arena_r[:, 2048 * r:2048 * (r + 1)].rearrange("p (k c) -> p k c", k=KT) for r in (1, 2, 9)]
        ybh, ybl, mgh, mgl = (arena_r[:, 2048 * r:2048 * (r + 1)].rearrange("p (k t) -> p k t", k=KT) for r in (3, 10, 8, 6))
        panel_r = [ring_r[:, s * 4096:(s + 1) * 4096].rearrange("p (k c) -> p k c", k=KT) for s in range(3)]
        KQ = arena[:, 2048:6144].rearrange("p (h c w t) -> p h c w t", h=8, c=2, w=2)
        AR = arena[:, 2048:6144].rearrange("p (m c w t) -> p m c w t", m=8, c=2, w=2)
        BK = arena[:, 6144:10240].rearrange("p (m c w t) -> p m c w t", m=8, c=2, w=2)
        MM = scr[:, 0:8192].rearrange("p (u w t) -> p u w t", u=16, w=4)
        TI = scr[:, 8192:10240].rearrange("p (u t) -> p u t", u=16)
        TI2 = scr[:, 8192:10240]
        GN2 = scr[0:8, 0:512]
        ON = R[1][0:8, 0:T]
        RN, RV = R[1][64:80, 0:T], R[0][64:80, 0:T]
        QDt = R[4][:, 0:1024]
        TT = scr[:, 10240:12288].rearrange("p (u t) -> p u t", u=16)
        Ep = scr[:, 0:2064].rearrange("p (m c t) -> p m c t", m=8, c=2)
        En = scr[:, 2064:4112].rearrange("p (m c t) -> p m c t", m=8, c=2)
        AA, T1, SQ = (scr[:, 4112 + 2048 * n:6160 + 2048 * n] for n in range(3))
        LS = ring[:, 4096:8192]
        lw = LS[0:65, 3072:3072 + T]

        ss, rstd = small[:, 0:2], small[:, 2:4]
        cc, ncc = small[:, 8:24], small[:, 24:40]
        dsc = small[:, 40:48]
        alog, dtb, negA = small[0:8, 56:57], small[0:8, 57:58], small[0:8, 58:59]
        tb = small[:, 64:128].rearrange("p (w c h) -> p w c h", w=4, c=2)

        w_in = A["w_in"].rearrange("l (k p) c -> p (l k) c", p=P)
        w_proj = [A[n].rearrange("l (k p) c -> p (l k) c", p=P) for n in ("proj_a", "proj_b", "w_out")]
        w_gu = A["w_gate_up"].rearrange("l e (k p) c -> p (l e k) c", p=P)
        w_dn = A["w_down"].rearrange("l e (k p) c -> p (l e k) c", p=P)
        b_gu = A["b_gate_up"].rearrange("l e c -> (l e) c")

        H2 = R[0].rearrange("p (c d) -> p c d", c=2)
        h2T = W3[1]
        rt_w = R[3][:, 0:256].rearrange("p (k e) -> p k e", k=KT)
        rt_b = R[3][0:1, 256:288]
        tab = R[2][:, 0:34 * 4].rearrange("p (e w) -> p e w", e=34)
        lg, sel, gt, tmp32 = (R[2][:, 256 + 64 * n:320 + 64 * n].rearrange("p (c e) -> p c e", c=2) for n in range(4))
        top, topi = R[2][:, 512:528].rearrange("p (c e) -> p c e", c=2), R[2][:, 528:544].rearrange("p (c e) -> p c e", c=2)
        topf = R[2][:, 544:560].rearrange("p (c e) -> p c e", c=2)
        nmx, gsum, grec = R[2][:, 560:562], R[2][:, 562:564], R[2][:, 564:566]
        cur = R[2][:, 568:576].rearrange("p (q w) -> p q w", q=2)
        cnt = R[2][0:1, 576:608]
        cmax, cge, csum = R[2][0:1, 608:609], R[2][0:1, 610:618], R[2][0:1, 618:619]
        gT = R[2][0:32, 640:896]
        nfb = R[5][:, 0:1024]
        bdn = R[4][0:32, 0:1024]
        brow = R[5][0:1, 1024:2048], R[3][0:1, 1024:2048]
        Psel = R[6][:, 0:256].rearrange("p (c s) -> p c s", c=2)
        Pgat = R[6][:, 256:512].rearrange("p (c s) -> p c s", c=2)
        PgT = R[6][:, 1024:1536].rearrange("p (q c t) -> p q c t", q=2, c=2)
        xgT = R[7].rearrange("p (q k s) -> p q k s", q=2, k=KT)
        ysb = R[10].rearrange("p (q n) -> p q n", q=2)
        glu, sgm = R[8][:, 0:512], R[8][:, 512:1024]
        lin, act_h = R[8][:, 1024:1536], R[8][:, 1536:2048]
        actT = R[9][:, 0:512].rearrange("p (c s) -> p c s", c=4)

        def gu_slot(s):
            return ring[:, s * 2048:(s + 1) * 2048] if s < 6 else scr[:, (s - 6) * 2048:(s - 5) * 2048]

        def dn_slot(s):
            return scr[:, (s + 2) * 2048:(s + 3) * 2048].rearrange("p (k c) -> p k c", k=2)

        late_slot, late_in = (2, 0, 2, 1, 0, 2), (7, 9, 8, 11, 10, 9)

        def projected(n):
            return n if n <= 8 else 2 * n - 8

        block = ctx.enter_context(nc.Block())

        first = [C_Q, C_K, C_V, C_Z, C_R, C_RK, C_RV, C_GA, C_GB]
        MM0 = 4
        HB = 6

        @block.sync
        def _(sp):
            def load(dst, src, sem):
                sp.dma_start(dst, src).then_inc(S(sem), 16)

            load(x[:, :, :], A["x"].rearrange("b (c p) d -> p (b c) d", p=P), "x_in")
            load(cst[:, :], A["consts"], "cst_in")
            load(R[7][0:8, 0:P], A["norm_mix"].rearrange("l (r c) -> (l r) c", c=P), "par_in")
            load(R[7][8:ROWS_A, 0:P], A["gdn_conv"].rearrange("l w (r c) -> (l w r) c", c=P), "par_in")
            at = 0
            for name, n in (("rwkv_mu", 26), ("rwkv_a0", 8), ("rwkv_k_k", 8), ("rwkv_k_a", 8), ("rwkv_r_k", 8),
                            ("rwkv_ln_w", 8), ("rwkv_ln_b", 8), ("norm_ffn", 8), ("gdn_norm", 1)):
                src = A[name].rearrange("l h n -> l (h n)") if name == "rwkv_r_k" else A[name]
                load(R[7][at:at + n, P:2 * P], src.rearrange("l (r c) -> (l r) c", c=P), "par_in")
                at += n
            load(panel[0][:, :, 0:256], w_in[:, :, C_LORA:C_LORA + 256], "panel_in0")
            load(panel[0][:, :, 256:272], w_in[:, :, C_B:C_B + 16], "panel_in0")
            load(scr[:, 0:(LEVELS - 1) * 2 * P], A["masks"], "msk_in")
            load(alog, A["gdn_A_log"].rearrange("l h -> h l"), "row_in")
            load(dtb, A["gdn_dt_bias"].rearrange("l h -> h l"), "row_in")
            with sp.Fori(0, 2) as i:
                for j in range(9):
                    sp.wait_ge(S("mm_ready"), 18 * i + (MM0 + 2 * j - 2))
                    load(panel[(1 + j) % 3], w_in[:, :, bass.ds(512 * i + first[j], PANEL)], f"panel_in{(1 + j) % 3}")
            sp.wait_ge(S("mm_ready"), MM0 + 2 + 2 * 16)
            load(LS[0:64, 0:1024], A["rwkv_w2"].rearrange("l r c -> (l r) c"), "panel_in1")
            load(LS[64:128, 2048:3072], A["rwkv_a2"].rearrange("l r c -> (l r) c"), "panel_in1")
            load(LS[:, 1024:2048], A["rwkv_g2"].rearrange("l r c -> (l r) c"), "panel_in1")
            load(LS[64:65, 0:1024], A["rwkv_w0"], "panel_in1")
            def gate_up(it, e, s):
                sp.wait_ge(S("gu_used"), 8 * it + (s + 1))
                load(gu_slot(s), w_gu[:, bass.ds(8 * e + s, 1), :].rearrange("p k c -> p (k c)"), f"gu_in{s}")

            def down(it, e, s):
                sp.wait_ge(S("dn_used"), 4 * it + (s + 1))
                load(dn_slot(s), w_dn[:, bass.ds(8 * e + 2 * s, 2), :], f"dn_in{s}")

            def biases(it, e):
                sp.wait_ge(S("brow_used"), it + 1)
                for n in range(2):
                    load(brow[n], b_gu[bass.ds(e, 1), 1024 * n:1024 * (n + 1)], "brow_in")

            def late_panel(q):
                load(panel[late_slot[q]], w_proj[q // 2][:, :, PANEL * (q % 2):PANEL * (q % 2 + 1)], f"panel_in{late_slot[q]}")

            for q, (sem, count) in enumerate((("mm_ready", MM0 + 36), ("mm_ready", MM0 + 38), ("pj_ready", 2), ("gg_ready", 4))):
                sp.wait_ge(S(sem), count)
                late_panel(q)
            sp.wait_ge(S("rot_ready"), 2)
            for s in (6, 7):
                gate_up(0, 0, s)
            for s in range(4):
                down(0, 0, s)
            for q in (4, 5):
                sp.wait_ge(S("pj_ready"), 2 * q - 4)
                late_panel(q)
            sp.wait_ge(S("pj_ready"), 8)
            load(rt_w, A["router_w"].rearrange("l (k p) e -> p (l k) e", p=P), "rt_in")
            load(rt_b, A["router_b"], "rt_in")
            load(bdn, A["b_down"].rearrange("l e c -> (l e) c"), "bdn_in")
            load(nfb, A["norm_final"].rearrange("(a d) -> a d", a=1).partition_broadcast(P).rearrange("p a d -> p (a d)"), "nf_in")
            biases(0, 0)
            for s, before in ((2, 8), (3, 8), (0, 12), (1, 12), (4, 16), (5, 16)):
                sp.wait_ge(S("pj_ready"), before)
                gate_up(0, 0, s)

            def expert(it, e):
                for s in range(8):
                    gate_up(it, e, s)
                biases(it, e)
                for s in range(4):
                    down(it, e, s)

            with sp.Fori(1, NE) as e:
                expert(e, e)
            sp.wait_ge(S("passes_known"), 1)
            n = sp.value_load(passes[0:1, 0:1], min_val=1, max_val=T // slots)
            with sp.If(n > 1):
                with sp.Fori(1, n) as b:
                    with sp.Fori(0, NE) as e:
                        expert(NE * b + e, e)
            for c in range(NT):
                sp.wait_ge(S("y_ready"), c + 1)
                load(A["out"].rearrange("b (c p) d -> p (b c) d", p=P)[:, c, :], R[1][:, D * c:D * (c + 1)], "out_done")
            sp.wait_ge(S("out_done"), 16 * NT)

        @block.tensor
        def _(pe):
            mm, tr = nc.tensor.matmul, nc.tensor.transpose

            for name, v in (("mm_ready", MM0), ("gu_used", 8), ("dn_used", 4), ("brow_used", 1)):
                pe.sem_inc(S(name), v)
            pe.wait_ge(S("cst_in"), 16)
            pe.wait_ge(S("par_in"), 16 * 11)
            tr(ps[:, 6, 0:ROWS_A], R[7][0:ROWS_A, 0:P], cst[0:ROWS_A, 0:ROWS_A])
            tr(ps[:, 6, P:P + ROWS_B], R[7][0:ROWS_B, P:2 * P], cst[0:ROWS_B, 0:ROWS_B]).then_inc(S("par_T"), 1)
            pe.wait_ge(S("xs_ready"), 2)
            xs = R[10].rearrange("p (c d) -> p c d", c=2)
            for k in range(KT):
                for c in range(NT):
                    ins = tr(ps[:, k // 2, 256 * (k % 2) + P * c:256 * (k % 2) + P * (c + 1)], xs[:, c, P * k:P * (k + 1)], ident)
            ins.then_inc(S("xT_ready"), 1)

            pe.wait_ge(S("hT_ready"), 1)
            pe.wait_ge(S("panel_in0"), 32)
            for f, (c0, w) in enumerate(((256, 8), (264, 8))):
                for k in range(KT):
                    ins = mm(ps[0:8, 0, T * f:T * (f + 1)], panel[0][:, k, c0:c0 + w], hT[:, k, :], start=k == 0, stop=k == KT - 1)
            ins.then_inc(S("mm_ready"), 1)
            for f in range(2):
                for k in range(KT):
                    ins = mm(ps[:, 1, T * f:T * (f + 1)], panel[0][:, k, P * f:P * (f + 1)], hT[:, k, :], start=k == 0, stop=k == KT - 1)
            ins.then_inc(S("mm_ready"), 1)
            pe.wait_ge(S("input_low"), 1)
            with pe.Fori(0, 2) as i:
                for u in range(18):
                    j, half = u // 2, u % 2
                    pe.wait_ge(S("low_ready"), 18 * i + (u + 1))
                    pe.wait_ge(S("act_first"), 18 * i + (u - 3) if u >= 4 else (13 + u) * i + 2)
                    pe.wait_ge(S("dve_free"), 14 * i + (min(u - 6, 13) + 3 if u >= 6 else min(u + 1, 2)))
                    for f in range(2):
                        for k in range(KT):
                            out = ps[:, (2 + u) % HB, T * f:T * (f + 1)]
                            wh, wl = high[u % 3][:, k, P * f:P * (f + 1)], panel_r[(1 + j) % 3][:, k, P * (2 * half + f):P * (2 * half + f + 1)]
                            mm(out, wh, hTh[:, k, :], start=k == 0, stop=False)
                            mm(out, wh, hTl[:, k, :], start=False, stop=False)
                            ins = mm(out, wl, hTh[:, k, :], start=False, stop=k == KT - 1)
                    ins.then_inc(S("mm_ready"), 1)

            pe.wait_ge(S("act_first"), 38)
            pe.wait_ge(S("dve_free"), 30)
            for u in range(8):
                pe.wait_ge(S("gsq_ready"), u + 1)
                for f in range(2):
                    h, w = 2 * (u // 2) + f, u % 2
                    ins = mm(ps[0:8, (7, 5)[w], 0:T], uni(h), scr[:, 512 * u + T * f:512 * u + T * (f + 1)],
                             start=h == 0, stop=h == HEADS - 1)
            ins.then_inc(S("norm_sums"), 1)
            pe.wait_ge(S("gate_row"), 5)
            for w in range(4):
                for c in range(NT):
                    ins = tr(ps[:, 6, 8 * (2 * w + c):8 * (2 * w + c) + 8], rows[0:8, w, P * c:P * (c + 1)], cst[0:8, 0:8])
            ins.then_inc(S("tb_ready"), 1)
            pe.wait_ge(S("conv_done"), 12)
            for w in range(4):
                for q in range(4):
                    ins = tr(ps[:, w, P * q:P * (q + 1)], W3[4][:, 4 * (w % 2) + q, P * (w // 2):P * (w // 2 + 1)], ident)
                ins.then_inc(S("vT_ready"), 1)
            pe.wait_ge(S("norm_inverse"), 1)
            for h in range(HEADS):
                if h >= 2:
                    pe.wait_ge(S("norm_used"), h - 1)
                mm(ps[:, 4 + h % 2, :], spread(h), GN2, start=True, stop=True).then_inc(S("norm_spread"), 1)
            pe.wait_ge(S("vT_read"), 4)
            pe.wait_ge(S("norm_used"), 8)
            for h in range(HEADS):
                b = 2 * (h % 4)
                if h == 3:
                    pe.wait_ge(S("gd_ready"), 1)
                if h >= 4:
                    pe.wait_ge(S("head_done"), h - 3)
                mm(ps[:, b, :], cst[0:8, K_SEL + P * h:K_SEL + P * (h + 1)], rows[0:8, 0:2, :].rearrange("h w t -> h (w t)"), start=True, stop=True)
                for c in range(NT):
                    ins = mm(ps[:, b + 1, T * c:T * (c + 1)], KQ[:, h, c, 0, :], KQ[:, h, c, :, :].rearrange("p w t -> p (w t)"), start=True, stop=True)
                ins.then_inc(S("head_ready"), 1)

            def inverse(v):
                WS = R[9] if v else R[0]
                unit = lambda r, u: r[:, P * u:P * (u + 1)]
                for g in range(4):
                    if g >= 2:
                        pe.wait_ge(S("t_done"), 28 * v + g - 1)
                    for q in range(4):
                        ins = tr(ps[:, 4 + 2 * (g % 2), P * q:P * (q + 1)], MM[:, 4 * g + q, 0, :], ident)
                    ins.then_inc(S("t_ready"), 1)
                with pe.Fori(0, LEVELS - 2) as l:
                    for g in range(4):
                        pe.wait_ge(S("t_done"), 4 * l + (28 * v + g + 1))
                        for q in range(4):
                            ins = mm(unit(ps[:, g, :], q), MM[:, 4 * g + q, 0, :], TI[:, 4 * g + q, :], start=True, stop=True)
                        ins.then_inc(S("w_ready"), 1)
                    for g in range(4):
                        pe.wait_ge(S("w_copied"), 4 * l + (24 * v + g + 1))
                        pe.wait_ge(S("t_done"), 4 * l + (28 * v + g + 3))
                        b = 4 + 2 * (g % 2)
                        for q in range(4):
                            mm(unit(ps[:, b, :], q), TT[:, 4 * g + q, :], unit(WS, 4 * g + q), start=True, stop=True)
                        for q in range(4):
                            ins = mm(unit(ps[:, b + 1, :], q), unit(WS, 4 * g + q), TT[:, 4 * g + q, :], start=True, stop=True)
                        ins.then_inc(S("t_ready"), 1)
                lo, hi = slice(0, 64), slice(64, P)
                for g in range(4):
                    pe.wait_ge(S("t_done"), 28 * v + 4 * (LEVELS - 2) + g + 1)
                    for q in range(4):
                        ins = mm(ps[hi, g, 64 * q:64 * q + 64], MM[lo, 4 * g + q, 0, hi], TI[lo, 4 * g + q, lo], start=True, stop=True)
                    ins.then_inc(S("w_ready"), 1)
                for g in range(4):
                    pe.wait_ge(S("w_copied"), 24 * v + 4 * (LEVELS - 2) + g + 1)
                    pe.wait_ge(S("t_done"), 28 * v + 4 * (LEVELS - 2) + g + 3)
                    for q in range(4):
                        ins = mm(ps[lo, 4 + 2 * (g % 2), 64 * q:64 * q + 64], unit(WS, 4 * g + q)[hi, lo], TT[hi, 4 * g + q, hi], start=True, stop=True)
                    ins.then_inc(S("t_ready"), 1)
                pe.wait_ge(S("t_done"), 28 * (v + 1))

            pe.wait_ge(S("head_done"), 8)
            inverse(0)

            X, Kd, U = R[0][:, 0:1024], R[0][:, 1024:2048], scr[:, 8192:10240]
            QD, S1 = R[4][:, 0:1024], R[4][:, 1024:2048]
            hs = lambda t, h: t[:, P * h:P * (h + 1)]
            pe.wait_ge(S("gx_ready"), 1)
            for h in range(HEADS):
                ins = mm(ps[:, h // 4, P * (h % 4):P * (h % 4 + 1)], TT[:, 2 * h, :], hs(X, h), start=True, stop=True)
            ins.then_inc(S("gsolve_ready"), 1)
            for h in range(HEADS):
                ins = tr(ps[:, 2 + h // 4, P * (h % 4):P * (h % 4 + 1)], KQ[:, h, 0, 0, :], ident)
            ins.then_inc(S("gsolve_ready"), 1)
            pe.wait_ge(S("gsolve_copied"), 1)
            pe.wait_ge(S("gkd_copied"), 1)
            for h in range(HEADS):
                ins = mm(ps[:, 4 + h // 4, P * (h % 4):P * (h % 4 + 1)], hs(Kd, h), hs(U, h), start=True, stop=True)
            ins.then_inc(S("gsolve_ready"), 1)
            pe.wait_ge(S("gsolve_copied"), 2)
            for h in range(HEADS):
                ins = mm(ps[:, 6 + h // 4, P * (h % 4):P * (h % 4 + 1)], KQ[:, h, 1, 0, :], hs(S1, h), start=True, stop=True)
            ins.then_inc(S("gsolve_ready"), 1)
            pe.wait_ge(S("gx_ready"), 2)
            for h in range(HEADS):
                ins = mm(ps[:, 2 + h // 4, P * (h % 4):P * (h % 4 + 1)], TT[:, 2 * h + 1, :], hs(X, h), start=True, stop=True)
            ins.then_inc(S("gsolve_ready"), 1)
            pe.wait_ge(S("gsolve_copied"), 3)
            for h in range(HEADS):
                b = (0, 1, 4, 5)[h // 2]
                o0, o1 = (ps[:, b, T * (h % 2) + P * c:T * (h % 2) + P * (c + 1)] for c in range(2))
                mm(o0, hs(U, h), MM[:, 2 * h, 1, :], start=True, stop=True)
                mm(o1, hs(S1, h), hs(QD, h), start=True, stop=False)
                ins = mm(o1, U[:, 1024 + P * h:1024 + P * (h + 1)], MM[:, 2 * h + 1, 1, :], start=False, stop=True)
                if h % 2:
                    ins.then_inc(S("got_ready"), 1)
            for h in range(HEADS):
                pe.wait_ge(S("osq_ready"), h // 2 + 1)
                ins = mm(ps[0:8, 2, 0:T], uni(h), R[1][:, T * h:T * (h + 1)], start=h == 0, stop=h == HEADS - 1)
            ins.then_inc(S("norm_sums"), 1)

            pe.wait_ge(S("panel_in1"), 16 * 10)
            pe.wait_ge(S("lora_act"), 1)
            pe.wait_ge(S("got_read"), 4)
            for u in range(4):
                c, n = u // 2, u % 2
                b = (0, 1, 4, 5)[u]
                mm(ps[:, b, :], lw[:, P * c:P * (c + 1)], LS[0:65, 512 * n:512 * (n + 1)], start=True, stop=True).then_inc(S("rz_ready"), 1)
            pe.wait_ge(S("norm_inverse"), 2)
            for h in range(HEADS):
                ins = mm(ps[:, (2, 3, 6, 7)[h // 2], T * (h % 2):T * (h % 2 + 1)], spread(h), ON, start=True, stop=True)
                if h % 2:
                    ins.then_inc(S("norm_spread"), 1)
            for m in range(8):
                b = (2, 3, 6, 7)[m // 2]
                pe.wait_ge(S("norm_used"), m // 2 + 9)
                ins = mm(ps[:, b, T * (m % 2):T * (m % 2 + 1)], LS[64:128, 2048 + P * m:2048 + P * (m + 1)], lora[64:128, 0, :], start=True, stop=True)
                if m % 2:
                    ins.then_inc(S("raa_ready"), 1)
            SG = R[0].rearrange("p (c d) -> p c d", c=2)
            pe.wait_ge(S("rz_read"), 4)
            for m in range(8):
                b = (0, 1, 4, 5)[m // 2]
                for c in range(NT):
                    ins = mm(ps[:, b, P * (2 * (m % 2) + c):P * (2 * (m % 2) + c + 1)], SG[:, c, P * m:P * (m + 1)], incl, start=True, stop=True)
                if m % 2:
                    ins.then_inc(S("rg_ready"), 1)
            pe.wait_ge(S("raa_read"), 8)
            pe.wait_ge(S("rsq_ready"), 1)
            for m in range(8):
                ins = mm(ps[64:80, 2, 0:T], duo(m), SQ[:, T * m:T * (m + 1)], start=m == 0, stop=m == 7)
            ins.then_inc(S("norm_sums"), 1)
            pe.wait_ge(S("norm_inverse"), 3)
            for m in range(8):
                ins = mm(ps[:, (3, 6, 7, 2)[m // 2], T * (m % 2):T * (m % 2 + 1)], spread(m, True), RN, start=True, stop=True)
                if m % 2:
                    ins.then_inc(S("norm_spread"), 1)
            pe.wait_ge(S("norm_used"), 16)
            pe.wait_ge(S("rrk_ready"), 1)
            for q in range(4):
                mm(ps[:, (2, 3, 6, 7)[q], :], blk, SQ[:, 512 * q:512 * (q + 1)], start=True, stop=True).then_inc(S("rbn_ready"), 1)

            def piece(u, bank, n):
                f = n // 2
                for k in range(4 * (n % 2), 4 * (n % 2) + 4):
                    ins = mm(ps[:, bank, T * f:T * (f + 1)], panel[late_slot[u // 2]][:, k, P * (2 * (u % 2) + f):P * (2 * (u % 2) + f + 1)],
                             W3[5][:, k, :], start=k == 0, stop=k == KT - 1)
                if n == 3:
                    ins.then_inc(S("pj_ready"), 1)

            V = R[0].rearrange("p (c d) -> p c d", c=2)
            for hf in range(2):
                pe.wait_ge(S("prep_done"), hf + 1)
                if hf:
                    pe.wait_ge(S("rot_read"), 1)
                    pe.wait_ge(S("pj_taken"), 2)
                for u in range(16):
                    m, p, c = 4 * hf + u // 4, (u // 2) % 2, u % 2
                    q = slice(64 * p, 64 * p + 64)
                    b = (0, 1, 4, 5)[u % 4]
                    if hf == 0 and u == 2:
                        pe.wait_ge(S("rexp_done"), 2)
                    if u >= 4:
                        pe.wait_ge(S("rm_read"), 16 * hf + u - 3)
                    rhs = AR[q, m, c, :, :].rearrange("p w t -> p (w t)")
                    mm(ps[:, b, 0:T], BK[q, m, c, 0, :], rhs, start=True, stop=True)
                    mm(ps[:, b, T:2 * T], BK[q, m, c, 1, :], rhs, start=True, stop=True).then_inc(S("rm_ready"), 1)
                if hf == 0:
                    pe.wait_ge(S("rbn_read"), 4)
                    for w in range(4):
                        for q in range(4):
                            ins = tr(ps[:, (6, 7, 2, 3)[w], P * q:P * (q + 1)], W3[10][:, 4 * (w % 2) + q, P * (w // 2):P * (w // 2 + 1)], ident)
                        ins.then_inc(S("rv_ready"), 1)
                    pe.wait_ge(S("rv_read"), 4)
                pe.wait_ge(S("rm_read"), 16 * (hf + 1))
                inverse(1 + hf)
                vh = lambda c, h: V[:, c, 512 * hf + 64 * h:512 * hf + 64 * h + 64]
                YS, KB = R[9][:, 0:512], R[9][:, 1024:2048]
                SS = R[9][:, 512:768]
                U0, U1 = scr[:, 8192:8704], scr[:, 8704:9216]
                if hf == 0:
                    pe.wait_ge(S("norm_used"), 12)
                    for q in range(2):
                        pe.wait_ge(S(f"panel_in{late_slot[q]}"), 16 * late_in[q])
                for h in range(8):
                    ins = mm(ps[:, 0, 64 * h:64 * h + 64], MM[:, 2 * h, 2, :], vh(0, h), start=True, stop=True)
                ins.then_inc(S("ry_ready"), 1)
                for w in range(2):
                    for m in range(4):
                        ins = tr(ps[:, 2 + w, P * m:P * (m + 1)], BK[:, 4 * hf + m, 0, w, :], ident)
                ins.then_inc(S("rkb_ready"), 1)
                piece(2 * hf, 6, 0)
                pe.wait_ge(S("ry_copied"), 2 * hf + 1)
                for h in range(8):
                    ins = mm(ps[:, 1, 64 * h:64 * h + 64], TT[:, 2 * h, :], YS[:, 64 * h:64 * h + 64], start=True, stop=True)
                ins.then_inc(S("ru_ready"), 1)
                piece(2 * hf, 6, 1)
                pe.wait_ge(S("ru_copied"), 2 * hf + 1)
                pe.wait_ge(S("rkb_copied"), hf + 1)
                for h in range(8):
                    m, p = h // 2, h % 2
                    out = ps[64 * p:64 * p + 64, 4, 64 * m:64 * m + 64]
                    mm(out, KB[:, 512 + P * m + 64 * p:512 + P * m + 64 * p + 64], vh(0, h), start=True, stop=False)
                    ins = mm(out, KB[:, P * m + 64 * p:P * m + 64 * p + 64], U0[:, 64 * h:64 * h + 64], start=False, stop=True)
                ins.then_inc(S("rs_ready"), 1)
                piece(2 * hf, 6, 2)
                pe.wait_ge(S("rs_copied"), hf + 1)
                for h in range(8):
                    m, p = h // 2, h % 2
                    q = slice(64 * p, 64 * p + 64)
                    out = ps[:, 5 + 2 * p, 64 * m:64 * m + 64]
                    mm(out, AR[q, 4 * hf + m, 1, 0, :], SS[q, 64 * m:64 * m + 64], start=True, stop=False)
                    ins = mm(out, MM[:, 2 * h + 1, 2, :], vh(1, h), start=False, stop=True)
                ins.then_inc(S("ry_ready"), 1)
                piece(2 * hf, 6, 3)
                pe.wait_ge(S("ry_copied"), 2 * hf + 2)
                for h in range(8):
                    ins = mm(ps[:, 0, 64 * h:64 * h + 64], TT[:, 2 * h + 1, :], YS[:, 64 * h:64 * h + 64], start=True, stop=True)
                ins.then_inc(S("ru_ready"), 1)
                if hf == 0:
                    for n in range(4):
                        piece(1, 1, n)
                pe.wait_ge(S("ru_copied"), 2 * hf + 2)
                for h in range(8):
                    m, p = h // 2, h % 2
                    q = slice(64 * p, 64 * p + 64)
                    o0, o1 = (ps[q, 2 + m // 2, T * (m % 2) + P * c:T * (m % 2) + P * (c + 1)] for c in range(2))
                    mm(o0, vh(0, h), MM[:, 2 * h, 3, :], start=True, stop=False)
                    mm(o0, U0[:, 64 * h:64 * h + 64], MM[:, 2 * h, 1, :], start=False, stop=True)
                    mm(o1, vh(1, h), MM[:, 2 * h + 1, 3, :], start=True, stop=False)
                    mm(o1, U1[:, 64 * h:64 * h + 64], MM[:, 2 * h + 1, 1, :], start=False, stop=False)
                    ins = mm(o1, SS[q, 64 * m:64 * m + 64], AR[q, 4 * hf + m, 1, 1, :], start=False, stop=True)
                ins.then_inc(S("rot_ready"), 1)

            pe.wait_ge(S("rot_read"), 2)
            pe.wait_ge(S("pj_taken"), 3)
            for q in range(4):
                mm(ps[:, 4 + q, :], blk, R[10][:, 512 * q:512 * (q + 1)], start=True, stop=True).then_inc(S("rmu_ready"), 1)
            pe.wait_ge(S("rmu_read"), 4)
            for m in range(8):
                ins = mm(ps[:, 4 + m // 2, T * (m % 2):T * (m % 2 + 1)], LS[:, 1024 + P * m:1024 + P * (m + 1)], lora[:, 1, :], start=True, stop=True)
                if m % 2:
                    ins.then_inc(S("gg_ready"), 1)

            def branch(u, yh, yl):
                pe.wait_ge(S("low_ready"), 32 + u + 1)
                for f in range(2):
                    for k in range(KT):
                        if u == 4 and f == 0 and k % 2 == 0:
                            pe.wait_ge(S("yb_low"), k // 2 + 1)
                        out = ps[:, u, T * f:T * (f + 1)]
                        c0 = P * (2 * (u % 2) + f)
                        wh, wl = high2[u % 3][:, k, P * f:P * (f + 1)], panel_r[late_slot[u // 2]][:, k, c0:c0 + P]
                        mm(out, wh, yh[:, k, :], start=k == 0, stop=False)
                        mm(out, wh, yl[:, k, :], start=False, stop=False)
                        ins = mm(out, wl, yh[:, k, :], start=False, stop=k == KT - 1)
                ins.then_inc(S("pj_ready"), 1)

            piece(3, 1, 0)
            piece(3, 1, 1)
            pe.wait_ge(S("gg_read"), 4)
            for m in range(8):
                pe.wait_ge(S("rvs_ready"), m // 2 + 1)
                ins = mm(ps[64:80, 4, 0:T], duo(m), R[0][:, T * m:T * (m + 1)], start=m == 0, stop=m == 7)
            ins.then_inc(S("norm_sums"), 1)
            piece(3, 1, 2)
            piece(3, 1, 3)
            pe.wait_ge(S("norm_inverse"), 4)
            for m in range(8):
                ins = mm(ps[:, 4 + m // 2, T * (m % 2):T * (m % 2 + 1)], spread(m, True), RV, start=True, stop=True)
                if m % 2:
                    ins.then_inc(S("norm_spread"), 1)
            for u in range(4, 8):
                branch(u, ybh, ybl)
            for n in range(2):
                for half in range(2):
                    hp = 8 + 2 * n + half
                    pe.wait_ge(S("low_ready"), 32 + hp + 1)
                    for c in range(NT):
                        for k in range(KT):
                            if hp == 8 and c == 0 and k % 2 == 0:
                                pe.wait_ge(S("merged_low"), k // 2 + 1)
                            out, w = ps[:, 2 * n + c, T * half:T * (half + 1)], slice(P * c, P * (c + 1))
                            wh, wl = high2[hp % 3][:, k, :], panel_r[late_slot[4 + n]][:, k, T * half:T * (half + 1)]
                            mm(out, mgh[:, k, w], wh, start=k == 0, stop=False)
                            mm(out, mgh[:, k, w], wl, start=False, stop=False)
                            ins = mm(out, mgl[:, k, w], wh, start=False, stop=k == KT - 1)
                        ins.then_inc(S("pj_ready"), 1)

            pe.wait_ge(S("h2_ready"), 1)
            for k in range(KT):
                for c in range(NT):
                    ins = tr(ps[:, 4 + k // 2, 256 * (k % 2) + P * c:256 * (k % 2) + P * (c + 1)], H2[:, c, P * k:P * (k + 1)], ident)
                if k % 2:
                    ins.then_inc(S("h2T_ready"), 1)
            pe.wait_ge(S("rt_in"), 32)
            for k in range(KT):
                pe.wait_ge(S("h2T_copied"), k // 2 + 1)
                for c in range(NT):
                    mm(ps[:, c, 0:NE], h2T[:, k, P * c:P * (c + 1)], rt_w[:, k, :], start=k == 0, stop=False)
            for c in range(NT):
                ins = mm(ps[:, c, 0:NE], cst[0:1, K_ONE:K_ONE + P], rt_b, start=False, stop=True)
            ins.then_inc(S("lg_ready"), 1)
            pe.wait_ge(S("sel_ready"), 1)
            mm(ps[:, 1, 0:NE], strict, sel[:, 0, :], start=True, stop=True)
            mm(ps[:, 1, NE:2 * NE], strict, sel[:, 1, :], start=True, stop=False)
            mm(ps[:, 1, NE:2 * NE], ones, sel[:, 0, :], start=False, stop=True)
            mm(ps[0:1, 1, 2 * NE:3 * NE], ones[:, 0:1], sel[:, 0, :], start=True, stop=False)
            mm(ps[0:1, 1, 2 * NE:3 * NE], ones[:, 0:1], sel[:, 1, :], start=False, stop=True)
            for c in range(NT):
                ins = tr(ps[0:NE, 2, P * c:P * (c + 1)], gt[:, c, :], ident)
            ins.then_inc(S("pos_ready"), 1)
            def gated_bias(bank):
                c, n = bank // 2, bank % 2
                mm(ps[:, bank, :], gT[:, P * c:P * (c + 1)], bdn[:, 512 * n:512 * (n + 1)], start=True, stop=False, skip_group_check=True)

            def scatter(par_, banks=range(4), last=False):
                for bank in banks:
                    c, n = bank // 2, bank % 2
                    ins = mm(ps[:, bank, :], PgT[:, par_, c, :], ysb[:, par_, 512 * n:512 * (n + 1)], start=False, stop=last, skip_group_check=True)
                return ins

            def gather(half):
                for k in range(4):
                    for c in range(NT):
                        kk = 4 * half + k
                        ins = mm(ps[:, 7, P * k:P * (k + 1)], H2[:, c, P * kk:P * (kk + 1)], Psel[:, c, :], start=c == 0, stop=c == NT - 1)
                ins.then_inc(S("xg_ready"), 1)

            def expert(it, pair, par_, q):
                pe.wait_ge(S("xg_copied"), it + 2 - q)
                for k in range(KT):
                    if q == 0 and k == 2:
                        for c in range(NT):
                            ins = tr(ps[:, 7, P * c:P * (c + 1)], Pgat[:, c, :], ident)
                        ins.then_inc(S("pt_ready"), 1)
                    pe.wait_ge(S(f"gu_in{k}"), 16 * it + 16)
                    for n in range(4):
                        s = slice(64 * (n % 2), 64 * (n % 2) + 64)
                        ins = mm(ps[s, 4 + n // 2, :], xgT[:, par_, k, 64 * q:64 * q + 64], gu_slot(k)[:, 512 * n:512 * (n + 1)],
                                 start=k == 0, stop=False, skip_group_check=True)
                    ins.then_inc(S("gu_used"), 1)
                pe.wait_ge(S("brow_in"), 32 * it + 32)
                for n in range(4):
                    s = slice(64 * (n % 2), 64 * (n % 2) + 64)
                    ins = mm(ps[s, 4 + n // 2, :], cst[0:1, K_ONE:K_ONE + 64], brow[n // 2][:, 512 * (n % 2):512 * (n % 2 + 1)],
                             start=False, stop=True, skip_group_check=True)
                ins.then_inc(S("brow_used"), 1)
                pe.wait_ge(S("sel_made"), pair + 2)
                pe.wait_ge(S("pt_copied") if q == 0 else S("xg_copied"), pair + 1 if q == 0 else it + 2)
                gather(q)
                pe.wait_ge(S("y_copied"), it + 1)
                scatter(1 - par_, (2 * q,))
                pe.wait_ge(S("h_ready"), it + 1)
                for j in range(4):
                    ins = tr(ps[:, 6, P * j:P * (j + 1)], act_h[:, P * j:P * (j + 1)], ident)
                ins.then_inc(S("at_ready"), 1)
                scatter(1 - par_, (2 * q + 1,))
                pe.wait_ge(S("at_copied"), it + 1)
                for kk in range(KT):
                    b, half, sub = kk // 4, (kk // 2) % 2, kk % 2
                    if kk % 2 == 0:
                        pe.wait_ge(S(f"dn_in{kk // 2}"), 16 * it + 16)
                    for n in range(2):
                        ins = mm(ps[64 * n:64 * n + 64, 6, :], actT[:, 2 * b + sub, 64 * half:64 * half + 64],
                                 dn_slot(kk // 2)[:, kk % 2, 512 * n:512 * (n + 1)], start=kk == 0, stop=kk == KT - 1, skip_group_check=True)
                    if kk % 2:
                        ins.then_inc(S("dn_used"), 1)

            pe.wait_ge(S("sel_made"), 1)
            gather(0)
            pe.wait_ge(S("pos_read"), 1)
            pe.wait_ge(S("bdn_in"), 16)
            gated_bias(0)
            pe.wait_ge(S("xg_copied"), 1)
            gather(1)
            for bank in range(1, 4):
                gated_bias(bank)
            pe.wait_ge(S("passes_known"), 1)
            n = pe.value_load(passes[0:1, 0:1], min_val=1, max_val=T // slots)
            with pe.Fori(0, n) as b:
                with pe.Fori(0, NE // 4) as i:
                    for w in range(4):
                        expert(NE * b + 4 * i + w, NE // 2 * b + 2 * i + w // 2, w // 2, w % 2)
            pe.wait_ge(S("y_copied"), NE * n + 1)
            for c in range(NT):
                scatter(1, (2 * c, 2 * c + 1), last=True).then_inc(S("sum_ready"), 1)

        @block.scalar
        def _(act):
            af = nc.scalar.activation

            act.wait_ge(S("x_in"), 16)
            for c in range(NT):
                ins = af(R[9][:, D * c:D * (c + 1)], x[:, c, :], ACT.Square, accum_out=ss[:, c:c + 1])
            ins.then_inc(S("act_step"), 1)
            act.wait_ge(S("act_step"), 1)
            act.wait_ge(S("cst_in"), 16)
            af(rstd, ss, ACT.Sqrt, scale=1.0 / D, bias=col(0)).then_inc(S("ss_ready"), 1)

            act.wait_ge(S("hT_ready"), 1)
            af(hTh, hT, ACT.Copy).then_inc(S("input_high"), 1)

            act.wait_ge(S("msk_read"), 1)

            def take_high(i, u):
                j, half = u // 2, u % 2
                if half == 0:
                    act.wait_ge(S(f"panel_in{(1 + j) % 3}"), 48 * i + 16 * (j // 3 + (3 if (1 + j) % 3 == 0 else 1)))
                act.wait_ge(S("mm_ready"), 18 * i + (MM0 + u))
                af(high[u % 3], panel[(1 + j) % 3][:, :, 256 * half:256 * half + 256], ACT.Copy).then_inc(S("high_ready"), 1)

            take_high(0, 0)
            act.wait_ge(S("mm_ready"), MM0 + 1)
            af(rows[0:8, 5, :], ps[0:8, 0, T:2 * T], ACT.Copy).then_inc(S("act_first"), 1)
            take_high(0, 1)
            act.wait_ge(S("mm_ready"), MM0 + 2)
            act.wait_ge(S("par_ready"), 1)
            af(lora[:, 0, :], ps[:, 1, 0:T], ACT.Copy, scale=omm[:, 24:25])
            af(lora[:, 1, :], ps[:, 1, T:2 * T], ACT.Copy, scale=omm[:, 25:26]).then_inc(S("act_first"), 1)
            take_high(0, 2)
            act.wait_ge(S("dve_free"), 1)
            af(rows[:, 1, :], rows[:, 4, :], ACT.Sigmoid).then_inc(S("gate_row"), 1)
            act.wait_ge(S("row_in"), 32)
            act.wait_ge(S("gate_row"), 2)
            af(negA, alog, ACT.Exp)
            af(rows[:, 3, :], rows[:, 3, :], ACT.Exp).then_inc(S("act_step"), 1)
            act.wait_ge(S("act_step"), 2)
            af(rows[:, 3, :], rows[:, 3, :], ACT.Ln, bias=cst[0:8, K_COL + 3:K_COL + 4]).then_inc(S("gate_row"), 1)
            act.wait_ge(S("gate_row"), 4)
            af(rows[:, 2, :], rows[:, 0, :], ACT.Exp)
            af(rows[:, 3, :], rows[:, 3, :], ACT.Exp).then_inc(S("gate_row"), 1)
            with act.Fori(0, 2) as i:
                for u in range(18):
                    j, half = u // 2, u % 2
                    b = (2 + u) % HB
                    act.wait_ge(S("mm_ready"), 18 * i + (MM0 + 3 + u))
                    if u < 6:
                        at = 1024 * (u % 2)
                        if u == 1:
                            act.wait_ge(S("dve_free"), 14 * i + 2)
                        elif u:
                            act.wait_ge(S("conv_done"), 6 * i + (u - 1))
                        for f in range(2):
                            ins = af(R[3][:, at + T * f:at + T * (f + 1)], ps[:, b, T * f:T * (f + 1)], ACT.Copy,
                                     scale=par[:, bass.ds(4 * i + (8 + 24 * 3 + 8 * j + 2 * half + f), 1)])
                        ins.then_inc(S("act_first"), 1)
                        take_high(i, u + 3)
                        act.wait_ge(S("dve_free"), 14 * i + (u + 3))
                        af(R[3][:, at + 512:at + 1024], R[3][:, at:at + 512], ACT.Sigmoid).then_inc(S("act_sig"), 1)
                    elif u < 8:
                        if u == 6:
                            act.wait_ge(S("conv_done"), 6 * i + 6)
                        af(R[3][:, 1024 + 512 * half:1536 + 512 * half], ps[:, b, :], ACT.Sigmoid).then_inc(S("act_first"), 1)
                    elif u < 14:
                        for f in range(2):
                            t = 8 * (j - 4) + 2 * half + f
                            ins = af(R[4 + j][:, bass.ds(1024 * i + T * (2 * half + f), T)], ps[:, b, T * f:T * (f + 1)], ACT.Copy,
                                     scale=omm[:, bass.ds(4 * i + t, 1)])
                        ins.then_inc(S("act_first"), 1)
                    else:
                        af(R[6 + (j - 7)][:, bass.ds(1024 * i + 512 * half, 512)], ps[:, b, :], ACT.Sigmoid).then_inc(S("act_first"), 1)
                    if 6 <= u < 15:
                        take_high(i, u + 3)
                    elif u >= 15:
                        with act.If(i < 1):
                            take_high(i + 1, u - 15)

            act.wait_ge(S("dve_free"), 2)
            af(lw[64:65, :].rearrange("p (c t) -> p c t", c=2), cst[64:65, K_ONE:K_ONE + P].unsqueeze(1).broadcast_to([1, 2, P]), ACT.Copy)
            af(lw[0:64, :], lora[0:64, 0, :], ACT.Tanh)
            af(lora[:, 1, :], lora[:, 1, :], ACT.Sigmoid).then_inc(S("lora_act"), 1)
            act.wait_ge(S("conv_done"), 12)
            for u in range(8):
                af(scr[:, 512 * u:512 * (u + 1)].rearrange("p (h c t) -> p h c t", h=2, c=2), KQ[:, 2 * (u // 2):2 * (u // 2) + 2, :, u % 2, :],
                   ACT.Square).then_inc(S("gsq_ready"), 1)
            act.wait_ge(S("norm_sums"), 1)
            af(GN2[:, 0:T], ps[0:8, 7, 0:T], ACT.Sqrt, bias=cst[0:8, K_COL:K_COL + 1])
            af(GN2[:, T:2 * T], ps[0:8, 5, 0:T], ACT.Sqrt, scale=float(P), bias=cst[0:8, K_COL + 1:K_COL + 2]).then_inc(S("norm_roots"), 1)
            for w in range(4):
                act.wait_ge(S("vT_ready"), w + 1)
                af(R[3][:, 1024 * (w // 2) + 512 * (w % 2):1024 * (w // 2) + 512 * (w % 2) + 512], ps[:, w, :], ACT.Copy).then_inc(S("vT_read"), 1)
            for h in range(HEADS):
                o = 1024 * (h % 2)
                DM, EG = TI2[:, o:o + 256], TI2[:, o + 768:o + 896]
                act.wait_ge(S("gd_ready"), h + 1)
                af(DM, DM, ACT.Exp)
                af(EG, ps[:, 2 * (h % 4), P:2 * P], ACT.Exp).then_inc(S("ge_ready"), 1)

            def identities(v):
                act.wait_ge(*[(S("head_done"), 8), (S("prep_done"), 2), (S("rot_ready"), 1)][v])
                if v == 1:
                    act.wait_ge(S("rbn_ready"), 4)
                af(TI, ident.unsqueeze(1).broadcast_to([P, 16, P]), ACT.Copy).then_inc(S("ti_ready"), 1)

            def inverse(v):
                WS = R[9] if v else R[0]
                with act.Fori(0, LEVELS - 2) as l:
                    for g in range(4):
                        act.wait_ge(S("w_ready"), 4 * l + (24 * v + g + 1))
                        af(WS[:, 512 * g:512 * (g + 1)], ps[:, g, :], ACT.Copy).then_inc(S("w_copied"), 1)
                for g in range(4):
                    act.wait_ge(S("w_ready"), 24 * v + 4 * (LEVELS - 2) + g + 1)
                    af(WS[64:P, 512 * g:512 * (g + 1)].rearrange("p (u t) -> p u t", u=4)[:, :, 0:64],
                       ps[64:P, g, 0:T].rearrange("p (u t) -> p u t", u=4), ACT.Copy).then_inc(S("w_copied"), 1)

            identities(0)
            inverse(0)
            U = scr[:, 8192:10240]
            two = lambda r: r.rearrange("p (b c) -> p b c", b=2)
            act.wait_ge(S("gsolve_ready"), 1)
            af(two(U[:, 0:1024]), ps[:, 0:2, :], ACT.Copy).then_inc(S("gsolve_copied"), 1)
            act.wait_ge(S("gsolve_ready"), 3)
            af(two(R[4][:, 1024:2048]), ps[:, 4:6, :], ACT.Copy).then_inc(S("gsolve_copied"), 1)
            act.wait_ge(S("gsolve_ready"), 5)
            af(two(U[:, 1024:2048]), ps[:, 2:4, :], ACT.Copy).then_inc(S("gsolve_copied"), 1)
            for q in range(4):
                act.wait_ge(S("got_ready"), q + 1)
                af(R[1][:, 512 * q:512 * (q + 1)], ps[:, (0, 1, 4, 5)[q], :], ACT.Square).then_inc(S("osq_ready"), 1)
            act.wait_ge(S("norm_sums"), 2)
            af(ON, ps[0:8, 2, 0:T], ACT.Sqrt, scale=1.0 / P, bias=cst[0:8, K_COL:K_COL + 1]).then_inc(S("norm_roots"), 1)

            for u in range(4):
                act.wait_ge(S("rz_ready"), u + 1)
                af(R[0][:, 512 * u:512 * (u + 1)], ps[:, (0, 1, 4, 5)[u], :], ACT.Sigmoid).then_inc(S("rz_read"), 1)
            for m in range(8):
                act.wait_ge(S("raa_ready"), m // 2 + 1)
                af(AA[:, T * m:T * (m + 1)], ps[:, (2, 3, 6, 7)[m // 2], T * (m % 2):T * (m % 2 + 1)], ACT.Sigmoid,
                   bias=par[:, P_A0 + m:P_A0 + m + 1]).then_inc(S("raa_read"), 1)
            act.wait_ge(S("norm_sums"), 3)
            af(RN, ps[64:80, 2, 0:T], ACT.Sqrt, bias=cst[64:80, K_COL:K_COL + 1]).then_inc(S("norm_roots"), 1)
            act.wait_ge(S("rcc_ready"), 1)
            af(Ep[:, :, :, 0], cc.rearrange("p (m c) -> p m c", m=8), ACT.Exp)
            af(dsc, dsc, ACT.Exp)
            for m in range(8):
                for c in range(NT):
                    src = ps[:, (0, 1, 4, 5)[m // 2], P * (2 * (m % 2) + c):P * (2 * (m % 2) + c + 1)]
                    af(Ep[:, m, c, 1:P + 1], src, ACT.Exp, scale=-DECAY, bias=cc[:, 2 * m + c:2 * m + c + 1])
                    ins = af(En[:, m, c, :], src, ACT.Exp, scale=DECAY, bias=ncc[:, 2 * m + c:2 * m + c + 1])
                if m % 4 == 3:
                    ins.then_inc(S("rexp_done"), 1)
            for hf in range(2):
                identities(1 + hf)
                if hf == 0:
                    for w in range(4):
                        act.wait_ge(S("rv_ready"), w + 1)
                        af(R[0][:, 1024 * (w // 2) + 512 * (w % 2):1024 * (w // 2) + 512 * (w % 2) + 512], ps[:, (6, 7, 2, 3)[w], :], ACT.Copy).then_inc(S("rv_read"), 1)
                inverse(1 + hf)
                for c in range(NT):
                    act.wait_ge(S("ry_ready"), 2 * hf + c + 1)
                    if c == 0:
                        af(R[9][:, 0:512], ps[:, 0, :], ACT.Copy).then_inc(S("ry_copied"), 1)
                    else:
                        pair = R[9][:, 0:512].rearrange("p (m w v) -> p m w v", m=4, w=2)
                        for w in range(2):
                            ins = af(pair[:, :, w, :], ps[:, 5 + 2 * w, 0:256].rearrange("p (m v) -> p m v", m=4), ACT.Copy)
                        ins.then_inc(S("ry_copied"), 1)
                    act.wait_ge(S("ru_ready"), 2 * hf + c + 1)
                    af(scr[:, 8192 + 512 * c:8704 + 512 * c], ps[:, (1, 0)[c], :], ACT.Copy, scale=-1.0).then_inc(S("ru_copied"), 1)
                act.wait_ge(S("rot_ready"), hf + 1)
                af(two(R[10][:, 1024 * hf:1024 * (hf + 1)]), ps[:, 2:4, :], ACT.Copy).then_inc(S("rot_read"), 1)

            def take_high2(hp):
                q, half = hp // 2, hp % 2
                if half == 0:
                    act.wait_ge(S(f"panel_in{late_slot[q]}"), 16 * late_in[q])
                if hp >= 7:
                    act.wait_ge(S("pj_ready"), projected(hp - 2))
                af(high2[hp % 3], panel[late_slot[q]][:, :, T * half:T * (half + 1)], ACT.Copy).then_inc(S("high_ready"), 1)

            for q in range(4):
                act.wait_ge(S("rmu_read"), q + 1)
                af(R[0][:, 512 * q:512 * (q + 1)], R[10][:, 512 * q:512 * (q + 1)], ACT.Square).then_inc(S("rvs_ready"), 1)
            take_high2(4)
            act.wait_ge(S("norm_sums"), 4)
            af(RV, ps[64:80, 4, 0:T], ACT.Sqrt, scale=1.0 / 64, bias=cst[64:80, K_COL + 2:K_COL + 3]).then_inc(S("norm_roots"), 1)
            take_high2(5)
            for q in range(4):
                act.wait_ge(S("yb_ready"), q + 1)
                af(ybh[:, 2 * q:2 * q + 2, :], W3[10][:, 2 * q:2 * q + 2, :], ACT.Copy).then_inc(S("input_high"), 1)
            for hp in range(6, 8):
                take_high2(hp)
            for q in range(4):
                act.wait_ge(S("merged"), q + 1)
                af(mgh[:, 2 * q:2 * q + 2, :], W3[6][:, 2 * q:2 * q + 2, :], ACT.Copy).then_inc(S("merged_high"), 1)
                if q < 3:
                    take_high2(8 + q)
            take_high2(11)

            act.wait_ge(S("x1_ready"), 4)
            for c in range(NT):
                ins = af(R[1][:, D * c:D * (c + 1)], x[:, c, :], ACT.Square, accum_out=small[:, 128 + c:129 + c])
            ins.then_inc(S("act_step"), 1)
            act.wait_ge(S("act_step"), 3)
            af(small[:, 130:132], small[:, 128:130], ACT.Sqrt, scale=1.0 / D, bias=col(0)).then_inc(S("roots_ready"), 1)
            act.wait_ge(S("top_ready"), 1)
            for c in range(NT):
                ins = af(tmp32[:, c, :], lg[:, c, :], ACT.Exp, bias=nmx[:, c:c + 1])
            ins.then_inc(S("lgexp_ready"), 1)

            def expert(it):
                act.wait_ge(S("glu_ready"), it + 1)
                af(sgm, glu, ACT.Sigmoid, scale=GLU_ALPHA).then_inc(S("sig_ready"), 1)

            act.wait_ge(S("passes_known"), 1)
            n = act.value_load(passes[0:1, 0:1], min_val=1, max_val=T // slots)
            with act.Fori(0, n) as b:
                with act.Fori(0, NE) as e:
                    expert(NE * b + e)
            for c in range(NT):
                act.wait_ge(S("x2_ready"), c + 1)
                af(R[0][:, D * c:D * (c + 1)], x[:, c, :], ACT.Square, accum_out=small[:, 132 + c:133 + c]).then_inc(S("act_step"), 1)
                act.wait_ge(S("act_step"), 4 + c)
                af(small[:, 134 + c:135 + c], small[:, 132 + c:133 + c], ACT.Sqrt, scale=1.0 / D, bias=col(0)).then_inc(S("roots_ready"), 1)

        @block.vector
        def _(dve):
            V = nc.vector
            steps = [0]

            def then(ins):
                steps[0] += 1
                ins.then_inc(S("dve_step"), 1)
                dve.wait_ge(S("dve_step"), steps[0])

            def bc(ap, n, axis=2, shape=None):
                return ap.unsqueeze(axis).broadcast_to(shape)

            dve.wait_ge(S("ss_ready"), 1)
            then(V.reciprocal(rstd, rstd))
            for c in range(NT):
                V.tensor_scalar(R[10][:, D * c:D * (c + 1)], x[:, c, :], rstd[:, c:c + 1], None, ALU.mult).then_inc(S("xs_ready"), 1)
            dve.wait_ge(S("par_T"), 1)
            V.tensor_copy(par[:, 0:ROWS_A], ps[:, 6, 0:ROWS_A])
            then(V.tensor_copy(par[:, P:P + ROWS_B], ps[:, 6, P:P + ROWS_B]))
            V.tensor_scalar(omka[:, :], par[:, P_KA:P_KA + 8], -1.0, 1.0, ALU.mult, ALU.add)
            V.tensor_scalar(omm[:, :], par[:, P_MU:P_MU + 26], -1.0, 1.0, ALU.mult, ALU.add).then_inc(S("par_ready"), 1)
            dve.wait_ge(S("xT_ready"), 1)
            for k in range(KT):
                ins = V.tensor_scalar(hT[:, k, :], ps[:, k // 2, T * (k % 2):T * (k % 2 + 1)], par[:, k:k + 1], None, ALU.mult)
            ins.then_inc(S("hT_ready"), 1)

            dve.wait_ge(S("msk_in"), 16)
            V.tensor_copy(msk[:, :], scr[:, 0:(LEVELS - 1) * 2 * P]).then_inc(S("msk_read"), 1)
            dve.wait_ge(S("act_first"), 1)
            V.tensor_copy(rows[0:8, 4, :], ps[0:8, 0, 0:T]).then_inc(S("dve_free"), 1)
            dve.wait_ge(S("act_first"), 2)
            for f in range(2):
                ins = V.scalar_tensor_tensor(out=lora[:, f, 1:T], in0=ps[:, 1, T * f:T * f + T - 1], scalar=par[:, P_MU + 24 + f:P_MU + 25 + f],
                                             in1=lora[:, f, 1:T], op0=ALU.mult, op1=ALU.add)
            ins.then_inc(S("dve_free"), 1)
            dve.wait_ge(S("gate_row"), 1)
            dve.wait_ge(S("row_in"), 32)
            then(V.tensor_scalar(rows[:, 2, :], rows[:, 5, :], dtb, None, ALU.add))
            V.scalar_tensor_tensor(out=rows[:, 3, :], in0=rows[:, 2, :], scalar=-1.0, in1=rows[:, 2, :], op0=ALU.mult, op1=ALU.min).then_inc(S("gate_row"), 1)
            dve.wait_ge(S("gate_row"), 3)
            then(V.scalar_tensor_tensor(out=rows[:, 3, :], in0=rows[:, 2, :], scalar=0.0, in1=rows[:, 3, :], op0=ALU.max, op1=ALU.add))
            then(V.tensor_scalar(rows[:, 2, :], rows[:, 3, :], negA, -1.0, ALU.mult, ALU.mult))
            for c in range(NT):
                s = slice(P * c, P * (c + 1))
                ins = V.tensor_tensor_scan(rows[:, 0, s], cst[0:8, K_ONE:K_ONE + P], rows[:, 2, s], 0.0, ALU.mult, ALU.add)
            then(ins)
            for c in range(NT):
                s = slice(P * c, P * (c + 1))
                ins = V.tensor_scalar(rows[:, 3, s], rows[:, 0, s], -1.0, rows[:, 0, P * (c + 1) - 1:P * (c + 1)], ALU.mult, ALU.add)
            ins.then_inc(S("gate_row"), 1)
            with dve.Fori(0, 2) as i:
                for u in range(14):
                    j, half = u // 2, u % 2
                    b = (2 + u) % HB
                    dve.wait_ge(S("act_first"), 18 * i + (u + 3))
                    if u < 6:
                        at = 1024 * (u % 2)
                        for w in (2, 1, 0):
                            s = 3 - w
                            for f in range(2):
                                ins = V.scalar_tensor_tensor(out=R[3][:, at + T * f + s:at + T * (f + 1)], in0=ps[:, b, T * f:T * (f + 1) - s],
                                                             scalar=par[:, bass.ds(4 * i + (8 + 24 * w + 8 * j + 2 * half + f), 1)],
                                                             in1=R[3][:, at + T * f + s:at + T * (f + 1)], op0=ALU.mult, op1=ALU.add)
                            if w:
                                ins.then_inc(S("conv_step"), 1)
                                dve.wait_ge(S("conv_step"), 12 * i + (2 * u + 3 - w))
                        ins.then_inc(S("dve_free"), 1)
                        dve.wait_ge(S("act_sig"), 6 * i + (u + 1))
                        a, g = (R[3][:, at + 512 * n:at + 512 * (n + 1)].rearrange("p (h c t) -> p h c t", h=2, c=2) for n in range(2))
                        if j < 2:
                            out = KQ[:, bass.ds(4 * i + 2 * half, 2), :, 1 - j, :]
                        else:
                            out = R[4][:, bass.ds(1024 * i + 512 * half, 512)].rearrange("p (h c t) -> p h c t", h=2, c=2)
                        V.tensor_tensor(out, a, g, ALU.mult).then_inc(S("conv_done"), 1)
                    elif u < 8:
                        V.tensor_tensor(R[5][:, bass.ds(1024 * i + 512 * half, 512)], ps[:, b, :], R[3][:, 1024 + 512 * half:1536 + 512 * half],
                                        ALU.mult).then_inc(S("dve_free"), 1)
                    else:
                        for f in range(2):
                            out = R[4 + j][:, bass.ds(1024 * i + T * (2 * half + f) + 1, T - 1)]
                            ins = V.scalar_tensor_tensor(out=out, in0=ps[:, b, T * f:T * (f + 1) - 1],
                                                         scalar=par[:, bass.ds(4 * i + (P_MU + 8 * (j - 4) + 2 * half + f), 1)],
                                                         in1=out, op0=ALU.mult, op1=ALU.add)
                        ins.then_inc(S("dve_free"), 1)

            dve.wait_ge(S("norm_roots"), 1)
            V.reciprocal(GN2, GN2).then_inc(S("norm_inverse"), 1)
            for h in range(HEADS):
                dve.wait_ge(S("norm_spread"), h + 1)
                v = KQ[:, h, :, :, :].rearrange("p c w t -> p w c t")
                V.tensor_tensor(v, v, ps[:, 4 + h % 2, :].rearrange("p (w c t) -> p w c t", w=2, c=2), ALU.mult).then_inc(S("norm_used"), 1)
            dve.wait_ge(S("tb_ready"), 1)
            then(V.tensor_copy(small[:, 64:128], ps[:, 6, 0:64]))
            ct = lambda r: r.rearrange("p (c t) -> p c t", c=2)
            both = lambda m: m.unsqueeze(1).broadcast_to([P, 2, P])
            work = lambda h: [TI2[:, 1024 * (h % 2) + a:1024 * (h % 2) + b] for a, b in ((0, 256), (256, 512), (512, 768), (768, 896))]
            dve.wait_ge(S("vT_ready"), 4)

            def differences(h):
                dve.wait_ge(S("head_ready"), h + 1)
                for c in range(NT):
                    ins = V.tensor_scalar(work(h)[0][:, P * c:P * (c + 1)], ps[:, 2 * (h % 4), P * c:P * (c + 1)], tb[:, 0, c, h:h + 1], 0.0, ALU.subtract, ALU.min)
                ins.then_inc(S("gd_ready"), 1)

            differences(0)
            for h in range(HEADS):
                b = 2 * (h % 4)
                DM, DI, DS, EG = work(h)
                if h < HEADS - 1:
                    differences(h + 1)
                dve.wait_ge(S("ge_ready"), h + 1)
                V.tensor_tensor(QDt[:, P * h:P * (h + 1)], KQ[:, h, 1, 1, :], EG, ALU.mult)
                V.tensor_tensor(ct(DS), ct(DM), both(C(K_M4)), ALU.mult)
                then(V.tensor_tensor(ct(DI), ct(DM), both(incl), ALU.mult))
                prod = ps[:, b + 1, :].rearrange("p (c w t) -> p c w t", c=2, w=2)
                V.tensor_tensor(MM[:, 2 * h:2 * h + 2, 1, :], prod[:, :, 1, :], ct(DI), ALU.mult)
                then(V.tensor_tensor(DS, ps[:, b, T:2 * T], DS, ALU.mult))
                V.tensor_tensor(MM[:, 2 * h:2 * h + 2, 0, :], prod[:, :, 0, :], ct(DS), ALU.mult).then_inc(S("head_done"), 1)

            def inverse(v):
                dve.wait_ge(S("ti_ready"), v + 1)
                if v:
                    dve.wait_ge(S("tt_ready"), v)
                four = lambda b: ps[:, b, :].rearrange("p (u t) -> p u t", u=4)
                mask = lambda r, w: r[:, P * w:P * (w + 1)].unsqueeze(1).broadcast_to([P, 4, P])
                for g in range(4):
                    dve.wait_ge(S("t_ready"), 28 * v + g + 1)
                    V.copy_predicated(TI[:, 4 * g:4 * g + 4, :], mask(msk, 0), four(4 + 2 * (g % 2)))
                    V.copy_predicated(TT[:, 4 * g:4 * g + 4, :], mask(msk, 1), MM[:, 4 * g:4 * g + 4, 0, :]).then_inc(S("t_done"), 1)
                with dve.Fori(0, LEVELS - 2) as l:
                    dve.wait_ge(S("t_done"), 4 * l + (28 * v + 4))
                    V.tensor_copy(lvl[:, :], msk[:, bass.ds(2 * P * l + 2 * P, 2 * P)]).then_inc(S("lvl_ready"), 1)
                    dve.wait_ge(S("lvl_ready"), l + ((LEVELS - 2) * v + 1))
                    for g in range(4):
                        dve.wait_ge(S("t_ready"), 4 * l + (28 * v + g + 5))
                        dve.sem_inc(S("t_seen"), 1)
                        for w, t in enumerate((TI, TT)):
                            ins = V.copy_predicated(t[:, 4 * g:4 * g + 4, :], mask(lvl, w), four(4 + 2 * (g % 2) + w))
                        ins.then_inc(S("t_done"), 1)
                for g in range(4):
                    dve.wait_ge(S("t_ready"), 28 * v + 4 * (LEVELS - 1) + g + 1)
                    V.tensor_copy(TT[0:64, 4 * g:4 * g + 4, 64:P], ps[0:64, 4 + 2 * (g % 2), 0:T].rearrange("p (u t) -> p u t", u=4)).then_inc(S("t_done"), 1)

            then(V.tensor_copy(TT, ident.unsqueeze(1).broadcast_to([P, 16, P])))
            inverse(0)
            hd = lambda r, k=8: r.rearrange("p (h t) -> p h t", h=k)
            tbc = lambda w, c: tb[:, w, c, :].unsqueeze(2).broadcast_to([P, 8, P])
            two = lambda a: ps[:, a:a + 2, :].rearrange("p b (h t) -> p (b h) t", h=4)
            dve.wait_ge(S("t_done"), 28)
            dve.wait_ge(S("vT_read"), 4)
            V.tensor_tensor(hd(R[0][:, 0:1024]), hd(R[3][:, 0:1024]), tbc(1, 0), ALU.mult).then_inc(S("gx_ready"), 1)
            dve.wait_ge(S("gsolve_ready"), 2)
            V.tensor_tensor(hd(R[0][:, 1024:2048]), two(2), tbc(3, 0), ALU.mult).then_inc(S("gkd_copied"), 1)
            dve.wait_ge(S("gsolve_ready"), 4)
            X = R[0][:, 0:1024]
            then(V.tensor_tensor(hd(X), two(6), tbc(2, 1), ALU.mult))
            then(V.tensor_tensor(X, R[3][:, 1024:2048], X, ALU.subtract))
            V.tensor_tensor(hd(X), hd(X), tbc(1, 1), ALU.mult).then_inc(S("gx_ready"), 1)
            for q in range(4):
                dve.wait_ge(S("osq_ready"), q + 1)
                V.tensor_copy(R[2][:, 512 * q:512 * (q + 1)], ps[:, (0, 1, 4, 5)[q], :]).then_inc(S("got_read"), 1)
            dve.wait_ge(S("got_read"), 4)
            dve.wait_ge(S("norm_roots"), 2)
            V.reciprocal(ON, ON).then_inc(S("norm_inverse"), 1)
            then(V.scalar_tensor_tensor(out=R[5], in0=R[2], scalar=par[:, P_GN:P_GN + 1], in1=R[5], op0=ALU.mult, op1=ALU.mult))
            for q in range(4):
                o = R[5][:, 512 * q:512 * (q + 1)]
                dve.wait_ge(S("norm_spread"), q + 9)
                V.tensor_tensor(o, ps[:, (2, 3, 6, 7)[q], :], o, ALU.mult).then_inc(S("norm_used"), 1)
            for m in range(8):
                dve.wait_ge(S("raa_read"), m + 1)
                ins = V.tensor_scalar(BK[:, m, :, 1, :], AA[:, T * m:T * (m + 1)].rearrange("p (c t) -> p c t", c=2),
                                      par[:, P_KA + m:P_KA + m + 1], omka[:, m:m + 1], ALU.mult, ALU.add)
            then(ins)

            ccv = cc.rearrange("p (m c) -> p m c", m=8)
            dsv = small[:, 48:56]
            for q in range(4):
                dve.wait_ge(S("rg_ready"), q + 1)
                ins = V.tensor_scalar(cc[:, 4 * q:4 * q + 4], ps[:, (0, 1, 4, 5)[q], P // 2 - 1::P], DECAY, None, ALU.mult)
            then(ins)
            for q in range(4):
                ins = V.scalar_tensor_tensor(out=dsv[:, 2 * q:2 * q + 2], in0=ps[:, (0, 1, 4, 5)[q], P - 1::2 * P], scalar=-DECAY,
                                             in1=ccv[:, 2 * q:2 * q + 2, 0], op0=ALU.mult, op1=ALU.add)
            then(ins)
            V.tensor_scalar(ncc, cc, -1.0, None, ALU.mult)
            V.tensor_tensor(dsc, dsv, ccv[:, :, 1], ALU.subtract).then_inc(S("rcc_ready"), 1)
            m4 = lambda r: r.rearrange("p (m c t) -> p m c t", m=8, c=2)
            dve.wait_ge(S("rsq_ready"), 1)
            V.tensor_tensor(m4(R[9]), m4(R[9]), BK[:, :, :, 1, :], ALU.mult).then_inc(S("rk_ready"), 1)
            dve.wait_ge(S("norm_roots"), 3)
            V.reciprocal(RN, RN).then_inc(S("norm_inverse"), 1)
            for q in range(4):
                o = T1[:, 512 * q:512 * (q + 1)]
                dve.wait_ge(S("norm_spread"), q + 13)
                V.tensor_tensor(o, ps[:, (3, 6, 7, 2)[q], :], o, ALU.mult).then_inc(S("norm_used"), 1)
            dve.wait_ge(S("norm_used"), 16)
            V.tensor_tensor(AA, T1, AA, ALU.mult).then_inc(S("rta_ready"), 1)
            dve.wait_ge(S("rta_ready"), 1)
            dve.wait_ge(S("rk_ready"), 1)
            for hf in range(2):
                m = slice(4 * hf, 4 * hf + 4)
                dve.wait_ge(S("rexp_done"), hf + 1)
                V.tensor_tensor(AR[:, m, :, 0, :], m4(T1)[:, m], Ep[:, m, :, 0:P], ALU.mult)
                V.tensor_tensor(AR[:, m, :, 1, :], m4(R[8])[:, m], Ep[:, m, :, 1:P + 1], ALU.mult)
                if hf == 0:
                    V.tensor_tensor(BK[:, m, :, 1, :], m4(R[9])[:, m], En[:, m], ALU.mult)
                else:
                    dve.wait_ge(S("rbk_ready"), 1)
                V.tensor_tensor(BK[:, m, :, 0, :], m4(AA)[:, m], En[:, m], ALU.mult).then_inc(S("prep_done"), 1)
            def gated(u, bank):
                g = R[6][:, 512 * u:512 * (u + 1)]
                dve.wait_ge(S("pj_ready"), u + 1)
                V.tensor_tensor(g, ps[:, bank, :], g, ALU.mult).then_inc(S("pj_taken"), 1)

            dve.wait_ge(S("prep_done"), 2)
            for hf in range(2):
                for u in range(16):
                    dve.wait_ge(S("rm_ready"), 16 * hf + u + 1)
                    V.tensor_tensor(MM[:, u, :, :].rearrange("p w t -> p (w t)"), ps[:, (0, 1, 4, 5)[u % 4], :], C(K_M4, 4 * P), ALU.mult).then_inc(S("rm_read"), 1)
                    if hf == 0 and u in (5, 7, 9, 11):
                        q = (u - 5) // 2
                        if q == 0:
                            dve.wait_ge(S("rrk_ready"), 1)
                        dve.wait_ge(S("rbn_ready"), q + 1)
                        V.tensor_tensor(R[8][:, 512 * q:512 * (q + 1)], ps[:, (2, 3, 6, 7)[q], :], R[10][:, 512 * q:512 * (q + 1)], ALU.mult).then_inc(S("rbn_read"), 1)
                inverse(1 + hf)
                dve.wait_ge(S("rkb_ready"), hf + 1)
                V.tensor_copy(R[9][:, 1024:2048].rearrange("p (b c) -> p b c", b=2), ps[:, 2:4, :]).then_inc(S("rkb_copied"), 1)
                dve.wait_ge(S("rs_ready"), hf + 1)
                V.tensor_tensor(R[9][:, 512:768].rearrange("p (m v) -> p m v", m=4), ps[:, 4, 0:256].rearrange("p (m v) -> p m v", m=4),
                                dsc[:, 4 * hf:4 * hf + 4].unsqueeze(2).broadcast_to([P, 4, 64]), ALU.mult).then_inc(S("rs_copied"), 1)
                for u in (0, 1) if hf == 0 else (2,):
                    gated(u, (6, 1)[u % 2])
            dve.wait_ge(S("rot_read"), 2)
            for q in range(4):
                o = R[10][:, 512 * q:512 * (q + 1)]
                dve.wait_ge(S("rmu_ready"), q + 1)
                V.scalar_tensor_tensor(out=o, in0=ps[:, 4 + q, :], scalar=-1.0 / 64, in1=o, op0=ALU.mult, op1=ALU.add).then_inc(S("rmu_read"), 1)
            dve.wait_ge(S("rmu_read"), 4)
            dve.wait_ge(S("r8_ready"), 1)
            for q in range(4):
                o, w = (R[r][:, 512 * q:512 * (q + 1)] for r in (10, 8))
                dve.wait_ge(S("gg_ready"), q + 1)
                V.tensor_tensor(w, ps[:, 4 + q, :], w, ALU.mult)
                dve.wait_ge(S("rvs_ready"), q + 1)
                V.tensor_tensor(o, ps[:, 4 + q, :], o, ALU.mult).then_inc(S("gg_read"), 1)
            dve.wait_ge(S("gg_read"), 4)
            dve.wait_ge(S("norm_roots"), 4)
            V.reciprocal(RV, RV).then_inc(S("norm_inverse"), 1)
            gated(3, 1)
            def branch_low(q):
                dve.wait_ge(S("input_high"), q + 2)
                k = slice(2 * q, 2 * q + 2)
                V.tensor_tensor(ybl[:, k, :], W3[10][:, k, :], ybh[:, k, :].bitcast(F32), ALU.subtract).then_inc(S("yb_low"), 1)

            for q in range(4):
                dve.wait_ge(S("norm_spread"), q + 17)
                for m in (2 * q, 2 * q + 1):
                    o = R[10][:, T * m:T * (m + 1)]
                    ins = V.scalar_tensor_tensor(out=o, in0=o, scalar=par[:, P_LNW + m:P_LNW + m + 1],
                                                 in1=ps[:, 4 + m // 2, T * (m % 2):T * (m % 2 + 1)], op0=ALU.mult, op1=ALU.mult)
                ins.then_inc(S("norm_used"), 1)
                dve.wait_ge(S("norm_used"), q + 17)
                o = slice(512 * q, 512 * (q + 1))
                V.tensor_tensor(R[10][:, o], R[10][:, o], R[8][:, o], ALU.add).then_inc(S("yb_ready"), 1)
                if q:
                    branch_low(q - 1)
            branch_low(3)

            def merged_low(q):
                dve.wait_ge(S("merged_high"), q + 1)
                k = slice(2 * q, 2 * q + 2)
                V.tensor_tensor(mgl[:, k, :], W3[6][:, k, :], mgh[:, k, :].bitcast(F32), ALU.subtract).then_inc(S("merged_low"), 1)

            dve.wait_ge(S("pj_taken"), 4)
            for q in range(4):
                ga, gb = (R[r][:, 512 * q:512 * (q + 1)] for r in (6, 7))
                dve.wait_ge(S("pj_ready"), q + 5)
                then(V.tensor_tensor(gb, ps[:, 4 + q, :], gb, ALU.mult))
                V.tensor_tensor(ga, ga, gb, ALU.add).then_inc(S("merged"), 1)
                if q:
                    merged_low(q - 1)
            merged_low(3)
            for n in range(2):
                for c in range(NT):
                    dve.wait_ge(S("pj_ready"), 11 + 4 * n + c)
                    o = x[:, c, 512 * n:512 * (n + 1)]
                    V.tensor_tensor(o, ps[:, 2 * n + c, :], o, ALU.add).then_inc(S("x1_ready"), 1)

            dve.wait_ge(S("roots_ready"), 1)
            then(V.reciprocal(small[:, 130:132], small[:, 130:132]))
            for c in range(NT):
                ins = V.tensor_scalar(H2[:, c, :], x[:, c, :], small[:, 130 + c:131 + c], None, ALU.mult)
            ins.then_inc(S("h2_ready"), 1)
            for k in range(KT):
                dve.wait_ge(S("h2T_ready"), k // 2 + 1)
                ins = V.tensor_scalar(h2T[:, k, :], ps[:, 4 + k // 2, T * (k % 2):T * (k % 2 + 1)], par[:, P_NF + k:P_NF + k + 1], None, ALU.mult)
                if k % 2:
                    ins.then_inc(S("h2T_copied"), 1)
            dve.wait_ge(S("lg_ready"), 1)
            then(V.tensor_copy(lg, ps[:, 0:2, 0:NE]))
            for c in range(NT):
                ins = V.max(top[:, c, :], lg[:, c, :])
            then(ins)
            V.tensor_scalar(nmx, top[:, :, 0], -1.0, None, ALU.mult).then_inc(S("top_ready"), 1)
            for c in range(NT):
                ins = V.max_index(topi[:, c, :].bitcast(U32), top[:, c, :], lg[:, c, :])
            then(ins)
            then(V.tensor_copy(topf, topi.bitcast(U32)))
            i32 = cst[:, K_IOTA:K_IOTA + NE]
            for q in range(4):
                for c in range(NT):
                    if q == 0:
                        ins = V.tensor_scalar(sel[:, c, :], i32, topf[:, c, 0:1], None, ALU.is_equal)
                    else:
                        ins = V.scalar_tensor_tensor(out=sel[:, c, :], in0=i32, scalar=topf[:, c, q:q + 1], in1=sel[:, c, :], op0=ALU.is_equal, op1=ALU.add)
                then(ins)
            dve.wait_ge(S("lgexp_ready"), 1)
            then(V.tensor_tensor(gt, tmp32, sel, ALU.mult))
            then(V.tensor_reduce(gsum, gt, AX.X, ALU.add))
            then(V.reciprocal(grec, gsum))
            V.tensor_tensor(gt, gt, grec.unsqueeze(2).broadcast_to([P, 2, NE]), ALU.mult).then_inc(S("sel_ready"), 1)
            dve.wait_ge(S("sel_ready"), 1)
            dve.wait_ge(S("pos_ready"), 1)
            tpos, tgat = (tab[:, 0:NE, 2 * w:2 * w + 2].rearrange("p e c -> p c e") for w in range(2))
            V.tensor_copy(tgat, gt)
            then(V.scalar_tensor_tensor(out=tmp32, in0=ps[:, 1, 0:2 * NE].rearrange("p (c e) -> p c e", c=2), scalar=1.0, in1=sel, op0=ALU.add, op1=ALU.mult))
            then(V.tensor_scalar(tpos, tmp32, -1.0, None, ALU.add))
            iot = C(K_IOTA)

            def choose():
                for q in range(2):
                    for c in range(NT):
                        s = slice(64 * q, 64 * q + 64)
                        V.tensor_scalar(Psel[:, c, s], iot[:, s], cur[:, q, c:c + 1], None, ALU.is_equal)
                        ins = V.tensor_scalar(Pgat[:, c, s], iot[:, s], cur[:, q, c:c + 1], cur[:, q, 2 + c:3 + c], ALU.is_equal, ALU.mult)
                ins.then_inc(S("sel_made"), 1)

            then(V.tensor_copy(cur, tab[:, 0:2, :]))
            choose()
            V.tensor_copy(gT, ps[0:NE, 2, 0:T])
            V.tensor_copy(tab[:, NE:NE + 2, :], tab[:, 0:2, :])
            then(V.tensor_copy(cnt, ps[0:1, 1, 2 * NE:3 * NE]))
            V.tensor_reduce(cmax, cnt, AX.X, ALU.max).then_inc(S("pos_read"), 1)
            dve.wait_ge(S("pos_read"), 1)
            then(V.tensor_scalar(cge, cst[0:1, K_COL + 8:K_COL + 16], cmax, None, ALU.is_lt))
            V.tensor_scalar(tab[:, NE:NE + 2, 0:2], tab[:, NE:NE + 2, 0:2], -float(slots), None, ALU.add)
            then(V.tensor_reduce(csum, cge, AX.X, ALU.add))
            V.tensor_copy(passes[:, :], csum).then_inc(S("passes_known"), 1)
            V.memset(PgT[:, 1, :, :].rearrange("p c t -> p (c t)"), 0.0)
            V.memset(ysb[:, 1, :], 0.0).then_inc(S("y_copied"), 1)
            nfeat = par[:, P_NF:P_NF + 8].unsqueeze(2).broadcast_to([P, 8, P])
            fl = lambda w: ps[:, 4:6, :].rearrange("p b (f w) -> p b f w", w=2)[:, :, :, w]
            v2 = lambda r: r.rearrange("p (b f) -> p b f", b=2)

            def take_tokens(halves_before, par_, half):
                k = slice(4 * half, 4 * half + 4)
                dve.wait_ge(S("xg_ready"), halves_before + 1)
                V.tensor_tensor(xgT[:, par_, k, :], ps[:, 7, :].rearrange("p (k s) -> p k s", k=4), nfeat[:, k, :], ALU.mult).then_inc(S("xg_copied"), 1)

            def expert(it, pair, e, par_, q):
                if q == 0:
                    dve.wait_ge(S("pt_ready"), pair + 1)
                    V.tensor_copy(PgT[:, par_, :, :].rearrange("p c t -> p (c t)"), ps[:, 7, 0:T]).then_inc(S("pt_copied"), 1)
                    V.tensor_copy(cur, tab[:, bass.ds(e + 2, 2), :]).then_inc(S("cur_ready"), 1)
                    dve.wait_ge(S("cur_ready"), pair + 1)
                    choose()
                dve.wait_ge(S("brow_used"), it + 2)
                V.tensor_scalar(v2(glu), fl(0), GLU_LIMIT, None, ALU.min).then_inc(S("glu_ready"), 1)
                V.tensor_scalar(v2(lin), fl(1), GLU_LIMIT, -GLU_LIMIT, ALU.min, ALU.max).then_inc(S("moe_step"), 1)
                dve.wait_ge(S("moe_step"), 2 * it + 1)
                V.scalar_tensor_tensor(out=lin, in0=lin, scalar=1.0, in1=glu, op0=ALU.add, op1=ALU.mult).then_inc(S("moe_step"), 1)
                dve.wait_ge(S("moe_step"), 2 * it + 2)
                dve.wait_ge(S("sig_ready"), it + 1)
                V.tensor_tensor(act_h, lin, sgm, ALU.mult).then_inc(S("h_ready"), 1)
                take_tokens(it + 2, 1 - par_, q)
                dve.wait_ge(S("at_ready"), it + 1)
                V.tensor_copy(actT.rearrange("p c s -> p (c s)"), ps[:, 6, :]).then_inc(S("at_copied"), 1)
                dve.wait_ge(S("dn_used"), 4 * it + 8)
                for n in range(2):
                    ins = V.tensor_copy(ysb[64 * q:64 * q + 64, par_, 512 * n:512 * (n + 1)], ps[64 * n:64 * n + 64, 6, :])
                ins.then_inc(S("y_copied"), 1)

            for half in range(2):
                take_tokens(half, 0, half)
            dve.wait_ge(S("passes_known"), 1)
            n = dve.value_load(passes[0:1, 0:1], min_val=1, max_val=T // slots)
            with dve.Fori(0, n) as b:
                with dve.Fori(0, NE // 4) as i:
                    for w in range(4):
                        expert(NE * b + 4 * i + w, NE // 2 * b + 2 * i + w // 2, 4 * i + w, w // 2, w % 2)
                V.tensor_scalar(tab[:, :, 0:2], tab[:, :, 0:2], -float(slots), None, ALU.add).then_inc(S("pass_done"), 1)
                dve.wait_ge(S("pass_done"), b + 1)

            for c in range(NT):
                dve.wait_ge(S("sum_ready"), c + 1)
                V.tensor_tensor(x[:, c, :], ps[:, 2 * c:2 * c + 2, :].rearrange("p b c -> p (b c)"), x[:, c, :], ALU.add).then_inc(S("x2_ready"), 1)
            dve.wait_ge(S("nf_in"), 16)
            for c in range(NT):
                dve.wait_ge(S("roots_ready"), 2 + c)
                then(V.reciprocal(small[:, 134 + c:135 + c], small[:, 134 + c:135 + c]))
                V.scalar_tensor_tensor(out=R[1][:, D * c:D * (c + 1)], in0=x[:, c, :], scalar=small[:, 134 + c:135 + c], in1=nfb,
                                       op0=ALU.mult, op1=ALU.mult).then_inc(S("y_ready"), 1)

        @block.gpsimd
        def _(pool):
            G = nc.gpsimd
            pool.wait_ge(S("input_high"), 1)
            G.tensor_tensor(hTl, hT, hTh.bitcast(F32), ALU.subtract).then_inc(S("input_low"), 1)
            with pool.Fori(0, 2) as i:
                for u in range(18):
                    j, half = u // 2, u % 2
                    pool.wait_ge(S("high_ready"), 18 * i + (u + 1))
                    w, low = (r[(1 + j) % 3][:, :, 256 * half:256 * half + 256] for r in (panel, panel_r))
                    G.tensor_tensor(low, w, high[u % 3].bitcast(F32), ALU.subtract).then_inc(S("low_ready"), 1)
            pool.wait_ge(S("got_ready"), 4)
            G.tensor_tensor(T1.rearrange("p (m t) -> p m t", m=8), W3[9], cols8(P_KK), ALU.mult).then_inc(S("pool_step"), 1)
            pool.wait_ge(S("pool_step"), 1)
            G.tensor_tensor(SQ, T1, T1, ALU.mult).then_inc(S("rsq_ready"), 1)
            pool.wait_ge(S("norm_sums"), 3)
            pool.wait_ge(S("rk_ready"), 1)
            G.tensor_tensor(SQ, R[8], R[9], ALU.mult).then_inc(S("pool_step"), 1)
            pool.wait_ge(S("pool_step"), 2)
            G.tensor_tensor(SQ.rearrange("p (m t) -> p m t", m=8), SQ.rearrange("p (m t) -> p m t", m=8), cols8(P_RK), ALU.mult).then_inc(S("rrk_ready"), 1)
            pool.wait_ge(S("rexp_done"), 2)
            G.tensor_tensor(BK[:, 4:8, :, 1, :], R[9].rearrange("p (m c t) -> p m c t", m=8, c=2)[:, 4:8], En[:, 4:8], ALU.mult).then_inc(S("rbk_ready"), 1)
            eye = ident.unsqueeze(1).broadcast_to([P, 16, P])
            pool.wait_ge(S("rbn_ready"), 4)
            G.tensor_copy(TT, eye).then_inc(S("tt_ready"), 1)
            pool.wait_ge(S("rbn_read"), 4)
            G.tensor_tensor(W3[8], W3[8], cols8(P_LNB), ALU.add).then_inc(S("r8_ready"), 1)
            pool.wait_ge(S("rot_ready"), 1)
            G.tensor_copy(TT, eye).then_inc(S("tt_ready"), 1)
            for hp in range(4, 12):
                q, half = hp // 2, hp % 2
                pool.wait_ge(S("high_ready"), 32 + hp + 1)
                w, low = (r[late_slot[q]][:, :, T * half:T * (half + 1)] for r in (panel, panel_r))
                G.tensor_tensor(low, w, high2[hp % 3].bitcast(F32), ALU.subtract).then_inc(S("low_ready"), 1)


_NAMES = ["x", "norm_mix", "w_in", "gdn_conv", "gdn_A_log", "gdn_dt_bias", "gdn_norm", "rwkv_mu", "rwkv_w0", "rwkv_w2", "rwkv_a0",
          "rwkv_a2", "rwkv_g2", "rwkv_k_k", "rwkv_k_a", "rwkv_r_k", "rwkv_ln_w", "rwkv_ln_b", "proj_a", "proj_b", "w_out", "norm_ffn",
          "router_w", "router_b", "w_gate_up", "b_gate_up", "w_down", "b_down", "norm_final"]


def kernel(**inputs):
    import numpy as _np
    import concourse.bacc as _bacc
    from concourse import mybir as _mybir
    from concourse.bass_utils import run_bass_kernel_spmd as _run

    nc = _bacc.Bacc("TRN2", target_bir_lowering=False, num_devices=1)
    consts, masks = shape_constants()
    arrays, aps = {}, {}
    for name in _NAMES:
        arrays[f"in_{name}"] = _np.ascontiguousarray(inputs[name])
    arrays["in_consts"], arrays["in_masks"] = consts, masks
    for full, a in arrays.items():
        aps[full[3:]] = nc.dram_tensor(full, a.shape, _mybir.dt.from_np(a.dtype), kind="ExternalInput").ap()
    aps["out"] = nc.dram_tensor("out_0", (1, T, D), F32, kind="ExternalOutput").ap()
    hybrid_block(nc, aps)
    r = _run(nc, [arrays], core_ids=[0])
    return r.results[0]["out_0"]
```
